# Optimizing a Trainium2 kernel written in Bass

```python
import jax
import jax.numpy as jnp
from jax import lax
import numpy as np
import math
import jax, jax.numpy as jnp

D_MODEL = 1024
BATCH = 1
SEQ = 256
DEPTH = 2

N_EVEN = (DEPTH + 1) // 2
N_ODD = DEPTH // 2
EPS = 1e-6
ROPE_THETA = 10000.0

D_FF = -(-(8 * D_MODEL) // (3 * 256)) * 256

CONV_WIDTH = D_MODEL // 2
POOL_WIDTH = D_MODEL - CONV_WIDTH
POOL_WINDOWS = (2, 4, 8, 16)
POOL_GROUP = POOL_WIDTH // len(POOL_WINDOWS)
SHORT_CONV_K = 3
EVEN_IN = 3 * CONV_WIDTH + POOL_WIDTH

HEAD_DIM = 64
NSA_WIDTH = D_MODEL // 2
NSA_HEADS = NSA_WIDTH // HEAD_DIM
NSA_KV_GROUPS = 2
GROUP_SIZE = NSA_HEADS // NSA_KV_GROUPS
KV_WIDTH = NSA_KV_GROUPS * HEAD_DIM
CMP_BLOCK = 32
CMP_STRIDE = 16
CMP_HIDDEN = 4 * HEAD_DIM
SEL_BLOCK = 64
N_SELECT = 8
WINDOW = 512
Q_BLOCK = 128
FORCE_SCORE = 1e4
NEG = -1e30
TINY = 1e-30
CONF_WIDTH = D_MODEL - NSA_WIDTH
CONF_K = 31
ODD_PARTS = (NSA_WIDTH, KV_WIDTH, KV_WIDTH, KV_WIDTH, KV_WIDTH, KV_WIDTH, KV_WIDTH,
             3 * NSA_HEADS, 2 * CONF_WIDTH)
ODD_IN = sum(ODD_PARTS)


def rms_norm(x, g):
    xf = x.astype(jnp.float32)
    y = xf * lax.rsqrt(jnp.mean(xf * xf, axis=-1, keepdims=True) + EPS)
    return (y * g.astype(jnp.float32)).astype(x.dtype)

def layer_norm(x, g, b):
    xf = x.astype(jnp.float32)
    mu = jnp.mean(xf, axis=-1, keepdims=True)
    var = jnp.mean(jnp.square(xf - mu), axis=-1, keepdims=True)
    y = (xf - mu) * lax.rsqrt(var + EPS)
    return (y * g.astype(jnp.float32) + b.astype(jnp.float32)).astype(x.dtype)

def rope_tables(seq_len):
    inv = 1.0 / (ROPE_THETA ** (jnp.arange(0, HEAD_DIM, 2, dtype=jnp.float32) / HEAD_DIM))
    ang = jnp.arange(seq_len, dtype=jnp.float32)[:, None] * inv[None, :]
    return jnp.cos(ang), jnp.sin(ang)

def apply_rope(x, cos, sin):
    xf = x.astype(jnp.float32)
    x1, x2 = jnp.split(xf, 2, axis=-1)
    c = cos[None, :, None, :]
    s = sin[None, :, None, :]
    return jnp.concatenate([x1 * c - x2 * s, x2 * c + x1 * s], axis=-1).astype(x.dtype)

def causal_dwconv(x, w):
    k, c = w.shape
    return lax.conv_general_dilated(
        x, w[:, None, :].astype(x.dtype), window_strides=(1,), padding=[(k - 1, 0)],
        dimension_numbers=('NWC', 'WIO', 'NWC'), feature_group_count=c)

def masked_softmax(s, mask):
    s = jnp.where(mask, s.astype(jnp.float32), NEG)
    m = jnp.max(s, axis=-1, keepdims=True)
    e = jnp.where(mask, jnp.exp(s - m), 0.0)
    return e / jnp.maximum(jnp.sum(e, axis=-1, keepdims=True), TINY)

def swiglu(h, wg, wu, wd):
    return (jax.nn.silu(h @ wg) * (h @ wu)) @ wd

def multiscale_pool(v, pool_w, pool_scale):
    bsz, t, _ = v.shape
    vg = v.reshape(bsz, t, len(POOL_WINDOWS), POOL_GROUP)
    cs = jnp.cumsum(vg.astype(jnp.float32), axis=1)
    pos = jnp.arange(t)
    means = []
    for gi, w in enumerate(POOL_WINDOWS):
        c = cs[:, :, gi]
        prev = jnp.pad(c, ((0, 0), (w, 0), (0, 0)))[:, :t]
        cnt = jnp.minimum(pos + 1, w).astype(jnp.float32)[None, :, None]
        means.append((c - prev) / cnt)
    pooled = jnp.stack(means, axis=2).astype(v.dtype) - vg
    y = jnp.einsum('btgc,gcd->btgd', pooled, pool_w)
    return y.reshape(bsz, t, POOL_WIDTH) * pool_scale

def short_conv_pool_mixer(h, w_in, conv_w, pool_w, pool_scale, w_out):
    u = h @ w_in
    b_gate, c_gate, v_conv, v_pool = jnp.split(
        u, [CONV_WIDTH, 2 * CONV_WIDTH, 3 * CONV_WIDTH], axis=-1)
    y_conv = b_gate * causal_dwconv(c_gate * v_conv, conv_w)
    y_pool = multiscale_pool(v_pool, pool_w, pool_scale)
    return jnp.concatenate([y_conv, y_pool], axis=-1) @ w_out

def compress_blocks(tok, pos_emb, w1, w2):
    bsz, g, t, dh = tok.shape
    n_cmp = (t - CMP_BLOCK) // CMP_STRIDE + 1
    idx = jnp.arange(n_cmp)[:, None] * CMP_STRIDE + jnp.arange(CMP_BLOCK)[None, :]
    blocks = tok[:, :, idx] + pos_emb
    flat = blocks.reshape(bsz, g, n_cmp, CMP_BLOCK * dh)
    return jax.nn.gelu(flat @ w1) @ w2

def native_sparse_attention(q, k_cmp, v_cmp, k_slc, v_slc, k_win, v_win, gates,
                            q_norm, k_norm, cmp_pos, cmp_w1, cmp_w2, cos, sin):
    bsz, t = q.shape[0], q.shape[1]
    q = apply_rope(rms_norm(q, q_norm), cos, sin)
    ks = apply_rope(rms_norm(k_slc, k_norm[0]), cos, sin)
    kw = apply_rope(rms_norm(k_win, k_norm[1]), cos, sin)
    kc_tok = apply_rope(k_cmp, cos, sin)
    to_bgtd = lambda a: a.transpose(0, 2, 1, 3)
    kc = rms_norm(compress_blocks(to_bgtd(kc_tok), cmp_pos[0], cmp_w1[0], cmp_w2[0]), k_norm[2])
    vc = compress_blocks(to_bgtd(v_cmp), cmp_pos[1], cmp_w1[1], cmp_w2[1])
    ks, vs, kw, vw = to_bgtd(ks), to_bgtd(v_slc), to_bgtd(kw), to_bgtd(v_win)

    q5 = q.reshape(bsz, t, NSA_KV_GROUPS, GROUP_SIZE, HEAD_DIM).transpose(0, 2, 3, 1, 4)
    g5 = gates.reshape(bsz, t, NSA_KV_GROUPS, GROUP_SIZE, 3).transpose(0, 2, 3, 1, 4)

    n_cmp = kc.shape[2]
    n_sb = t // SEL_BLOCK
    n_sel = min(N_SELECT, n_sb)
    cmp_start = jnp.arange(n_cmp) * CMP_STRIDE
    cmp_end = cmp_start + CMP_BLOCK - 1
    sb_start = jnp.arange(n_sb) * SEL_BLOCK
    overlap = ((cmp_start[:, None] < sb_start[None, :] + SEL_BLOCK)
               & (cmp_end[:, None] >= sb_start[None, :])).astype(jnp.float32)
    ks_blocks = ks.reshape(bsz, NSA_KV_GROUPS, n_sb, SEL_BLOCK, HEAD_DIM)
    vs_blocks = vs.reshape(bsz, NSA_KV_GROUPS, n_sb, SEL_BLOCK, HEAD_DIM)
    kw_pad = jnp.pad(kw, ((0, 0), (0, 0), (WINDOW, 0), (0, 0)))
    vw_pad = jnp.pad(vw, ((0, 0), (0, 0), (WINDOW, 0), (0, 0)))
    bi = jnp.arange(bsz)[:, None, None, None]
    gi = jnp.arange(NSA_KV_GROUPS)[None, :, None, None]
    scale = HEAD_DIM ** -0.5

    def query_block(qb):
        q0 = qb * Q_BLOCK
        qblk = lax.dynamic_slice_in_dim(q5, q0, Q_BLOCK, axis=3)
        gblk = lax.dynamic_slice_in_dim(g5, q0, Q_BLOCK, axis=3)
        pos = q0 + jnp.arange(Q_BLOCK)
        s_c = jnp.einsum('bgrqd,bgnd->bgrqn', qblk, kc).astype(jnp.float32) * scale
        p_cmp = masked_softmax(s_c, cmp_end[None, :] <= pos[:, None])
        o_cmp = jnp.einsum('bgrqn,bgnd->bgrqd', p_cmp.astype(vc.dtype), vc)
        imp = jnp.einsum('bgrqn,nj->bgqj', p_cmp, overlap)
        cur = pos // SEL_BLOCK
        jj = jnp.arange(n_sb)[None, :]
        forced = (jj == 0) | (jj == cur[:, None]) | (jj == cur[:, None] - 1)
        valid = sb_start[None, :] <= pos[:, None]
        score = jnp.where(valid, jnp.where(forced, FORCE_SCORE, imp), -1.0)
        _, top_idx = lax.top_k(score, n_sel)
        k_sel = ks_blocks[bi, gi, top_idx].reshape(bsz, NSA_KV_GROUPS, Q_BLOCK, n_sel * SEL_BLOCK, HEAD_DIM)
        v_sel = vs_blocks[bi, gi, top_idx].reshape(bsz, NSA_KV_GROUPS, Q_BLOCK, n_sel * SEL_BLOCK, HEAD_DIM)
        tok_pos = (top_idx[..., None] * SEL_BLOCK + jnp.arange(SEL_BLOCK)).reshape(
            bsz, NSA_KV_GROUPS, Q_BLOCK, n_sel * SEL_BLOCK)
        sel_mask = (tok_pos <= pos[None, None, :, None])[:, :, None]
        s_s = jnp.einsum('bgrqd,bgqkd->bgrqk', qblk, k_sel).astype(jnp.float32) * scale
        p_s = masked_softmax(s_s, sel_mask)
        o_slc = jnp.einsum('bgrqk,bgqkd->bgrqd', p_s.astype(v_sel.dtype), v_sel)
        k_band = lax.dynamic_slice_in_dim(kw_pad, q0, WINDOW + Q_BLOCK, axis=2)
        v_band = lax.dynamic_slice_in_dim(vw_pad, q0, WINDOW + Q_BLOCK, axis=2)
        kpos = q0 - WINDOW + jnp.arange(WINDOW + Q_BLOCK)
        w_mask = ((kpos[None, :] <= pos[:, None]) & (kpos[None, :] > pos[:, None] - WINDOW)
                  & (kpos[None, :] >= 0))
        s_w = jnp.einsum('bgrqd,bgkd->bgrqk', qblk, k_band).astype(jnp.float32) * scale
        p_w = masked_softmax(s_w, w_mask)
        o_win = jnp.einsum('bgrqk,bgkd->bgrqd', p_w.astype(v_band.dtype), v_band)
        return gblk[..., 0:1] * o_cmp + gblk[..., 1:2] * o_slc + gblk[..., 2:3] * o_win

    out = lax.map(query_block, jnp.arange(t // Q_BLOCK))
    return out.transpose(1, 0, 4, 2, 3, 5).reshape(bsz, t, NSA_WIDTH)

def sparse_attn_conformer_mixer(h, w_in, q_norm, k_norm, cmp_pos, cmp_w1, cmp_w2,
                                conf_dw, conf_dw_b, conf_ln_g, conf_ln_b, w_out, cos, sin):
    bsz, t, _ = h.shape
    u = h @ w_in
    offs = []
    acc = 0
    for p in ODD_PARTS[:-1]:
        acc += p
        offs.append(acc)
    q, kc, vc, ks, vs, kw, vw, gt, cf = jnp.split(u, offs, axis=-1)
    heads = lambda a: a.reshape(bsz, t, NSA_HEADS, HEAD_DIM)
    kvs = lambda a: a.reshape(bsz, t, NSA_KV_GROUPS, HEAD_DIM)
    gates = jax.nn.sigmoid(gt).reshape(bsz, t, NSA_HEADS, 3)
    o_nsa = native_sparse_attention(heads(q), kvs(kc), kvs(vc), kvs(ks), kvs(vs), kvs(kw), kvs(vw),
                                    gates, q_norm, k_norm, cmp_pos, cmp_w1, cmp_w2, cos, sin)
    a, b = jnp.split(cf, 2, axis=-1)
    z = a * jax.nn.sigmoid(b)
    z = causal_dwconv(z, conf_dw) + conf_dw_b
    z = jax.nn.silu(layer_norm(z, conf_ln_g, conf_ln_b))
    return jnp.concatenate([o_nsa, z], axis=-1) @ w_out

def first_inputs(seed: int = 0) -> dict:
    key = jax.random.key(seed)
    ks = jax.random.split(key, 24)
    nrm = lambda k, shape, s: jax.random.normal(k, shape, jnp.float32) * s
    d = D_MODEL
    return {
        'x': nrm(ks[0], (BATCH, SEQ, d), 1.0),
        'norm_mix': 1.0 + nrm(ks[1], (DEPTH, d), 0.05),
        'norm_ffn': 1.0 + nrm(ks[2], (DEPTH, d), 0.05),
        'ffn_gate': nrm(ks[3], (DEPTH, d, D_FF), d ** -0.5),
        'ffn_up': nrm(ks[4], (DEPTH, d, D_FF), d ** -0.5),
        'ffn_down': nrm(ks[5], (DEPTH, D_FF, d), 0.5 * D_FF ** -0.5),
        'w_in_even': nrm(ks[6], (N_EVEN, d, EVEN_IN), d ** -0.5),
        'conv_a': nrm(ks[7], (N_EVEN, SHORT_CONV_K, CONV_WIDTH), SHORT_CONV_K ** -0.5),
        'pool_w': nrm(ks[8], (N_EVEN, len(POOL_WINDOWS), POOL_GROUP, POOL_GROUP), POOL_GROUP ** -0.5),
        'pool_scale': 1.0 + nrm(ks[9], (N_EVEN, POOL_WIDTH), 0.1),
        'w_out_even': nrm(ks[10], (N_EVEN, d, d), 0.5 * d ** -0.5),
        'w_in_odd': nrm(ks[11], (N_ODD, d, ODD_IN), d ** -0.5),
        'q_norm': 1.0 + nrm(ks[12], (N_ODD, HEAD_DIM), 0.05),
        'k_norm': 1.0 + nrm(ks[13], (N_ODD, 3, HEAD_DIM), 0.05),
        'cmp_pos': nrm(ks[14], (N_ODD, 2, CMP_BLOCK, HEAD_DIM), 0.1),
        'cmp_w1': nrm(ks[15], (N_ODD, 2, CMP_BLOCK * HEAD_DIM, CMP_HIDDEN), (CMP_BLOCK * HEAD_DIM) ** -0.5),
        'cmp_w2': nrm(ks[16], (N_ODD, 2, CMP_HIDDEN, HEAD_DIM), CMP_HIDDEN ** -0.5),
        'conf_dw': nrm(ks[17], (N_ODD, CONF_K, CONF_WIDTH), CONF_K ** -0.5),
        'conf_dw_b': nrm(ks[18], (N_ODD, CONF_WIDTH), 0.02),
        'conf_ln_g': 1.0 + nrm(ks[19], (N_ODD, CONF_WIDTH), 0.05),
        'conf_ln_b': nrm(ks[20], (N_ODD, CONF_WIDTH), 0.02),
        'w_out_odd': nrm(ks[21], (N_ODD, d, d), 0.5 * d ** -0.5),
    }

def first_block(x, norm_mix, norm_ffn, ffn_gate, ffn_up, ffn_down,
              w_in_even, conv_a, pool_w, pool_scale, w_out_even,
              w_in_odd, q_norm, k_norm, cmp_pos, cmp_w1, cmp_w2,
              conf_dw, conf_dw_b, conf_ln_g, conf_ln_b, w_out_odd):
    cos, sin = rope_tables(x.shape[1])
    for i in range(DEPTH):
        h = rms_norm(x, norm_mix[i])
        if i % 2 == 0:
            e = i // 2
            x = x + short_conv_pool_mixer(h, w_in_even[e], conv_a[e], pool_w[e],
                                          pool_scale[e], w_out_even[e])
        else:
            o = i // 2
            x = x + sparse_attn_conformer_mixer(h, w_in_odd[o], q_norm[o], k_norm[o], cmp_pos[o],
                                                cmp_w1[o], cmp_w2[o], conf_dw[o], conf_dw_b[o],
                                                conf_ln_g[o], conf_ln_b[o], w_out_odd[o], cos, sin)
        x = x + swiglu(rms_norm(x, norm_ffn[i]), ffn_gate[i], ffn_up[i], ffn_down[i])
    return x


DEPTH_2 = 1

W_BR = D_MODEL // 2
N_BRANCH = 3
H_A = W_BR // HEAD_DIM
MOBA_BLOCK = 256
MOBA_TOPK = 3
MOBA_QCHUNK = 32
DIL_PAIRS = ((128, 1), (512, 4), (2048, 16))
N_DIL = len(DIL_PAIRS)
H_B = W_BR // HEAD_DIM
DIL_QCHUNK = 64
H_C = W_BR // HEAD_DIM
KV_C = 2
SWA_WINDOW = 128
N_BUCKETS = 32
REL_MAX_DIST = 2048
H_TOT = H_A + N_DIL * H_B + H_C
OFF_A = 0
OFF_B = H_A
OFF_C = H_A + N_DIL * H_B

NEG_INF = -1e30

SPLIT_SIZES = ([W_BR] * 4
               + [N_DIL * W_BR] * 3 + [W_BR]
               + [W_BR, KV_C * HEAD_DIM, KV_C * HEAD_DIM, W_BR]
               + [N_BRANCH * D_MODEL])
C_IN = int(sum(SPLIT_SIZES))
SPLIT_POINTS = [int(v) for v in np.cumsum(SPLIT_SIZES)[:-1]]


def rms_norm_2(x, g):
    x32 = x.astype(jnp.float32)
    y = x32 * lax.rsqrt(jnp.mean(x32 * x32, axis=-1, keepdims=True) + EPS)
    return (y * g.astype(jnp.float32)).astype(x.dtype)

def rel_bucket(dist):
    dist = jnp.maximum(dist, 0)
    max_exact = N_BUCKETS // 2
    log_ratio = jnp.log(jnp.maximum(dist, 1).astype(jnp.float32) / max_exact) / math.log(REL_MAX_DIST / max_exact)
    large = max_exact + (log_ratio * (N_BUCKETS - max_exact)).astype(jnp.int32)
    large = jnp.minimum(large, N_BUCKETS - 1)
    return jnp.where(dist < max_exact, dist, large)

def moba_attention(q, k, v, bias_tab):
    b, s, h, dh = q.shape
    s_pad = -(-s // MOBA_BLOCK) * MOBA_BLOCK
    pad = ((0, 0), (0, s_pad - s), (0, 0), (0, 0))
    qh, kh, vh = [jnp.pad(t, pad).transpose(0, 2, 1, 3) for t in (q, k, v)]
    nb = s_pad // MOBA_BLOCK
    kb = kh.reshape(b, h, nb, MOBA_BLOCK, dh)
    vb = vh.reshape(b, h, nb, MOBA_BLOCK, dh)
    k_mean = jnp.mean(kb.astype(jnp.float32), axis=3)
    gate = jnp.einsum('bhsd,bhnd->bhsn', qh.astype(jnp.float32), k_mean)
    q_blk = jnp.arange(s_pad) // MOBA_BLOCK
    past = jnp.arange(nb)[None, :] < q_blk[:, None]
    gate = jnp.where(past, gate, NEG_INF)
    n_sel = min(MOBA_TOPK, max(nb - 1, 1))
    _, top_idx = lax.top_k(gate, n_sel)
    sel_valid = jnp.arange(n_sel)[None, :] < jnp.minimum(q_blk, MOBA_TOPK)[:, None]
    scale = dh ** -0.5
    bias_tab = bias_tab.astype(jnp.float32)
    b_idx = jnp.arange(b)[:, None, None, None]
    h_idx = jnp.arange(h)[None, :, None, None]
    h_idx5 = jnp.arange(h)[None, :, None, None, None]
    blk_off = jnp.arange(MOBA_BLOCK)

    def chunk(c):
        t0 = c * MOBA_QCHUNK
        t = t0 + jnp.arange(MOBA_QCHUNK)
        q_c = lax.dynamic_slice_in_dim(qh, t0, MOBA_QCHUNK, axis=2)
        idx_c = lax.dynamic_slice_in_dim(top_idx, t0, MOBA_QCHUNK, axis=2)
        valid_c = lax.dynamic_slice_in_dim(sel_valid, t0, MOBA_QCHUNK, axis=0)
        k_sel = kb[b_idx, h_idx, idx_c]
        v_sel = vb[b_idx, h_idx, idx_c]
        s_sel = jnp.einsum('bhqd,bhqjkd->bhqjk', q_c, k_sel,
                           preferred_element_type=jnp.float32) * scale
        key_pos = idx_c[..., None] * MOBA_BLOCK + blk_off
        dist = t[:, None, None] - key_pos
        bias_sel = bias_tab[h_idx5, rel_bucket(dist)]
        s_sel = jnp.where(valid_c[:, :, None], s_sel + bias_sel, NEG_INF)
        n_own = t0 // MOBA_BLOCK
        k_own = lax.dynamic_index_in_dim(kb, n_own, axis=2, keepdims=False)
        v_own = lax.dynamic_index_in_dim(vb, n_own, axis=2, keepdims=False)
        s_own = jnp.einsum('bhqd,bhkd->bhqk', q_c, k_own,
                           preferred_element_type=jnp.float32) * scale
        dist_own = t[:, None] - (n_own * MOBA_BLOCK + blk_off)[None, :]
        s_own = jnp.where(dist_own >= 0, s_own + bias_tab[:, rel_bucket(dist_own)], NEG_INF)
        n_s = n_sel * MOBA_BLOCK
        logits = jnp.concatenate([s_sel.reshape(b, h, MOBA_QCHUNK, n_s), s_own], axis=-1)
        p = jax.nn.softmax(logits, axis=-1)
        p_sel = p[..., :n_s].reshape(b, h, MOBA_QCHUNK, n_sel, MOBA_BLOCK).astype(v.dtype)
        p_own = p[..., n_s:].astype(v.dtype)
        out = (jnp.einsum('bhqjk,bhqjkd->bhqd', p_sel, v_sel, preferred_element_type=jnp.float32)
               + jnp.einsum('bhqk,bhkd->bhqd', p_own, v_own, preferred_element_type=jnp.float32))
        return out.astype(v.dtype)

    out = lax.map(chunk, jnp.arange(s_pad // MOBA_QCHUNK))
    out = out.transpose(1, 0, 3, 2, 4).reshape(b, s_pad, h, dh)
    return out[:, :s]

def dilated_attention(q, k, v, bias_tab):
    b, s, _, h, dh = q.shape
    scale = dh ** -0.5
    bias_tab = bias_tab.astype(jnp.float32)
    n_keys = [w // d + 1 for (w, d) in DIL_PAIRS]
    k_pads = [jnp.pad(k[:, :, gi], ((0, 0), (w, 0), (0, 0), (0, 0))) for gi, (w, d) in enumerate(DIL_PAIRS)]
    v_pads = [jnp.pad(v[:, :, gi], ((0, 0), (w, 0), (0, 0), (0, 0))) for gi, (w, d) in enumerate(DIL_PAIRS)]
    bias_g = [bias_tab[gi * h:(gi + 1) * h][:, rel_bucket(d * jnp.arange(n_keys[gi]))]
              for gi, (w, d) in enumerate(DIL_PAIRS)]

    def chunk(c):
        t0 = c * DIL_QCHUNK
        t = t0 + jnp.arange(DIL_QCHUNK)
        q_c = lax.dynamic_slice_in_dim(q, t0, DIL_QCHUNK, axis=1)
        outs, lses = [], []
        for gi, (w, d) in enumerate(DIL_PAIRS):
            steps = jnp.arange(n_keys[gi]) * d
            idx = t[:, None] + w - steps[None, :]
            k_g = k_pads[gi][:, idx]
            v_g = v_pads[gi][:, idx]
            logits = jnp.einsum('bqhd,bqjhd->bhqj', q_c[:, :, gi], k_g,
                                preferred_element_type=jnp.float32) * scale + bias_g[gi][:, None, :]
            logits = jnp.where((t[:, None] - steps[None, :]) >= 0, logits, NEG_INF)
            lse = jax.nn.logsumexp(logits, axis=-1)
            p = jnp.exp(logits - lse[..., None]).astype(v.dtype)
            outs.append(jnp.einsum('bhqj,bqjhd->bqhd', p, v_g, preferred_element_type=jnp.float32))
            lses.append(lse)
        wts = jax.nn.softmax(jnp.stack(lses, axis=0), axis=0)
        out = sum(wts[gi].transpose(0, 2, 1)[..., None] * outs[gi] for gi in range(N_DIL))
        return out.astype(v.dtype)

    out = lax.map(chunk, jnp.arange(s // DIL_QCHUNK))
    return out.transpose(1, 0, 2, 3, 4).reshape(b, s, h, dh)

def swa_sink_attention(q, k, v, sinks, bias_tab):
    b, s, h, dh = q.shape
    kvh = k.shape[2]
    rep = h // kvh
    W = SWA_WINDOW
    nb = s // W
    scale = dh ** -0.5
    qb = q.reshape(b, nb, W, kvh, rep, dh)
    kb = k.reshape(b, nb, W, kvh, dh)
    vb = v.reshape(b, nb, W, kvh, dh)

    def with_prev(t):
        prev = jnp.pad(t, ((0, 0), (1, 0), (0, 0), (0, 0), (0, 0)))[:, :-1]
        return jnp.concatenate([prev, t], axis=2)

    kk, vv = with_prev(kb), with_prev(vb)
    logits = jnp.einsum('bnqgrd,bnkgd->bngrqk', qb, kk,
                        preferred_element_type=jnp.float32) * scale
    i = jnp.arange(W)
    j = jnp.arange(2 * W)
    dist = i[:, None] + W - j[None, :]
    key_pos = jnp.arange(nb)[:, None] * W - W + j[None, :]
    valid = ((dist >= 0) & (dist < W))[None] & (key_pos >= 0)[:, None, :]
    bias = bias_tab.astype(jnp.float32)[:, rel_bucket(dist)].reshape(kvh, rep, W, 2 * W)
    logits = jnp.where(valid[None, :, None, None], logits + bias, NEG_INF)
    sink = sinks.astype(jnp.float32).reshape(kvh, rep)[None, None, :, :, None, None]
    m = jnp.maximum(jnp.max(logits, axis=-1, keepdims=True), sink)
    e = jnp.exp(logits - m)
    p = e / (jnp.sum(e, axis=-1, keepdims=True) + jnp.exp(sink - m))
    out = jnp.einsum('bngrqk,bnkgd->bnqgrd', p.astype(v.dtype), vv, preferred_element_type=jnp.float32)
    return out.reshape(b, s, h, dh).astype(v.dtype)

def second_inputs(seed: int = 0) -> dict:
    key = jax.random.key(seed)
    ks = jax.random.split(key, 8)
    x = jax.random.normal(ks[0], (BATCH, SEQ, D_MODEL), jnp.float32)
    ln_g = 1.0 + 0.02 * jax.random.normal(ks[1], (DEPTH_2, D_MODEL), jnp.float32)
    w_in = jax.random.normal(ks[2], (DEPTH_2, D_MODEL, C_IN), jnp.float32) * D_MODEL ** -0.5
    qk_g = 1.0 + 0.02 * jax.random.normal(ks[3], (DEPTH_2, 6, HEAD_DIM), jnp.float32)
    sinks = 0.5 * jax.random.normal(ks[4], (DEPTH_2, H_C), jnp.float32)
    w_branch = jax.random.normal(ks[5], (DEPTH_2, N_BRANCH, W_BR, D_MODEL), jnp.float32) * W_BR ** -0.5
    w_out = jax.random.normal(ks[6], (DEPTH_2, D_MODEL, D_MODEL), jnp.float32) * D_MODEL ** -0.5
    rel_bias = 0.2 * jax.random.normal(ks[7], (H_TOT, N_BUCKETS), jnp.float32)
    return {"x": x, "ln_g": ln_g, "w_in": w_in, "qk_g": qk_g, "sinks": sinks,
            "w_branch": w_branch, "w_out": w_out, "rel_bias": rel_bias}

def second_block(x, ln_g, w_in, qk_g, sinks, w_branch, w_out, rel_bias):
    b, s, _ = x.shape
    for l in range(DEPTH_2):
        hn = rms_norm_2(x, ln_g[l])
        proj = jnp.einsum('bsd,dc->bsc', hn, w_in[l])
        (qa, ka, va, ga, qb, kb, vb, gb, qc, kc, vc, gc, gate_logits) = jnp.split(proj, SPLIT_POINTS, axis=-1)
        g = qk_g[l]
        qa = rms_norm_2(qa.reshape(b, s, H_A, HEAD_DIM), g[0])
        ka = rms_norm_2(ka.reshape(b, s, H_A, HEAD_DIM), g[1])
        o_a = moba_attention(qa, ka, va.reshape(b, s, H_A, HEAD_DIM), rel_bias[OFF_A:OFF_A + H_A])
        qb = rms_norm_2(qb.reshape(b, s, N_DIL, H_B, HEAD_DIM), g[2])
        kb = rms_norm_2(kb.reshape(b, s, N_DIL, H_B, HEAD_DIM), g[3])
        o_b = dilated_attention(qb, kb, vb.reshape(b, s, N_DIL, H_B, HEAD_DIM),
                                rel_bias[OFF_B:OFF_B + N_DIL * H_B])
        qc = rms_norm_2(qc.reshape(b, s, H_C, HEAD_DIM), g[4])
        kc = rms_norm_2(kc.reshape(b, s, KV_C, HEAD_DIM), g[5])
        o_c = swa_sink_attention(qc, kc, vc.reshape(b, s, KV_C, HEAD_DIM), sinks[l],
                                 rel_bias[OFF_C:OFF_C + H_C])
        branches = jnp.stack([o_a.reshape(b, s, W_BR) * jax.nn.silu(ga),
                              o_b.reshape(b, s, W_BR) * jax.nn.silu(gb),
                              o_c.reshape(b, s, W_BR) * jax.nn.silu(gc)], axis=2)
        br = jnp.einsum('bsiw,iwd->bsid', branches, w_branch[l])
        gates = jax.nn.sigmoid(gate_logits.reshape(b, s, N_BRANCH, D_MODEL))
        merged = jnp.sum(gates * br, axis=2)
        x = x + jnp.einsum('bsd,de->bse', merged, w_out[l])
    return x


def setup_inputs(seed=0):
    out = dict(first_inputs(seed))
    for name, value in second_inputs(seed + 1).items():
        if name != "x":
            out[name + "_2"] = value
    return out


def reference(
    x, norm_mix, norm_ffn, ffn_gate, ffn_up, ffn_down, w_in_even, conv_a, pool_w, pool_scale,
    w_out_even, w_in_odd, q_norm, k_norm, cmp_pos, cmp_w1, cmp_w2, conf_dw, conf_dw_b,
    conf_ln_g, conf_ln_b, w_out_odd, ln_g_2, w_in_2, qk_g_2, sinks_2, w_branch_2, w_out_2,
    rel_bias_2,
):
    x = first_block(
        x, norm_mix, norm_ffn, ffn_gate, ffn_up, ffn_down, w_in_even, conv_a, pool_w,
        pool_scale, w_out_even, w_in_odd, q_norm, k_norm, cmp_pos, cmp_w1, cmp_w2, conf_dw,
        conf_dw_b, conf_ln_g, conf_ln_b, w_out_odd,
    )
    return second_block(
        x, ln_g_2, w_in_2, qk_g_2, sinks_2, w_branch_2, w_out_2, rel_bias_2,
    )


_drawn_inputs = setup_inputs


def setup_inputs(seed=0):
    import zlib

    import numpy as np

    out = dict(_drawn_inputs(seed))
    spreads = {}
    factors = {'q_norm': 8.0,
     'k_norm': 8.0,
     'cmp_pos': 5.177,
     'conf_dw_b': 6.494,
     'conf_ln_g': 5.13,
     'conf_ln_b': 8.0,
     'ln_g_2': 8.0,
     'qk_g_2': 8.0,
     'sinks_2': 59.579,
     'rel_bias_2': 3.526}
    for name, (base, spread) in spreads.items():
        noise = np.random.default_rng([zlib.crc32(name.encode()), seed]).standard_normal(out[name].shape)
        drawn = base * np.exp(spread * noise) if base else spread * noise
        out[name] = jnp.asarray(drawn.astype(out[name].dtype))
    for name, factor in factors.items():
        out[name] = (out[name] * factor).astype(out[name].dtype)
    return out
```

```python
from contextlib import ExitStack

import numpy as np
import concourse.bass as bass
from concourse import mybir

F32 = mybir.dt.float32
F32R = mybir.dt.float32r
ALU = mybir.AluOpType
ACT = mybir.ActivationFunctionType
AX = mybir.AxisListType

P = 128
T = 256
NT = T // P
D = 1024
KC = D // P
FF = 2816
HD = 64
EPS = 1e-6
NEG = -1e30
TINY = 1e-30
CW = 512
CC = CW // P
WINDOWS = (2, 4, 8, 16)
CONF_K = 31
N_CMP = (T - 32) // 16 + 1
N_BUCKETS = 32
H_TOT = 40
DREL = T + P

RAW = 3
SPLIT = 3
TILE = 2048
FFC = 256
FSTEPS = FF // FFC

V_NORM_MIX, V_NORM_FFN, V_LN2, V_CONV_A, V_POOL_S, V_DWB, V_LNG, V_LNB, V_QK, V_POS = (
    0, 16, 32, 40, 52, 56, 60, 64, 68, 74)
V_ROWS = 106


def constants():
    t = np.arange(T)
    inv = (1.0 / (np.float32(10000.0) ** (np.arange(0, HD, 2, dtype=np.float32) / np.float32(HD)))).astype(np.float32)
    ang = t.astype(np.float32)[:, None] * inv[None, :]
    cnt = np.stack([np.minimum(t + 1, w) for w in WINDOWS]).astype(np.float32)
    dist = 255 - np.arange(DREL)
    d0 = np.maximum(dist, 0)
    large = 16 + (np.log(np.maximum(d0, 1).astype(np.float32) / np.float32(16))
                  / np.float32(np.log(2048 / 16)) * 16).astype(np.int32)
    bucket = np.where(d0 < 16, d0, np.minimum(large, N_BUCKETS - 1))
    onehot = (bucket[None, :] == np.arange(N_BUCKETS)[:, None]).astype(np.float32)
    ok = dist >= 0
    rows = [ok] * 8 + [ok & (dist <= 128)] * 8 + [ok & (dist % 4 == 0)] * 8 + [ok & (dist % 16 == 0)] * 8 \
        + [ok & (dist < 128)] * 8
    relmask = np.where(np.stack(rows), 0.0, NEG).astype(np.float32)
    p = np.arange(P)
    causal = np.where(p[:, None] + P - t[None, :] >= 0, 0.0, NEG).astype(np.float32)
    cmp_end = np.arange(N_CMP) * 16 + 31
    seen = (cmp_end[None, :] <= t[:, None]).astype(np.float32)
    return {
        "c_ident": np.eye(P, dtype=np.float32),
        "c_cos": np.cos(ang).astype(np.float32),
        "c_sin": np.sin(ang).astype(np.float32),
        "c_rcnt": (np.float32(1) / cnt).astype(np.float32),
        "c_onehot": onehot,
        "c_relmask": relmask,
        "c_causal": causal,
        "c_seen": seen,
        "c_unseen": np.where(seen > 0, 0.0, NEG).astype(np.float32),
    }


def tile_list(a):
    def feature(w, c0):
        return w.rearrange("(k p) n -> p k n", p=P)[:, :, c0:c0 + 256]

    def token(w, c0, half):
        return w.rearrange("(k p) n -> p k n", p=P)[:, 4 * half:4 * half + 4, c0:c0 + 512]

    def rows(w, r):
        return w.rearrange("(k p) n -> p k n", p=P)[:, 2 * r:2 * r + 2, :]

    w = a["w_in_even"][0]
    mix0 = [feature(w, c) for c in (1536, 1792, 512, 1024, 0, 768, 1280, 256)]
    mix0 += [rows(a["w_out_even"][0], r) for r in (2, 3, 0, 1)]
    w = a["w_in_odd"][0]
    conf = 512 + 6 * 128 + 24
    mix1 = [feature(w, conf + 512), feature(w, conf)]
    mix1 += [token(w, 0, 0), token(w, 0, 1), token(w, 512, 0), token(w, 512, 1), feature(w, 1024)]
    mix1 += [feature(w, conf + 768), feature(w, conf + 256)]
    for kv in range(2):
        c = a["cmp_w1"][0, kv].rearrange("(k p) n -> p k n", p=P)
        mix1 += [c[:, 0:8, :], c[:, 8:16, :]]
    mix1 += [rows(a["w_out_odd"][0], r) for r in range(4)]
    return mix0, mix1


SCRATCH = 22800


def build(nc, a, out):
    ctx = ExitStack()
    with ctx:
        def sb(name, shape, dt=F32):
            return ctx.enter_context(nc.sbuf_tensor(name + "_sb", shape, dt))

        def sem(name):
            return ctx.enter_context(nc.semaphore(name))

        raw = sb("raw", [P, RAW, TILE])
        whi = sb("whi", [P, SPLIT, TILE], F32R)
        wlo = sb("wlo", [P, SPLIT, TILE], F32R)
        x = sb("x", [P, NT, D])
        hhi = sb("hhi", [P, KC, T], F32R)
        hlo = sb("hlo", [P, KC, T], F32R)
        yhi = sb("yhi", [P, KC, T], F32R)
        ylo = sb("ylo", [P, KC, T], F32R)
        gwhi = sb("gwhi", [P, KC, 24], F32R)
        gwlo = sb("gwlo", [P, KC, 24], F32R)
        ident = sb("ident", [P, P])
        vec = sb("vec", [P, V_ROWS])
        dwv = sb("dwv", [P, CONF_K, CC])
        qk8 = sb("qk8", [P, 6])
        eps = sb("eps", [P, 1])
        nhalf = sb("nhalf", [P, 24])
        ssum = sb("ssum", [P, NT])
        smean = sb("smean", [P, NT])
        sinv = sb("sinv", [P, NT])
        b_ss = sb("b_ss", [P, 2, 2, NT, 8])
        b_inv = sb("b_inv", [P, 2, NT, 8])
        comb = sb("comb", [P, 8, 2, 8])
        nsink = sb("nsink", [P, 2, 8])
        onesd = sb("onesd", [P, P])
        nmax = sb("nmax", [P, 10, 8])
        psum_ = sb("psum_", [P, 10, 8])
        rsum = sb("rsum", [P, 10, 8])
        ps = ctx.enter_context(nc.psum_tensor("ps", [P, 8, 512], F32))
        scratch = sb("scratch", [P, SCRATCH])

        def carver(start=0):
            at = [start]

            def carve(*shape):
                n = int(np.prod(shape))
                part = scratch[:, at[0]:at[0] + n]
                at[0] += n
                assert at[0] <= SCRATCH, at[0]
                if len(shape) > 1:
                    names = "abcd"[:len(shape)]
                    part = part.rearrange(f"p ({' '.join(names)}) -> p {' '.join(names)}",
                                          **{c: m for c, m in zip(names, shape)})
                return part
            carve.at = at
            return carve

        def scratch_at(carve):
            return carve.at[0]

        carve = carver()
        xn = carve(NT, D)
        sg = carve(2, 2, T)
        gu = carve(2, 2, T)
        ghi = yhi[:, 0:4, :].rearrange("p (b f) t -> p b f t", b=2)
        glo = ylo[:, 0:4, :].rearrange("p (b f) t -> p b f t", b=2)
        carve = carver(NT * D)
        pool_a = carve(CC, 272)
        pool_b = carve(CC, 272)
        pool_c = carve(CC, 272)
        ctile = carve(CC, T)
        cvp = carve(CC, T + 2)
        yb = carve(CC, T)
        rcnt = carve(CC, T)
        pw = carve(CC, P)
        vrow = carve(P)[0:V_ROWS, :]
        vrow2 = carve(P)[0:CONF_K * CC, :]
        relb = carve(N_BUCKETS)[0:H_TOT]
        relT = carve(H_TOT)[0:N_BUCKETS]
        onehot = carve(DREL)[0:N_BUCKETS]
        relmask = carve(DREL)[0:H_TOT]
        relrow = carve(DREL)[0:H_TOT]

        carve = carver(NT * D)
        th = carve(2, 2, T)
        dsq = th.rearrange("p a b t -> p (a b) t")
        zp = carve(CC, T + CONF_K - 1)
        zc = carve(CC, T)
        rstd = carve(T)
        uk = carve(NT, 6, 2, HD)
        cosn = carve(NT, HD // 2)
        sinn = carve(NT, HD // 2)
        causal = carve(T)
        qT = carve(CC, T)
        kT = carve(2, 2, T)
        tok2 = carve(2, 2, T)
        flat = carve(2, 16, 2 * N_CMP)
        hid = carve(5, 2, 2 * N_CMP)
        hid2 = carve(2, 2, 2 * N_CMP)
        cw2 = carve(2, 2, HD)
        kcn = carve(4, 2, 2, HD)[0:N_CMP]
        vcs = carve(2, HD)[0:N_CMP]
        g2 = carve(HD)[0:N_CMP]
        kcT = carve(2, 16)
        seen = carve(NT, N_CMP)
        unseen = carve(NT, N_CMP)
        gwr = carve(KC, 24)
        gth = carve(NT, 24)
        gate3 = carve(NT, 24)
        cst = carve(NT, 4, 8)
        wgt = carve(NT, 3, 8)
        u_ss = carve(2, NT, 12)
        u_inv = carve(NT, 12)
        kc_ss = carve(3, 2)[0:N_CMP]
        early = carver(scratch_at(carve))
        uq = early(NT, 8, HD)
        usq = early(12, HD)
        rt = early(4, 20, HD // 2)
        gains = early(16, HD)
        hb = early(NT, 24, HD)
        obr = carve(NT, 2, 512)
        oacc = carve(NT, 512)
        ot = carve(2, 512)
        pc = carve(NT, 8, N_CMP)
        pcT = carve(8, P)[0:N_CMP]
        carve = carver()
        qraw = carve(NT, 512)
        kraw = carve(NT, 512)
        vb = carve(2, NT, 512)
        q2T = carve(2, CC, T)
        k2T = carve(2, CC, T)
        bt = carve(2, 4, T)
        ob = carve(4, NT, 512)
        gsil = carve(2, NT, 512)
        gs = carve(4, T)
        rb = carve(4, T)
        macc = carve(KC, T)
        gth2 = gs.rearrange("p (i a) t -> p i (a t)", i=2)
        brT = rb
        mt = scratch[:, 0:CC * T].rearrange("p (c t) -> p c t", c=CC)
        late_end = scratch_at(carve)
        carve = carver(SCRATCH - 8 * T)
        lg = carve(2, T)
        pr = carve(4, T)
        pT = carve(2, 2, P)

        bias_dram = nc.dram_tensor("bias_rows_dram", (H_TOT, P, DREL), F32, kind="Internal").ap()
        JOB_START, JOB_TAIL = (3, 1, 1, 1, 0), (1, 1, 1, 10, 1)

        tile_landed = [sem(f"tile_landed{r}") for r in range(RAW)]
        hi_ready, lo_ready, tile_used = sem("hi_ready"), sem("lo_ready"), sem("tile_used")
        x_landed, consts_landed = sem("x_landed"), sem("consts_landed")
        eps_set, zero_set = sem("eps_set"), sem("zero_set")
        vec_T, vec_ready = sem("vec_T"), sem("vec_ready")
        sq_sum, rms_mean, rms_inv = sem("sq_sum"), sem("rms_mean"), sem("rms_inv")
        xn_ready, xn_T, h_hi, h_lo = sem("xn_ready"), sem("xn_T"), sem("h_hi"), sem("h_lo")
        x_added, out_done = sem("x_added"), sem("out_done")
        c_copied, cv_ready, conv_step, yc_ready, v_copied = (
            sem("c_copied"), sem("cv_ready"), sem("conv_step"), sem("yc_ready"), sem("v_copied"))
        pool_step, pool_mm = sem("pool_step"), sem("pool_mm")
        y_hi, y_lo = sem("y_hi"), sem("y_lo")
        bias_loaded, bias_T, bias_copied, bias_mm, bias_rows, bias_written, bt_landed, sink_landed = (
            sem("bias_loaded"), sem("bias_T"), sem("bias_copied"), sem("bias_mm"), sem("bias_rows"),
            sem("bias_written"), [sem(f"bt_landed{g}") for g in range(2)], sem("sink_landed"))
        emptied, b_squared, b_summed, b_mean, b_root, b_scaled, b_T, b_gated = (
            sem("emptied"), sem("b_squared"), sem("b_summed"), sem("b_mean"), sem("b_root"), sem("b_scaled"),
            sem("b_T"), sem("b_gated"))
        b_tanh, b_silu = sem("b_tanh"), sem("b_silu")
        c_step, c_exp, o_scaled, o_gated, br_hi, br_lo, m_mul, m_sum, m_hi, m_lo = (
            sem("c_step"), sem("c_exp"), sem("o_scaled"), sem("o_gated"), sem("br_hi"), sem("br_lo"),
            sem("m_mul"), sem("m_sum"), sem("m_hi"), sem("m_lo"))
        nhalf_set, half_set = sem("nhalf_set"), sem("half_set")
        vec_landed, ident_landed, pw_landed = sem("vec_landed"), sem("ident_landed"), sem("pw_landed")
        silu_ready, gu_ready, gu_hi, gu_lo = sem("silu_ready"), sem("gu_ready"), sem("gu_hi"), sem("gu_lo")
        stored = sem("stored")
        s_ready, s_shifted, p_ready, pT_ready, pT_copied, pv_done, o_copied = (
            sem("s_ready"), sem("s_shifted"), sem("p_ready"), sem("pT_ready"), sem("pT_copied"),
            sem("pv_done"), sem("o_copied"))
        m1_consts, zpad_set, g_hi, g_lo, gates_done, gate_tanh, gate_ready = (
            sem("m1_consts"), sem("zpad_set"), sem("g_hi"), sem("g_lo"), sem("gates_done"), sem("gate_tanh"),
            sem("gate_ready"))
        th_ready, z_ready, conf_step, u_copied, u_squared, u_summed, u_mean, u_root = (
            sem("th_ready"), sem("z_ready"), sem("conf_step"), sem("u_copied"), sem("u_squared"),
            sem("u_summed"), sem("u_mean"), sem("u_root"))
        u_normed, kv_copied, rope_v, rope_p, heads_T, qT_ready, tok_ready = (
            sem("u_normed"), sem("kv_copied"), sem("rope_v"), sem("rope_p"), sem("heads_T"), sem("qT_ready"),
            sem("tok_ready"))
        flat_ready, flat_hi, flat_lo, hid_copied, gelu_step, gelu_tanh, w2_done = (
            sem("flat_ready"), sem("flat_hi"), sem("flat_lo"), sem("hid_copied"), sem("gelu_step"),
            sem("gelu_tanh"), sem("w2_done"))
        kc_copied, kc_step, kc_summed, kc_T, kcT_ready = (
            sem("kc_copied"), sem("kc_step"), sem("kc_summed"), sem("kc_T"), sem("kcT_ready"))
        cs_ready, cs_step, cs_exp, pc_T, pcT_ready, oc_done = (
            sem("cs_ready"), sem("cs_step"), sem("cs_exp"), sem("pc_T"), sem("pcT_ready"), sem("oc_done"))
        fin_w, fin_v, fin_p, oacc_ready, oT_done, oT_hi, oT_lo = (
            sem("fin_w"), sem("fin_v"), sem("fin_p"), sem("oacc_ready"), sem("oT_done"), sem("oT_hi"),
            sem("oT_lo"))
        ln_mm, ln_dev, ln_sq, ln_root, ln_inv, ln_norm, z_silu, z_hi, z_lo = (
            sem("ln_mm"), sem("ln_dev"), sem("ln_sq"), sem("ln_root"), sem("ln_inv"), sem("ln_norm"),
            sem("z_silu"), sem("z_hi"), sem("z_lo"))

        mix0, mix1 = tile_list(a)
        N_MIX0 = 0
        N_FFN0 = N_MIX0 + len(mix0)
        N_MIX1 = N_FFN0 + 3 * FSTEPS
        N_FFN1 = N_MIX1 + len(mix1)
        N_B2 = N_FFN1 + 3 * FSTEPS
        total_tiles = N_B2 + 55

        def split_hi(act, n0, i=0):
            if isinstance(i, int) and n0 + 6 * i >= total_tiles:
                return
            act.wait_ge(tile_landed[n0 % RAW], i * (16 * 6 // RAW) + 16 * (n0 // RAW + 1))
            if not isinstance(i, int) or n0 + 6 * i >= SPLIT:
                act.wait_ge(tile_used, i * 6 + (n0 - SPLIT + 1))
            nc.scalar.activation(whi[:, n0 % SPLIT, :], raw[:, n0 % RAW, :], ACT.Copy).then_inc(hi_ready, 1)

        def split_lo(dve, n0, i=0):
            if isinstance(i, int) and n0 + 6 * i >= total_tiles:
                return
            dve.wait_ge(hi_ready, i * 6 + (n0 + 1))
            nc.vector.tensor_tensor(wlo[:, n0 % SPLIT, :], raw[:, n0 % RAW, :],
                                    whi[:, n0 % SPLIT, :].bitcast(F32), ALU.subtract).then_inc(lo_ready, 1)

        def load_tile(sp, n0, src, i=0):
            if not isinstance(i, int) or n0 + 6 * i >= RAW:
                sp.wait_ge(lo_ready, i * 6 + (n0 - RAW + 1))
            sp.dma_start(raw[:, n0 % RAW, :].rearrange("p (k n) -> p k n", k=src.shape[1]),
                         src).then_inc(tile_landed[n0 % RAW], 16)

        def product(dst, l_hi, l_lo, r_hi, r_lo, first, last):
            nc.tensor.matmul(dst, l_hi, r_hi, start=first, stop=False)
            nc.tensor.matmul(dst, l_hi, r_lo, start=False, stop=False)
            return nc.tensor.matmul(dst, l_lo, r_hi, start=False, stop=last)

        def w_parts(n, k):
            s = n % SPLIT
            return (whi[:, s, :].rearrange("p (k n) -> p k n", k=k), wlo[:, s, :].rearrange("p (k n) -> p k n", k=k))

        def mm_feature(n, bank):
            nc.tensor.wait_ge(lo_ready, n + 1)
            hi, lo = w_parts(n, KC)
            for f in range(2):
                for k in range(KC):
                    c = slice(f * P, f * P + P)
                    mm = product(ps[:, bank, f * T:(f + 1) * T], hi[:, k, c], lo[:, k, c],
                                 hhi[:, k, :], hlo[:, k, :], k == 0, k == KC - 1)
            mm.then_inc(tile_used, 1)

        def mm_rows(n, lhs_hi, lhs_lo, k0, first, last, bank=0):
            hi, lo = w_parts(n, 2)
            for k in range(2):
                for i in range(NT):
                    for h in range(2):
                        tok, c = slice(i * P, i * P + P), slice(h * 512, h * 512 + 512)
                        mm = product(ps[:, bank + 2 * i + h, :], lhs_hi[:, k0 + k, tok], lhs_lo[:, k0 + k, tok],
                                     hi[:, k, c], lo[:, k, c], first and k == 0, last and k == 1)
            return mm

        def norm_act(act, e, v0):
            act.wait_ge(x_landed, 16)
            if e:
                act.wait_ge(x_added, 4 * e)
            for i in range(NT):
                nc.scalar.activation(xn[:, i, :], x[:, i, :], ACT.Square,
                                     accum_out=ssum[:, i:i + 1]).then_inc(sq_sum, 1)
            for k in range(KC):
                act.wait_ge(xn_T, 4 * e + k // 2 + 1)
                if k == 0:
                    act.wait_ge(vec_ready, 2)
                nc.scalar.activation(hhi[:, k, :], ps[:, 4 + k // 2, (k % 2) * T:(k % 2 + 1) * T], ACT.Copy,
                                     scale=vec[:, v0 + k:v0 + k + 1]).then_inc(h_hi, 1)

        def norm_pool(pool, e):
            pool.wait_ge(sq_sum, NT * (e + 1))
            nc.gpsimd.tensor_scalar(smean[:, :], ssum[:, :], 1.0 / D, EPS, ALU.mult, ALU.add)\
                .then_inc(rms_mean, 1)
            pool.wait_ge(rms_mean, e + 1)
            nc.gpsimd.tensor_tensor(sinv[:, :], smean[:, :], nhalf[:, 0:NT], ALU.pow).then_inc(rms_inv, 1)

        def norm_dve(dve, e, v0):
            dve.wait_ge(rms_inv, e + 1)
            for i in range(NT):
                nc.vector.tensor_scalar(xn[:, i, :], x[:, i, :], sinv[:, i:i + 1], None,
                                        ALU.mult).then_inc(xn_ready, 1)
            for k in range(KC):
                dve.wait_ge(h_hi, KC * e + k // 2 * 2 + 2)
                nc.vector.scalar_tensor_tensor(hlo[:, k, :], ps[:, 4 + k // 2, (k % 2) * T:(k % 2 + 1) * T],
                                               vec[:, v0 + k:v0 + k + 1], hhi[:, k, :].bitcast(F32),
                                               ALU.mult, ALU.subtract).then_inc(h_lo, 1)

        def norm_pe(pe, e):
            pe.wait_ge(xn_ready, NT * (e + 1))
            for k in range(KC):
                for i in range(NT):
                    c = (k % 2) * T + i * P
                    mm = nc.tensor.transpose(ps[:, 4 + k // 2, c:c + P], xn[:, i, k * P:(k + 1) * P], ident[:, :])
                if k % 2:
                    mm.then_inc(xn_T, 1)
            pe.wait_ge(h_lo, KC * (e + 1))

        def add_x(bank=0):
            for j in range(4):
                i, h = j // 2, j % 2
                xs = x[:, i, h * 512:(h + 1) * 512]
                nc.vector.tensor_tensor(xs, xs, ps[:, bank + j, :], ALU.add).then_inc(x_added, 1)

        def g_tile(n, c):
            return n if c == 0 else n + 3 * c - 1

        def d_tile(n, c):
            return n + 3 * c + 4 if c < FSTEPS - 1 else n + 3 * c + 2

        def ffn_src(l, kind, c):
            if kind == "d":
                return a["ffn_down"][l].rearrange("(k p) n -> p k n", p=P)[:, bass.ds(c * 2, 2), :]
            w = a["ffn_gate" if kind == "g" else "ffn_up"][l]
            return w.rearrange("(k p) n -> p k n", p=P)[:, :, bass.ds(c * FFC, FFC)]

        def steps_of(engine, step, tail):
            step(0, 0)
            step(1, 0)
            with engine.Fori(0, 4) as i:
                step(2, i)
                step(3, i)
            step(10, 0)
            tail()

        def ffn_sp(sp, l, n):
            def step(c, i):
                load_tile(sp, g_tile(n, c), ffn_src(l, "g", i * 2 + c), i)
                load_tile(sp, g_tile(n, c) + 1, ffn_src(l, "u", i * 2 + c), i)
                if c:
                    load_tile(sp, d_tile(n, c - 1), ffn_src(l, "d", i * 2 + (c - 1)), i)
            steps_of(sp, step, lambda: load_tile(sp, n + 32, ffn_src(l, "d", FSTEPS - 1)))

        def ffn_act(act, l, n):
            def step(c, i):
                g, b = g_tile(n, c), 4 + 2 * (c % 2)
                split_hi(act, g + 2, i)
                act.wait_ge(tile_used, i * 6 + (g + 1))
                nc.scalar.activation(sg[:, c % 2, :, :].rearrange("p f t -> p (f t)"), ps[:, b, :],
                                     ACT.Silu).then_inc(silu_ready, 1)
                if c:
                    split_hi(act, g + 3, i)
                split_hi(act, g + 3 + (1 if c else 0), i)
                act.wait_ge(gu_ready, i * 2 + (FSTEPS * l + c + 1))
                nc.scalar.activation(ghi[:, c % 2, :, :], gu[:, c % 2, :, :], ACT.Copy).then_inc(gu_hi, 1)
            steps_of(act, step, lambda: split_hi(act, n + 34))

        def ffn_dve(dve, l, n):
            def step(c, i):
                g, b = g_tile(n, c), 4 + 2 * (c % 2)
                split_lo(dve, g + 2, i)
                if c:
                    split_lo(dve, g + 3, i)
                dve.wait_ge(silu_ready, i * 2 + (FSTEPS * l + c + 1))
                dve.wait_ge(tile_used, i * 6 + (g + 2))
                nc.vector.tensor_tensor(gu[:, c % 2, :, :].rearrange("p f t -> p (f t)"),
                                        sg[:, c % 2, :, :].rearrange("p f t -> p (f t)"),
                                        ps[:, b + 1, :], ALU.mult).then_inc(gu_ready, 1)
                split_lo(dve, g + 3 + (1 if c else 0), i)
                dve.wait_ge(gu_hi, i * 2 + (FSTEPS * l + c + 1))
                nc.vector.tensor_tensor(glo[:, c % 2, :, :], gu[:, c % 2, :, :],
                                        ghi[:, c % 2, :, :].bitcast(F32), ALU.subtract).then_inc(gu_lo, 1)
            steps_of(dve, step, lambda: split_lo(dve, n + 34))
            dve.wait_ge(tile_used, n + 3 * FSTEPS)
            add_x()

        def ffn_pe(pe, l, n):
            def down(c, i, first=False):
                t = d_tile(n, c)
                pe.wait_ge(lo_ready, i * 6 + (t + 1))
                pe.wait_ge(gu_lo, i * 2 + (FSTEPS * l + c + 1))
                mm = mm_rows(t, ghi[:, c % 2, :, :], glo[:, c % 2, :, :], 0, first, c == FSTEPS - 1)
                mm.then_inc(tile_used, 1)

            def step(c, i):
                g, b = g_tile(n, c), 4 + 2 * (c % 2)
                if c >= 2:
                    pe.wait_ge(gu_ready, i * 2 + (FSTEPS * l + c - 1))
                for t, bank in ((g, b), (g + 1, b + 1)):
                    pe.wait_ge(lo_ready, i * 6 + (t + 1))
                    hi, lo = w_parts(t, KC)
                    for f in range(2):
                        for k in range(KC):
                            cs = slice(f * P, f * P + P)
                            mm = product(ps[:, bank, f * T:(f + 1) * T], hi[:, k, cs], lo[:, k, cs],
                                         hhi[:, k, :], hlo[:, k, :], k == 0, k == KC - 1)
                    mm.then_inc(tile_used, 1)
                if c:
                    down(c - 1, i, c == 1)
            steps_of(pe, step, lambda: down(FSTEPS - 1, 0))

        def o_bank(g):
            return 4 + g % 2 if g < 4 else 4

        def job_s(pe, jobs, m0, m):
            q, k, bias, v, g = jobs[m]
            if m0 + m >= 2:
                pe.wait_ge(s_shifted, m0 + m - 1)
            nc.tensor.matmul(ps[:, (m0 + m) % 2, 0:len(v) * P], q, k, start=True, stop=True).then_inc(s_ready, 1)

        def job_t(pe, jobs, m0, m):
            n = m0 + m
            pe.wait_ge(p_ready, n + 1)
            if n >= 2:
                pe.wait_ge(pT_copied, n - 1)
            for j in range(len(jobs[m][3])):
                mm = nc.tensor.transpose(ps[:, 2 + n % 2, j * P:(j + 1) * P], pr[:, n % 4, j * P:(j + 1) * P],
                                         ident[:, :])
            mm.then_inc(pT_ready, 1)

        def job_pv(pe, jobs, m0, m):
            n, v, g = m0 + m, jobs[m][3], (m0 + m) // 8
            pe.wait_ge(pT_copied, n + 1)
            if n % 8 == 0 and g >= 2:
                pe.wait_ge(o_copied, g if g >= 4 else g - 1)
            for j in range(len(v)):
                mm = nc.tensor.matmul(ps[:, o_bank(g), (n % 8) * HD:(n % 8 + 1) * HD], pT[:, n % 2, j, :], v[j],
                                      start=(j == 0), stop=(j == len(v) - 1))
            mm.then_inc(pv_done, 1)

        def job_shift(dve, jobs, m0, m):
            n, (q, k, bias, v, g) = m0 + m, jobs[m]
            w = len(v) * P
            dve.wait_ge(s_ready, n + 1)
            if n >= 2:
                dve.wait_ge(p_ready, n - 1)
            nc.vector.tensor_tensor_reduce(lg[:, n % 2, 0:w], ps[:, n % 2, 0:w], bias, -1.0, 3e38, ALU.add,
                                           ALU.min, nmax[:, g, n % 8:n % 8 + 1]).then_inc(s_shifted, 1)

        def job_copy(dve, jobs, m0, m):
            n, w = m0 + m, len(jobs[m][3]) * P
            dve.wait_ge(pT_ready, n + 1)
            if n >= 2:
                dve.wait_ge(pv_done, n - 1)
            nc.vector.tensor_copy(pT[:, n % 2, :, :].rearrange("p j q -> p (j q)")[:, 0:w],
                                  ps[:, 2 + n % 2, 0:w]).then_inc(pT_copied, 1)

        def job_exp(act, jobs, m0, m):
            n, (q, k, bias, v, g) = m0 + m, jobs[m]
            w = len(v) * P
            act.wait_ge(s_shifted, n + 1)
            if n >= 4:
                act.wait_ge(pT_ready, n - 3)
            nc.scalar.activation(pr[:, n % 4, 0:w], lg[:, n % 2, 0:w], ACT.Exp, scale=-1.0,
                                 bias=nmax[:, g, n % 8:n % 8 + 1],
                                 accum_out=psum_[:, g, n % 8:n % 8 + 1]).then_inc(p_ready, 1)

        def group_out(act, g, dst, src=lambda bank: bank):
            act.wait_ge(pv_done, 8 * g + 8)
            nc.scalar.activation(dst, src(ps[:, o_bank(g), :]), ACT.Copy).then_inc(o_copied, 1)

        def pe_step(pe, jobs, m0, m):
            if m + 2 < len(jobs):
                job_s(pe, jobs, m0, m + 2)
            if 0 <= m < len(jobs):
                job_t(pe, jobs, m0, m)
            if m >= 1:
                job_pv(pe, jobs, m0, m - 1)

        def dve_step(dve, jobs, m0, m):
            if 0 <= m + 1 < len(jobs):
                job_shift(dve, jobs, m0, m + 1)
            if 0 <= m < len(jobs):
                job_copy(dve, jobs, m0, m)

        def act_step(act, jobs, m0, m):
            if 0 <= m + 1 < len(jobs):
                job_exp(act, jobs, m0, m + 1)

        jobs1 = []
        for i in range(NT):
            for br in range(2):
                for h in range(8):
                    half = slice((h % 2) * HD, (h % 2) * HD + HD)
                    jobs1.append((qT[half, h // 2, i * P:(i + 1) * P], kT[half, br, h // 4, 0:(i + 1) * P],
                                  causal[:, (1 - i) * P:T], [uk[:, j, 3 + 2 * br, h // 4, :] for j in range(i + 1)],
                                  2 * i + br))
        TOK, CMP, OUT1 = N_MIX1 + 2, N_MIX1 + 9, N_MIX1 + 13
        CONF = ((N_MIX1, N_MIX1 + 1), (N_MIX1 + 7, N_MIX1 + 8))
        CMP_STEP, GELU_STEP = (-2, 1, 8, 11), (3, 13)
        W2_STEP, KCT_STEP, SC_STEP, PCT_STEP, OC_STEP = (7, 16), 18, (19, 28), (22, 30), (24, 32)
        FIN_STEP, OT_STEP = (25, 33), (26, 34)

        def mix1_pe(pe):
            mm_feature(CONF[0][0], 0)
            mm_feature(CONF[0][1], 1)
            for t in range(2):
                for half in range(2):
                    n = TOK + 2 * t + half
                    pe.wait_ge(lo_ready, n + 1)
                    hi, lo = w_parts(n, 4)
                    for i in range(NT):
                        tok = slice(i * P, (i + 1) * P)
                        for k in range(4):
                            mm = product(ps[:, 4 + 2 * t + i, :], hhi[:, 4 * half + k, tok],
                                         hlo[:, 4 * half + k, tok], hi[:, k, :], lo[:, k, :],
                                         half == 0 and k == 0, half == 1 and k == 3)
                    mm.then_inc(tile_used, 1)
            n = TOK + 4
            pe.wait_ge(lo_ready, n + 1)
            pe.wait_ge(g_lo, 1)
            hi, lo = w_parts(n, KC)
            for i in range(NT):
                tok = slice(i * P, (i + 1) * P)
                for k in range(KC):
                    mm = product(ps[:, 2 + i, 256:280], hhi[:, k, tok], hlo[:, k, tok], gwhi[:, k, :],
                                 gwlo[:, k, :], k == 0, k == KC - 1)
                for k in range(KC):
                    mm = product(ps[:, 2 + i, 0:256], hhi[:, k, tok], hlo[:, k, tok], hi[:, k, :],
                                 lo[:, k, :], k == 0, k == KC - 1)
            mm.then_inc(tile_used, 1)
            pe.wait_ge(th_ready, 1)
            mm_feature(CONF[1][0], 0)
            pe.wait_ge(z_ready, 2)
            mm_feature(CONF[1][1], 1)
            pe.wait_ge(u_copied, 6)
            for i in range(NT):
                pe.wait_ge(rope_v, 3 * (i + 1))
                pe.wait_ge(rope_p, 3 * (i + 1))
                for c in range(12):
                    at = (c % 2) * T + i * P
                    mm = nc.tensor.transpose(ps[:, (4, 5, 6, 7, 2, 3)[c // 2], at:at + P],
                                             hb[:, i, 2 * c:2 * c + 2, :].rearrange("p h d -> p (h d)"), ident[:, :])
            mm.then_inc(heads_T, 1)
            pe.wait_ge(qT_ready, 4)
            pe.wait_ge(tok_ready, 8)
            pe.wait_ge(th_ready, 2)
            pe.wait_ge(z_ready, 4)
            for m in range(-2, 35):
                if m in CMP_STEP:
                    r = CMP_STEP.index(m)
                    kv, half = r // 2, r % 2
                    n = CMP + r
                    pe.wait_ge(lo_ready, n + 1)
                    pe.wait_ge(flat_lo, kv + 1)
                    if r == 2:
                        pe.wait_ge(hid_copied, 2)
                        pe.wait_ge(kc_copied, 1)
                    hi, lo = w_parts(n, KC)
                    for hc in range(2):
                        c = slice(hc * P, hc * P + P)
                        for k in range(KC):
                            fh = flat_part(yhi, kv)[:, 8 * half + k, :]
                            fl = flat_part(ylo, kv)[:, 8 * half + k, :]
                            mm = product(ps[:, 6 + hc, kv * 32:kv * 32 + 2 * N_CMP], hi[:, k, c], lo[:, k, c],
                                         fh, fl, half == 0 and k == 0, half == 1 and k == KC - 1)
                    mm.then_inc(tile_used, 1)
                pe_step(pe, jobs1, 0, m) if m <= len(jobs1) else None
                if m in W2_STEP:
                    kv = W2_STEP.index(m)
                    pe.wait_ge(gelu_step, 5 * (kv + 1))
                    for g in range(2):
                        for hc in range(2):
                            mm = nc.tensor.matmul(ps[0:N_CMP, 6 + kv, 128 + g * HD:128 + (g + 1) * HD],
                                                  hid2[:, kv, hc, g * N_CMP:(g + 1) * N_CMP], cw2[:, kv, hc, :],
                                                  start=(hc == 0), stop=(hc == 1))
                    mm.then_inc(w2_done, 1)
                if m == KCT_STEP:
                    pe.wait_ge(kc_step, 5)
                    pe.wait_ge(kc_copied, 2)
                    for g in range(2):
                        mm = nc.tensor.transpose(ps[:, 7, g * 16:g * 16 + N_CMP],
                                                 kcn[:, 3, g, :, :].rearrange("p c d -> p (c d)"),
                                                 ident[0:N_CMP, 0:N_CMP])
                    mm.then_inc(kc_T, 1)
                if m in SC_STEP:
                    i = SC_STEP.index(m)
                    pe.wait_ge(kcT_ready, 1)
                    if i:
                        pe.wait_ge(oT_lo, 1)
                    for h in range(8):
                        half = slice((h % 2) * HD, (h % 2) * HD + HD)
                        mm = nc.tensor.matmul(ps[:, 6 + h % 2, h // 2 * N_CMP:(h // 2 + 1) * N_CMP], qT[half, h // 2, i * P:(i + 1) * P],
                                              kcT[half, h // 4, 0:N_CMP], start=True, stop=True)
                    mm.then_inc(cs_ready, 1)
                if m in PCT_STEP:
                    i = PCT_STEP.index(m)
                    pe.wait_ge(cs_step, 7 * i + 4)
                    for h in range(8):
                        mm = nc.tensor.transpose(ps[0:N_CMP, 6 + h // 4, (h % 4) * P:(h % 4 + 1) * P],
                                                 pc[:, i, h, :], ident[:, :])
                    mm.then_inc(pc_T, 1)
                if m in OC_STEP:
                    i = OC_STEP.index(m)
                    pe.wait_ge(pcT_ready, 2 * i + 2)
                    for h in range(8):
                        mm = nc.tensor.matmul(ps[:, 6, h * HD:(h + 1) * HD], pcT[:, h, :], vcs[:, h // 4, :],
                                              start=True, stop=True)
                    mm.then_inc(oc_done, 1)
                if m in OT_STEP:
                    i = OT_STEP.index(m)
                    pe.wait_ge(oacc_ready, i + 1)
                    for c in range(4):
                        mm = nc.tensor.transpose(ps[:, 7, c * P:(c + 1) * P], oacc[:, i, c * P:(c + 1) * P], ident[:, :])
                    mm.then_inc(oT_done, 1)
            def channel_mean(src, bank):
                for c in range(CC):
                    mm = nc.tensor.matmul(ps[:, bank, 0:T], onesd[:, :], src[:, c, :], start=(c == 0),
                                          stop=(c == CC - 1))
                mm.then_inc(ln_mm, 1)

            def out_rows(j, k0, first, last):
                n = OUT1 + j
                pe.wait_ge(lo_ready, n + 1)
                mm_rows(n, yhi, ylo, k0, first, last).then_inc(tile_used, 1)
            pe.wait_ge(conf_step, CONF_K * CC)
            channel_mean(zc, 6)
            pe.wait_ge(oT_lo, 2)
            out_rows(0, 0, True, False)
            pe.wait_ge(ln_sq, 1)
            channel_mean(dsq, 5)
            out_rows(1, 2, False, False)
            pe.wait_ge(z_lo, 1)
            out_rows(2, 4, False, False)
            out_rows(3, 6, False, True)

        def flat_part(y, kv):
            return y[:, 2 * kv:2 * kv + 2, :].rearrange("p a t -> p (a t)")[:, 0:16 * 2 * N_CMP]\
                .rearrange("p (j n) -> p j n", j=16)

        def m1_loads(act):
            act.wait_ge(bias_written, 16)
            k_norm = a["k_norm"][0]
            w_gate = a["w_in_odd"][0].rearrange("(k p) n -> p k n", p=P)[:, :, 1280:1304]
            for dst, src in (
                    (gwr[:, :, :], w_gate),
                    (gains[:, 0:8, :], a["q_norm"][0:1].partition_broadcast(P).broadcast_to([P, 8, HD])),
                    (gains[:, 8:12, :], k_norm[0:1].partition_broadcast(P).broadcast_to([P, 4, HD])),
                    (gains[:, 12:16, :], k_norm[1:2].partition_broadcast(P).broadcast_to([P, 4, HD])),
                    (g2[:, :], k_norm[2].partition_broadcast(N_CMP)),
                    (cosn[:, :, :], a["c_cos"].rearrange("(i p) c -> p i c", p=P)),
                    (sinn[:, :, :], a["c_sin"].rearrange("(i p) c -> p i c", p=P)),
                    (causal[:, :], a["c_causal"]),
                    (seen[:, :, :], a["c_seen"].rearrange("(i p) c -> p i c", p=P)),
                    (unseen[:, :, :], a["c_unseen"].rearrange("(i p) c -> p i c", p=P)),
                    (cw2[:, 0, :, :], a["cmp_w2"][0, 0].rearrange("(c p) n -> p c n", p=P)),
                    (cw2[:, 1, :, :], a["cmp_w2"][0, 1].rearrange("(c p) n -> p c n", p=P))):
                act.dma_start(dst, src).then_inc(m1_consts, 16)

        def mix1_act(act):
            act.wait_ge(m1_consts, 16 * 12)
            nc.scalar.activation(gwhi[:, :, :], gwr[:, :, :], ACT.Copy).then_inc(g_hi, 1)

            def conf_tanh(pair):
                act.wait_ge(tile_used, CONF[pair][0] + 1)
                nc.scalar.activation(th[:, pair, :, :].rearrange("p f t -> p (f t)"), ps[:, 0, :], ACT.Tanh,
                                     scale=0.5).then_inc(th_ready, 1)

            for t in range(9):
                split_hi(act, N_MIX1 + t + 2)
                if t == 0:
                    conf_tanh(0)
                if t == 3:
                    act.wait_ge(tile_used, TOK + 2)
                    for i in range(NT):
                        nc.scalar.activation(uq[:, i, :, :].rearrange("p h d -> p (h d)"), ps[:, 4 + i, :],
                                             ACT.Copy).then_inc(u_copied, 1)
                if t == 5:
                    act.wait_ge(tile_used, TOK + 4)
                    for i in range(NT):
                        nc.scalar.activation(uk[:, i, 0:4, :, :].rearrange("p a g d -> p (a g d)"),
                                             ps[:, 6 + i, :], ACT.Copy).then_inc(u_copied, 1)
                if t == 6:
                    act.wait_ge(tile_used, TOK + 5)
                    for i in range(NT):
                        nc.scalar.activation(uk[:, i, 4:6, :, :].rearrange("p a g d -> p (a g d)"),
                                             ps[:, 2 + i, 0:256], ACT.Copy).then_inc(u_copied, 1)
                        nc.scalar.activation(gth[:, i, :], ps[:, 2 + i, 256:280], ACT.Tanh,
                                             scale=0.5).then_inc(gate_tanh, 1)
                if t == 7:
                    conf_tanh(1)
            act.wait_ge(heads_T, 1)
            for b in range(2):
                nc.scalar.activation(qT[:, 2 * b:2 * b + 2, :].rearrange("p c t -> p (c t)"), ps[:, 4 + b, :],
                                     ACT.Copy, scale=HD ** -0.5).then_inc(qT_ready, 1)
            for b in range(2):
                nc.scalar.activation(kT[:, b, :, :].rearrange("p c t -> p (c t)"), ps[:, 6 + b, :],
                                     ACT.Copy).then_inc(qT_ready, 1)
            for b in range(2):
                for c in range(2):
                    nc.scalar.activation(tok2[0:HD, b, c, :], ps[0:HD, 2 + b, c * T:(c + 1) * T],
                                         ACT.Copy).then_inc(tok_ready, 1)
                    nc.scalar.activation(tok2[HD:P, b, c, 0:T - 1], ps[HD:P, 2 + b, c * T + 1:(c + 1) * T],
                                         ACT.Copy).then_inc(tok_ready, 1)
            for kv in range(2):
                act.wait_ge(flat_ready, kv + 1)
                nc.scalar.activation(flat_part(yhi, kv), flat[:, kv, :, :], ACT.Copy).then_inc(flat_hi, 1)
            for m in range(-2, 35):
                if m in CMP_STEP:
                    split_hi(act, CMP + CMP_STEP.index(m) + 2)
                act_step(act, jobs1, 0, m)
                if m in GELU_STEP:
                    kv = GELU_STEP.index(m)
                    act.wait_ge(tile_used, CMP + 2 * kv + 2)
                    for hc in range(2):
                        nc.scalar.activation(hid[:, 0, hc, :], ps[:, 6 + hc, kv * 32:kv * 32 + 2 * N_CMP],
                                             ACT.Copy).then_inc(hid_copied, 1)
                    act.wait_ge(gelu_step, 5 * kv + 3)
                    nc.scalar.activation(hid[:, 3, :, :], hid[:, 3, :, :], ACT.Tanh,
                                         scale=0.7978845608028654).then_inc(gelu_tanh, 1)
                if m == W2_STEP[0] + 1:
                    act.wait_ge(w2_done, 1)
                    nc.scalar.activation(kcn[:, 0, :, 0, :], ps[0:N_CMP, 6, 128:256].rearrange("p (g d) -> p g d", g=2),
                                         ACT.Copy).then_inc(kc_copied, 1)
                if m == W2_STEP[1] + 1:
                    act.wait_ge(w2_done, 2)
                    nc.scalar.activation(vcs[:, :, :], ps[0:N_CMP, 7, 128:256].rearrange("p (g d) -> p g d", g=2),
                                         ACT.Copy).then_inc(kc_copied, 1)
                if m == KCT_STEP:
                    act.wait_ge(kc_T, 1)
                    nc.scalar.activation(kcT[:, :, 0:N_CMP],
                                         ps[:, 7, 0:32].rearrange("p (g n) -> p g n", g=2)[:, :, 0:N_CMP],
                                         ACT.Copy).then_inc(kcT_ready, 1)
                if m in SC_STEP:
                    i = SC_STEP.index(m)
                    act.wait_ge(cs_step, 7 * i + 3)
                    nc.scalar.activation(pc[:, i, :, :], pc[:, i, :, :], ACT.Exp).then_inc(cs_exp, 1)
                if m in PCT_STEP:
                    i = PCT_STEP.index(m)
                    act.wait_ge(pc_T, i + 1)
                    for b in range(2):
                        nc.scalar.activation(pcT[:, 4 * b:4 * b + 4, :].rearrange("p h q -> p (h q)"),
                                             ps[0:N_CMP, 6 + b, :], ACT.Copy).then_inc(pcT_ready, 1)
                if m >= 9 and m % 8 == 1:
                    g = m // 8 - 1
                    group_out(act, g, obr[:, g // 2, g % 2, :])
                if m in OT_STEP:
                    i = OT_STEP.index(m)
                    act.wait_ge(oT_done, i + 1)
                    nc.scalar.activation(yhi[:, 0:4, i * P:(i + 1) * P],
                                         ps[:, 7, :].rearrange("p (c q) -> p c q", c=4), ACT.Copy).then_inc(oT_hi, 1)
            split_hi(act, OUT1 + 2)
            act.wait_ge(ln_dev, 1)
            nc.scalar.activation(dsq[:, :, :], zc[:, :, :], ACT.Square).then_inc(ln_sq, 1)
            act.wait_ge(ln_mm, 2)
            nc.scalar.activation(rstd[:, :], ps[:, 5, 0:T], ACT.Sqrt, bias=eps[:, 0:1]).then_inc(ln_root, 1)
            split_hi(act, OUT1 + 3)
            act.wait_ge(ln_norm, 1)
            for c in range(CC):
                nc.scalar.activation(dsq[:, c, :], zc[:, c, :], ACT.Silu, scale=vec[:, V_LNG + c:V_LNG + c + 1],
                                     bias=vec[:, V_LNB + c:V_LNB + c + 1]).then_inc(z_silu, 1)
            act.wait_ge(z_silu, CC)
            nc.scalar.activation(yhi[:, 4:8, :], dsq[:, :, :], ACT.Copy).then_inc(z_hi, 1)
            split_hi(act, OUT1 + 4)
            split_hi(act, OUT1 + 5)

        def mix1_dve(dve):
            dve.wait_ge(bias_written, 16)
            dve.wait_ge(g_hi, 1)
            nc.vector.tensor_tensor(gwlo[:, :, :], gwr[:, :, :], gwhi[:, :, :].bitcast(F32),
                                    ALU.subtract).then_inc(g_lo, 1)
            dve.wait_ge(zpad_set, 1)
            dve.wait_ge(half_set, 1)

            def conf_z(pair):
                dve.wait_ge(th_ready, pair + 1)
                dve.wait_ge(tile_used, CONF[pair][1] + 1)
                for f in range(2):
                    nc.vector.scalar_tensor_tensor(zp[:, 2 * pair + f, CONF_K - 1:], th[:, pair, f, :], 1.0,
                                                   ps[:, 1, f * T:(f + 1) * T], ALU.add, ALU.mult)\
                        .then_inc(z_ready, 1)

            conv_at, conf_pair1 = [0], [False]

            def conf_taps(count):
                for _ in range(count):
                    s = conv_at[0]
                    if s == CONF_K * CC or (s == CONF_K * CC // 2 and not conf_pair1[0]):
                        return
                    conv_at[0] += 1
                    pair, k, f = s // (2 * CONF_K), s % (2 * CONF_K) // 2, s % 2
                    c = 2 * pair + f
                    src, w = zp[:, c, k:k + T], dwv[:, k, c:c + 1]
                    if k == 0:
                        dve.wait_ge(z_ready, c + 1)
                        nc.vector.tensor_scalar(zc[:, c, :], src, w, vec[:, V_DWB + c:V_DWB + c + 1], ALU.mult,
                                                ALU.add).then_inc(conf_step, 1)
                    else:
                        dve.wait_ge(conf_step, s - 1)
                        nc.vector.scalar_tensor_tensor(zc[:, c, :], src, w, zc[:, c, :], ALU.mult,
                                                       ALU.add).then_inc(conf_step, 1)

            def bc(ap, n, axis):
                return ap.unsqueeze(axis).broadcast_to([*ap.shape[:axis], n, *ap.shape[axis:]])

            def rope_norm(i):
                dve.wait_ge(u_squared, 3 * (i + 1))
                nc.vector.tensor_reduce(u_ss[:, 0, i, :], usq[:, :, :], AX.X, ALU.add).then_inc(u_summed, 1)
                conf_taps(4)
                dve.wait_ge(u_root, i + 1)
                inv = u_inv[:, i, :]
                nc.vector.tensor_tensor(hb[:, i, 0:8, :], uq[:, i, :, :], bc(inv[:, 0:8], HD, 2),
                                        ALU.mult).then_inc(u_normed, 1)
                for b in range(2):
                    for g in range(2):
                        at = 8 + 4 * b + 2 * g
                        nc.vector.tensor_scalar(hb[:, i, at:at + 2, :], bc(uk[:, i, 2 + 2 * b, g, :], 2, 1),
                                                inv[:, 8 + 2 * b + g:9 + 2 * b + g], None, ALU.mult)\
                            .then_inc(u_normed, 1)
                dve.wait_ge(u_normed, 6 * i + 5)
                nc.vector.tensor_tensor(hb[:, i, 0:16, :], hb[:, i, 0:16, :], gains[:, :, :],
                                        ALU.mult).then_inc(u_normed, 1)
                conf_taps(4)
                dve.wait_ge(u_normed, 6 * i + 6)
                dve.wait_ge(kv_copied, 2 * (i + 1))
                if i:
                    dve.wait_ge(rope_p, 3)
                x1, x2 = hb[:, i, 0:20, 0:32], hb[:, i, 0:20, 32:64]
                nc.vector.tensor_tensor(rt[:, 0], x1, bc(cosn[:, i, :], 20, 1), ALU.mult).then_inc(rope_v, 1)
                nc.vector.tensor_tensor(rt[:, 1], x2, bc(sinn[:, i, :], 20, 1), ALU.mult).then_inc(rope_v, 1)
                dve.wait_ge(rope_v, 3 * i + 2)
                dve.wait_ge(rope_p, 3 * i + 2)
                nc.vector.tensor_tensor(x1, rt[:, 0], rt[:, 1], ALU.subtract).then_inc(rope_v, 1)

            for t in range(9):
                split_lo(dve, N_MIX1 + t + 2)
                if t == 1:
                    conf_z(0)
                if t >= 1:
                    conf_taps((0, 3, 7, 7, 7, 7, 7, 5, 5)[t])
                if t == 7:
                    rope_norm(0)
                    rope_norm(1)
            conf_z(1)
            conf_pair1[0] = True
            for kv in range(2):
                dve.wait_ge(tok_ready, 4 * kv + 4)
                dve.wait_ge(u_copied, 6)
                src = tok2[:, kv, :, :]
                view = bass.AP(tensor=src.tensor, offset=src.offset,
                               ap=[list(src.ap[0]), [2, 16], [T, 2], [16, N_CMP]])
                pos = bc(bc(vec[:, V_POS + 16 * kv:V_POS + 16 * kv + 16], 2, 2), N_CMP, 3)
                nc.vector.tensor_tensor(flat[:, kv, :, :].rearrange("p j (g n) -> p j g n", g=2), view, pos,
                                        ALU.add).then_inc(flat_ready, 1)
            for kv in range(2):
                dve.wait_ge(flat_hi, kv + 1)
                nc.vector.tensor_tensor(flat_part(ylo, kv), flat[:, kv, :, :], flat_part(yhi, kv).bitcast(F32),
                                        ALU.subtract).then_inc(flat_lo, 1)

            def finish(i):
                dve.wait_ge(o_copied, 2 * i + 2)
                dve.wait_ge(p_ready, 16 * i + 16)
                nc.vector.reciprocal(rsum[:, 2 * i:2 * i + 2, :], psum_[:, 2 * i:2 * i + 2, :]).then_inc(fin_w, 1)
                dve.wait_ge(fin_w, 4 * i + 1)
                dve.wait_ge(gate_ready, 1)
                g3 = gate3[:, i, :].rearrange("p (h b) -> p b h", b=3)
                dve.wait_ge(cs_step, 7 * i + 7)
                nc.vector.tensor_tensor(wgt[:, i, 0, :], g3[:, 0, :], cst[:, i, 2, :], ALU.mult).then_inc(fin_w, 1)
                for b in range(2):
                    nc.vector.tensor_tensor(wgt[:, i, 1 + b, :], g3[:, 1 + b, :], rsum[:, 2 * i + b, :],
                                            ALU.mult).then_inc(fin_w, 1)
                dve.wait_ge(fin_w, 4 * i + 4)
                dve.wait_ge(oc_done, i + 1)

                def heads(ap):
                    return ap.rearrange("p (h d) -> p h d", h=8)
                nc.vector.tensor_tensor(heads(oacc[:, i, :]), heads(ps[:, 6, :]), bc(wgt[:, i, 0, :], HD, 2),
                                        ALU.mult).then_inc(fin_v, 1)
                for b in range(2):
                    nc.vector.tensor_tensor(heads(ot[:, b, :]), heads(obr[:, i, b, :]), bc(wgt[:, i, 1 + b, :], HD, 2),
                                            ALU.mult).then_inc(fin_v, 1)
                    dve.wait_ge(fin_v, 4 * i + 2 + 2 * b)
                    add = nc.vector.tensor_tensor(oacc[:, i, :], oacc[:, i, :], ot[:, b, :], ALU.add)
                    add.then_inc(fin_v if b == 0 else oacc_ready, 1)
                    if b == 0:
                        dve.wait_ge(fin_v, 4 * i + 3)

            for m in range(-2, 35):
                if m in CMP_STEP:
                    split_lo(dve, CMP + CMP_STEP.index(m) + 2)
                dve_step(dve, jobs1, 0, m)
                if m == W2_STEP[0] + 2:
                    dve.wait_ge(kc_step, 1)
                    nc.vector.tensor_reduce(kc_ss[:, 0, :], kcn[:, 1, :, 0, :], AX.X, ALU.add).then_inc(kc_summed, 1)
                if m in SC_STEP:
                    i = SC_STEP.index(m)
                    s, c = pc[:, i, :, :], cst[:, i]
                    dve.wait_ge(cs_ready, i + 1)
                    nc.vector.tensor_tensor(s.rearrange("p (q b) n -> p b q n", b=2),
                                            ps[:, 6:8, 0:4 * N_CMP].rearrange("p b (q n) -> p b q n", q=4),
                                            bc(bc(unseen[:, i, :], 4, 1), 2, 1), ALU.add).then_inc(cs_step, 1)
                    dve.wait_ge(cs_step, 7 * i + 1)
                    nc.vector.tensor_reduce(c[:, 0, :], s, AX.X, ALU.max).then_inc(cs_step, 1)
                    dve.wait_ge(cs_step, 7 * i + 2)
                    nc.vector.tensor_tensor(s, s, bc(c[:, 0, :], N_CMP, 2), ALU.subtract).then_inc(cs_step, 1)
                    conf_taps(2)
                    dve.wait_ge(cs_exp, i + 1)
                    nc.vector.tensor_tensor(s, s, bc(seen[:, i, :], 8, 1), ALU.mult).then_inc(cs_step, 1)
                    dve.wait_ge(cs_step, 7 * i + 4)
                    nc.vector.tensor_reduce(c[:, 1, :], s, AX.X, ALU.add).then_inc(cs_step, 1)
                    dve.wait_ge(cs_step, 7 * i + 5)
                    nc.vector.tensor_scalar(c[:, 1, :], c[:, 1, :], TINY, None, ALU.max).then_inc(cs_step, 1)
                    dve.wait_ge(cs_step, 7 * i + 6)
                    nc.vector.reciprocal(c[:, 2, :], c[:, 1, :]).then_inc(cs_step, 1)
                if m in FIN_STEP:
                    finish(FIN_STEP.index(m))
                if m in OT_STEP:
                    i = OT_STEP.index(m)
                    dve.wait_ge(oT_hi, i + 1)
                    nc.vector.tensor_tensor(ylo[:, 0:4, i * P:(i + 1) * P],
                                            ps[:, 7, :].rearrange("p (c q) -> p c q", c=4),
                                            yhi[:, 0:4, i * P:(i + 1) * P].bitcast(F32),
                                            ALU.subtract).then_inc(oT_lo, 1)
                conf_taps(2)
            conf_taps(CONF_K * CC)
            split_lo(dve, OUT1 + 2)
            dve.wait_ge(ln_mm, 1)
            nc.vector.tensor_tensor(zc[:, :, :], zc[:, :, :], bc(ps[:, 6, 0:T], CC, 1), ALU.subtract)\
                .then_inc(ln_dev, 1)
            split_lo(dve, OUT1 + 3)
            dve.wait_ge(ln_root, 1)
            nc.vector.reciprocal(rstd[:, :], rstd[:, :]).then_inc(ln_inv, 1)
            dve.wait_ge(ln_inv, 1)
            nc.vector.tensor_tensor(zc[:, :, :], zc[:, :, :], bc(rstd[:, :], CC, 1), ALU.mult).then_inc(ln_norm, 1)
            dve.wait_ge(z_hi, 1)
            nc.vector.tensor_tensor(ylo[:, 4:8, :], dsq[:, :, :], yhi[:, 4:8, :].bitcast(F32),
                                    ALU.subtract).then_inc(z_lo, 1)
            split_lo(dve, OUT1 + 4)
            split_lo(dve, OUT1 + 5)
            dve.wait_ge(tile_used, N_FFN1)
            add_x()

        def mix1_pool(pool):
            pool.wait_ge(x_added, 8)
            pool.wait_ge(bias_written, 16)
            nc.gpsimd.memset(zp[:, :, 0:CONF_K - 1], 0.0).then_inc(zpad_set, 1)

            def bc(ap, n, axis):
                return ap.unsqueeze(axis).broadcast_to([*ap.shape[:axis], n, *ap.shape[axis:]])

            def squares_q(i):
                pool.wait_ge(u_copied, i + 1)
                if i:
                    pool.wait_ge(u_summed, 1)
                nc.gpsimd.tensor_tensor(usq[:, 0:8, :], uq[:, i], uq[:, i], ALU.mult).then_inc(u_squared, 1)

            def squares_k(i):
                pool.wait_ge(u_copied, 5 + i)
                for b in range(2):
                    k = uk[:, i, 2 + 2 * b, :, :]
                    nc.gpsimd.tensor_tensor(usq[:, 8 + 2 * b:10 + 2 * b, :], k, k, ALU.mult).then_inc(u_squared, 1)

            def copies(i):
                for b in range(2):
                    nc.gpsimd.tensor_copy(hb[:, i, 16 + 4 * b:20 + 4 * b, :].rearrange("p (g c) d -> p g c d", g=2),
                                          bc(uk[:, i, b, :, :], 2, 2)).then_inc(kv_copied, 1)

            def roots(i):
                pool.wait_ge(u_summed, i + 1)
                nc.gpsimd.tensor_scalar(u_ss[:, 1, i, :], u_ss[:, 0, i, :], 1.0 / HD, EPS, ALU.mult, ALU.add)\
                    .then_inc(u_mean, 1)
                pool.wait_ge(u_mean, i + 1)
                nc.gpsimd.tensor_tensor(u_inv[:, i, :], u_ss[:, 1, i, :], nhalf[:, 0:12], ALU.pow).then_inc(u_root, 1)

            def rope(i):
                pool.wait_ge(u_normed, 6 * i + 6)
                pool.wait_ge(kv_copied, 2 * i + 2)
                x1, x2 = hb[:, i, 0:20, 0:32], hb[:, i, 0:20, 32:64]
                nc.gpsimd.tensor_tensor(rt[:, 2], x2, bc(cosn[:, i, :], 20, 1), ALU.mult).then_inc(rope_p, 1)
                nc.gpsimd.tensor_tensor(rt[:, 3], x1, bc(sinn[:, i, :], 20, 1), ALU.mult).then_inc(rope_p, 1)
                pool.wait_ge(rope_p, 3 * i + 2)
                pool.wait_ge(rope_v, 3 * i + 2)
                nc.gpsimd.tensor_tensor(x2, rt[:, 2], rt[:, 3], ALU.add).then_inc(rope_p, 1)

            squares_q(0)
            squares_k(0)
            copies(0)
            copies(1)
            roots(0)
            squares_q(1)
            squares_k(1)
            rope(0)
            roots(1)
            rope(1)
            pool.wait_ge(gate_tanh, 2)
            nc.gpsimd.tensor_scalar(gate3[:, :, :], gth[:, :, :], 0.5, 0.5, ALU.mult, ALU.add).then_inc(gate_ready, 1)

            def gelu(kv):
                h = hid[:, 0]
                pool.wait_ge(hid_copied, 2 * kv + 2)
                nc.gpsimd.tensor_tensor(hid[:, 1], h, h, ALU.mult).then_inc(gelu_step, 1)
                pool.wait_ge(gelu_step, 5 * kv + 1)
                nc.gpsimd.tensor_scalar(hid[:, 2], hid[:, 1], 0.044715, 1.0, ALU.mult, ALU.add).then_inc(gelu_step, 1)
                pool.wait_ge(gelu_step, 5 * kv + 2)
                nc.gpsimd.tensor_tensor(hid[:, 3], hid[:, 2], h, ALU.mult).then_inc(gelu_step, 1)
                pool.wait_ge(gelu_tanh, kv + 1)
                nc.gpsimd.tensor_scalar(hid[:, 4], hid[:, 3], 1.0, 0.5, ALU.add, ALU.mult).then_inc(gelu_step, 1)
                pool.wait_ge(gelu_step, 5 * kv + 4)
                nc.gpsimd.tensor_tensor(hid2[:, kv], hid[:, 4], h, ALU.mult).then_inc(gelu_step, 1)

            gelu(0)
            pool.wait_ge(kc_copied, 1)
            raw_kc = kcn[:, 0, :, 0, :]
            nc.gpsimd.tensor_tensor(kcn[:, 1, :, 0, :], raw_kc, raw_kc, ALU.mult).then_inc(kc_step, 1)
            nc.gpsimd.tensor_tensor(kcn[:, 2, :, 0, :], raw_kc, bc(g2[:, :], 2, 1), ALU.mult).then_inc(kc_step, 1)
            pool.wait_ge(kc_summed, 1)
            nc.gpsimd.tensor_scalar(kc_ss[:, 1, :], kc_ss[:, 0, :], 1.0 / HD, EPS, ALU.mult, ALU.add)\
                .then_inc(kc_step, 1)
            pool.wait_ge(kc_step, 3)
            nc.gpsimd.tensor_tensor(kc_ss[:, 2, :], kc_ss[:, 1, :], nhalf[0:N_CMP, 0:2], ALU.pow).then_inc(kc_step, 1)
            pool.wait_ge(kc_step, 4)
            nc.gpsimd.tensor_tensor(kcn[:, 3, :, :, :], bc(kcn[:, 2, :, 0, :], 2, 2),
                                    bc(bc(kc_ss[:, 2, :], 2, 2), HD, 3), ALU.mult).then_inc(kc_step, 1)
            gelu(1)

        W2 = a["w_in_2"][0].rearrange("(k p) n -> p k n", p=P)
        Q_COL = (0, 2048, 2560, 3072, 7168)
        K_COL = (512, 3584, 4096, 4608, 7680)
        V_COL = (1024, 5120, 5632, 6144)
        SG_COL = (1536, 6656, 7936)
        MG_COL = 8448
        G_ROW = ((0, 1), (2, 3), (2, 3), (2, 3), (4, 5))
        JOB0 = len(jobs1)
        units = []
        for u in range(5):
            jobs = []
            for hh in range(2):
                for i in range(NT):
                    for h in range(4 * hh, 4 * hh + 4):
                        half = slice((h % 2) * HD, (h % 2) * HD + HD)
                        kvh = h if u < 4 else h // 4
                        jobs.append((q2T[half, u % 2, h // 2, i * P:(i + 1) * P],
                                     k2T[half, u % 2, h // 2 if u < 4 else h // 4, 0:(i + 1) * P],
                                     bt[:, hh, h % 4, (1 - i) * P:T],
                                     [vb[:, u % 2, j, kvh * HD:(kvh + 1) * HD] for j in range(i + 1)],
                                     2 * u + hh))
            units.append(jobs)

        def token_tiles(c0):
            return [W2[:, 0:4, c0:c0 + 512], W2[:, 4:8, c0:c0 + 512]]

        def merge_items(b):
            out = []
            for j in range(2):
                for f in range(2):
                    c0 = MG_COL + D * b + 512 * j + 256 * f
                    out.append(("G", b, 2 * j + f, [W2[:, :, c0:c0 + 256]]))
                out.append(("R", b, j, [a["w_branch_2"][0, b].rearrange("(k p) n -> p k n", p=P)
                                        [:, :, 512 * j:512 * j + 512]]))
            return out

        def unit_items(u):
            if u == 4:
                return [("q", 4, 0, token_tiles(Q_COL[4])), ("kv", 4, 0, [W2[:, :, K_COL[4]:K_COL[4] + 256]])]
            return [("q", u, 0, token_tiles(Q_COL[u])), ("k", u, 0, token_tiles(K_COL[u])),
                    ("v", u, 0, token_tiles(V_COL[u]))]

        segments = [
            (unit_items(0) + [("s", 0, 0, token_tiles(SG_COL[0]))], None),
            (unit_items(1), 0),
            (unit_items(2), 1),
            (unit_items(3) + [("s", 1, 1, token_tiles(SG_COL[1]))], 2),
            (unit_items(4) + [("s", 2, 0, token_tiles(SG_COL[2]))] + merge_items(0), 3),
            (merge_items(1), 4),
            (merge_items(2), None),
        ]
        order, b2_tiles, uses, n_qk, n_T = [], [], 0, 0, 0

        def place_later(pending, entries, after):
            pending.append([after, entries])

        pending = []
        for items, u in segments:
            body = []
            for kind, who, j, srcs in items:
                use0 = uses
                uses += {"G": 1}.get(kind, 2)
                item = (kind, who, j, use0, N_B2 + len(b2_tiles), len(srcs))
                for t, src in enumerate(srcs):
                    n = N_B2 + len(b2_tiles)
                    b2_tiles.append(src)
                    for part in range(2):
                        body.append(("weights", item, n, t, part))
                        for p in pending:
                            p[0] -= 1
                        if not (part == 1 and t == len(srcs) - 1):
                            for p in [p for p in pending if p[0] <= 0 and p[1][0][0] != "turn"]:
                                body += p[1]
                                pending.remove(p)
                body.append(("empty", item))
                for p in [p for p in pending if p[0] <= 0]:
                    if p[1][0][0] == "turn":
                        p[1] = [(*p[1][0][:2], uses, n_T)]
                        n_turned = 1 if p[1][0][1][0] == "kv" else 2
                        uses += n_turned
                        n_T += n_turned
                    body += p[1]
                    pending.remove(p)
                if kind in ("q", "k", "kv"):
                    place_later(pending, [("sums", item, n_qk)], 1)
                    place_later(pending, [("turn", item)], 3)
                    n_qk += 1
                if kind == "s":
                    place_later(pending, [("gate", item)], 1)
                if kind == "R":
                    place_later(pending, [("merge", item)], 1)
            if u is not None:
                steps = []
                for m in range(-2, 17):
                    steps.append(("job", u, m))
                    if m in (8, 16):
                        steps.append(("group", u, m // 8 - 1))
                spots = [k for k, e in enumerate(body) if e[0] == "weights"]
                start = JOB_START[u]
                mixed, done = [], 0
                for k, e in enumerate(body):
                    mixed.append(e)
                    if e[0] == "weights":
                        at = spots.index(k) + 1 - start
                        want = max(0, at) * len(steps) // (len(spots) - start - JOB_TAIL[u])
                        mixed += steps[done:max(done, want)]
                        done = max(done, min(want, len(steps)))
                mixed += steps[done:]
                body = mixed
            order += body
            if u in (0, 3, 4):
                for p in [p for p in pending if p[1][0][0] == "merge"]:
                    order += p[1]
                    pending.remove(p)
                order.append(("finish", {0: 0, 3: 1, 4: 2}[u]))
                b = {0: 0, 3: 1, 4: 2}[u]
                order.append(("branch", b, uses))
                uses += 2
        for p in pending:
            order += p[1]
        assert len(b2_tiles) == 51
        N_OUT2 = N_B2 + len(b2_tiles)
        b2_tiles += [a["w_out_2"][0].rearrange("(k p) n -> p k n", p=P)[:, 2 * r:2 * r + 2, :] for r in range(4)]

        def bank(use):
            return 5 + use % 3

        def wait_use(pe, use):
            if use >= 3:
                pe.wait_ge(emptied, use - 2)

        def blk2_pe(pe):
            pe.wait_ge(x_added, 16)
            norm_pe(pe, 4)
            br_uses = {}
            for e in order:
                if e[0] == "weights":
                    _, (kind, who, j, use0, n0, count), n, t, part = e
                    if part == 0:
                        pe.wait_ge(lo_ready, n + 1)
                    if kind in "qkvs" or kind == "kv":
                        kc = KC if kind == "kv" else 4
                        if t == 0:
                            wait_use(pe, use0 + part)
                        hi, lo = w_parts(n, kc)
                        tok = slice(part * P, part * P + P)
                        for k in range(kc):
                            mm = product(ps[:, bank(use0 + part), 0:TILE // kc], hhi[:, 4 * t + k, tok],
                                         hlo[:, 4 * t + k, tok], hi[:, k, :], lo[:, k, :],
                                         t == 0 and k == 0, t == count - 1 and k == kc - 1)
                    elif kind == "G":
                        if part == 0:
                            wait_use(pe, use0)
                        hi, lo = w_parts(n, KC)
                        c = slice(part * P, part * P + P)
                        for k in range(KC):
                            mm = product(ps[:, bank(use0), part * T:(part + 1) * T], hi[:, k, c], lo[:, k, c],
                                         hhi[:, k, :], hlo[:, k, :], k == 0, k == KC - 1)
                    else:
                        if part == 0:
                            pe.wait_ge(br_lo, who + 1)
                        wait_use(pe, use0 + part)
                        hi, lo = w_parts(n, 4)
                        for f in range(2):
                            c = slice((2 * part + f) * P, (2 * part + f + 1) * P)
                            for k in range(4):
                                mm = product(ps[:, bank(use0 + part), f * T:(f + 1) * T], hi[:, k, c], lo[:, k, c],
                                             yhi[:, k, :], ylo[:, k, :], k == 0, k == 3)
                    if part == 1:
                        mm.then_inc(tile_used, 1)
                elif e[0] == "job":
                    _, u, m = e
                    if m == -2:
                        pe.wait_ge(emptied, turned_use(u))
                        if u == 0:
                            pe.wait_ge(h_lo, 5 * KC)
                    pe_step(pe, units[u], JOB0 + 16 * u, m)
                elif e[0] == "turn":
                    _, item, use, nt = e
                    raw_, width = (qraw, 4) if item[0] == "q" else (kraw, 4 if item[0] == "k" else 2)
                    pe.wait_ge(b_scaled, qk_index(item) * 2 + 2)
                    for b in range(width // 2):
                        wait_use(pe, use + b)
                        for c in range(2):
                            for i in range(NT):
                                mm = nc.tensor.transpose(
                                    ps[:, bank(use + b), c * T + i * P:c * T + (i + 1) * P],
                                    raw_[:, i, (2 * b + c) * P:(2 * b + c + 1) * P], ident[:, :])
                        mm.then_inc(b_T, 1)
                elif e[0] == "branch":
                    _, b, use = e
                    pe.wait_ge(o_gated, 2 * b + 2)
                    for f in range(2):
                        wait_use(pe, use + f)
                        for c in range(2):
                            for i in range(NT):
                                mm = nc.tensor.transpose(
                                    ps[:, bank(use + f), c * T + i * P:c * T + (i + 1) * P],
                                    ob[:, BR_OB[b], i, (2 * f + c) * P:(2 * f + c + 1) * P], ident[:, :])
                        mm.then_inc(b_T, 1)
            for r in range(4):
                pe.wait_ge(lo_ready, N_OUT2 + r + 1)
                pe.wait_ge(m_lo, 2 * r + 2)
                mm_rows(N_OUT2 + r, hhi, hlo, 2 * r, r == 0, r == 3).then_inc(tile_used, 1)

        BR_OB = (0, 1, 0)

        def qk_index(item):
            return next(e[2] for e in order if e[0] == "sums" and e[1] == item)

        def turned_use(u):
            last = 0
            for e in order:
                if e[0] == "turn" and e[1][1] == u:
                    last = max(last, e[2] + (1 if e[1][0] == "kv" else 2))
                if e[0] == "empty" and e[1][1] == u and e[1][0] in ("v", "kv"):
                    last = max(last, e[1][3] + 2)
            return last

        T_COUNT, at = {}, 0
        for e in order:
            if e[0] == "turn":
                T_COUNT[e[2]] = at
                at += 1 if e[1][0] == "kv" else 2
            if e[0] == "branch":
                T_COUNT[e[2]] = at
                at += 2

        LAST_Q_T = max(T_COUNT[e[2]] + 2 for e in order if e[0] == "turn" and e[1][0] == "q")

        def bias_load(act, u, hh):
            head0 = 8 * u + 4 * hh
            src = bass.AP(tensor=bias_dram.tensor, offset=bias_dram.offset + head0 * P * DREL + P - 1,
                          ap=[[DREL - 1, P], [P * DREL, 4], [1, T]])
            if u:
                act.wait_ge(s_shifted, JOB0 + 16 * (u - 1) + 8 * hh + 8)
            else:
                act.wait_ge(bias_written, 16)
            act.dma_start(bt[:, hh, :, :], src).then_inc(bt_landed[hh], 16)

        def blk2_act(act):
            act.wait_ge(h_lo, 5 * KC)
            act.dma_start(nsink[:, 0, :], a["sinks_2"][0].partition_broadcast(P)).then_inc(sink_landed, 16)
            bias_load(act, 0, 0)
            bias_load(act, 0, 1)
            for e in order:
                if e[0] == "weights" and e[4] == 0:
                    split_hi(act, e[2] + 2)
                elif e[0] == "empty":
                    kind, who, j, use0, n0, count = e[1]
                    act.wait_ge(tile_used, n0 + count)
                    if kind in ("q", "k"):
                        dst = qraw if kind == "q" else kraw
                        if qk_index(e[1]) >= 2:
                            act.wait_ge(b_T, before_T(e[1]))
                        for i in range(NT):
                            nc.scalar.activation(dst[:, i, :], ps[:, bank(use0 + i), :], ACT.Copy).then_inc(emptied, 1)
                    elif kind == "kv":
                        act.wait_ge(b_T, before_T(e[1]))
                        act.wait_ge(pv_done, JOB0 + 16 * 3)
                        for i in range(NT):
                            nc.scalar.activation(vb[:, 0, i, 0:2 * HD], ps[:, bank(use0 + i), 2 * HD:4 * HD],
                                                 ACT.Copy).then_inc(b_gated, 1)
                            src = ps[:, bank(use0 + i), 0:2 * HD].rearrange("p (g d) -> p g d", g=2)
                            nc.scalar.activation(
                                kraw[:, i, 0:4 * HD].rearrange("p (g c d) -> p g c d", g=2, c=2),
                                src.unsqueeze(2).broadcast_to([P, 2, 2, HD]), ACT.Copy).then_inc(emptied, 1)
                    elif kind == "v":
                        if who >= 2:
                            act.wait_ge(pv_done, JOB0 + 16 * (who - 1))
                        for i in range(NT):
                            nc.scalar.activation(vb[:, who % 2, i, :], ps[:, bank(use0 + i), :],
                                                 ACT.Copy).then_inc(emptied, 1)
                    elif kind == "s":
                        for i in range(NT):
                            nc.scalar.activation(gth2[:, i, :], ps[:, bank(use0 + i), :], ACT.Tanh,
                                                 scale=0.5).then_inc(b_tanh, 1)
                            nc.scalar.activation(gsil[:, j, i, :], ps[:, bank(use0 + i), :],
                                                 ACT.Copy).then_inc(emptied, 1)
                    elif kind == "G":
                        if 2 * who + j // 2 >= 1:
                            act.wait_ge(m_mul, 2 * who + j // 2)
                        elif True:
                            act.wait_ge(b_silu, 6)
                        nc.scalar.activation(gs[:, 2 * (j % 2):2 * (j % 2) + 2, :].rearrange("p f t -> p (f t)"),
                                             ps[:, bank(use0), :], ACT.Tanh, scale=0.5).then_inc(emptied, 1)
                    else:
                        if 2 * who + j >= 1:
                            act.wait_ge(m_mul, 2 * who + j)
                        act.wait_ge(br_lo, who + 1)
                        for f in range(2):
                            nc.scalar.activation(rb[:, 2 * f:2 * f + 2, :].rearrange("p f t -> p (f t)"),
                                                 ps[:, bank(use0 + f), :], ACT.Copy).then_inc(emptied, 1)
                elif e[0] == "turn":
                    _, item, use, nt = e
                    u = item[1]
                    q = item[0] == "q"
                    if u >= 2:
                        act.wait_ge(s_ready, JOB0 + 16 * (u - 1))
                    for b in range(1 if item[0] == "kv" else 2):
                        act.wait_ge(b_T, T_COUNT[use] + b + 1)
                        dst = (q2T if q else k2T)[:, u % 2, 2 * b:2 * b + 2, :].rearrange("p c t -> p (c t)")
                        g = qk8[:, G_ROW[u][0]:G_ROW[u][0] + 1] if q else                             vec[:, V_QK + G_ROW[u][1]:V_QK + G_ROW[u][1] + 1]
                        nc.scalar.activation(dst, ps[:, bank(use + b), :], ACT.Copy, scale=g).then_inc(emptied, 1)
                elif e[0] == "job":
                    _, u, m = e
                    act_step(act, units[u], JOB0 + 16 * u, m)
                    if m in (7, 15) and u < 4:
                        bias_load(act, u + 1, m // 8)
                elif e[0] == "group":
                    _, u, hh = e
                    if u == 4 and hh == 0:
                        act.wait_ge(b_T, T_COUNT[next(x[2] for x in order if x[0] == "branch")] + 2)
                    group_out(act, 4 + 2 * u + hh,
                              ob[:, u % 4, :, hh * 256:hh * 256 + 256],
                              lambda b: b.rearrange("p (i c) -> p i c", i=2))
                elif e[0] == "finish":
                    b = e[1]
                    if b == 1:
                        act.wait_ge(c_step, C_DIFF[1])
                        nc.scalar.activation(comb[:, 2:5], comb[:, 2:5], ACT.Exp).then_inc(c_exp, 1)
                    if b == 2:
                        act.wait_ge(c_step, C_DIFF[2])
                        nc.scalar.activation(comb[:, 1:3], comb[:, 1:3], ACT.Exp).then_inc(c_exp, 1)
                elif e[0] == "branch":
                    _, b, use = e
                    if b:
                        act.wait_ge(m_mul, 2 * b)
                    for f in range(2):
                        act.wait_ge(b_T, T_COUNT[use] + f + 1)
                        nc.scalar.activation(brT[:, 2 * f:2 * f + 2, :].rearrange("p c t -> p (c t)"),
                                             ps[:, bank(use + f), :], ACT.Copy, scale=0.5).then_inc(emptied, 1)
                    act.wait_ge(emptied, use + 2)
                    if b:
                        act.wait_ge(tile_used, R_TILE[b - 1])
                    nc.scalar.activation(yhi[:, 0:4, :], brT[:, :, :], ACT.Copy).then_inc(br_hi, 1)
            for r in range(4):
                act.wait_ge(m_sum, 5 if r < 2 else 6)
                if r == 0:
                    act.wait_ge(tile_used, N_OUT2)
                for k in range(2):
                    nc.scalar.activation(hhi[:, 2 * r + k, :], macc[:, 2 * r + k, :], ACT.Copy,
                                         scale=0.5).then_inc(m_hi, 1)
                split_hi(act, N_OUT2 + r + 2)

        R_TILE = [max(e[2] for e in order if e[0] == "weights" and e[1][0] == "R" and e[1][1] == b) + 1
                  for b in range(3)]
        C_DIFF = (0, 5, 13)

        def before_T(item):
            mine = "q" if item[0] == "q" else "k"
            last = 0
            for e in order:
                if e[0] == "empty" and e[1] == item:
                    return last
                if e[0] == "turn" and e[1][0][0] == mine:
                    last = T_COUNT[e[2]] + 2
            return last

        def bc(ap, n, axis):
            return ap.unsqueeze(axis).broadcast_to([*ap.shape[:axis], n, *ap.shape[axis:]])

        def blk2_dve(dve):
            dve.wait_ge(sink_landed, 16)
            nc.vector.tensor_scalar(nsink[:, 1, :], nsink[:, 0, :], -1.0, None, ALU.mult).then_inc(c_step, 1)
            merges = 0
            for e in order:
                if e[0] == "weights" and e[4] == 0:
                    split_lo(dve, e[2] + 2)
                elif e[0] == "sums":
                    _, item, nq = e
                    q = item[0] == "q"
                    heads = 4 if item[0] == "kv" else 8
                    sq = (q2T if q else k2T)[:, item[1] % 2].rearrange("p c t -> p (c t)")
                    dve.wait_ge(b_squared, 2 * nq + 2)
                    for i in range(NT):
                        nc.vector.tensor_reduce(
                            b_ss[:, nq % 2, 0, i, 0:heads],
                            sq[:, i * 512:i * 512 + heads * HD].rearrange("p (h d) -> p h d", h=heads),
                            AX.X, ALU.add).then_inc(b_summed, 1)
                elif e[0] == "gate":
                    kind, who, j, use0, n0, count = e[1]
                    for i in range(NT):
                        dve.wait_ge(emptied, use0 + i + 1)
                        nc.vector.scalar_tensor_tensor(gsil[:, j, i, :], gth2[:, i, :], 1.0, gsil[:, j, i, :],
                                                       ALU.add, ALU.mult).then_inc(b_silu, 1)
                elif e[0] == "merge":
                    kind, who, j, use0, n0, count = e[1]
                    dve.wait_ge(emptied, use0 + 2)
                    if who == 0:
                        nc.vector.scalar_tensor_tensor(macc[:, 4 * j:4 * j + 4, :], gs[:, :, :], 1.0, rb[:, :, :],
                                                       ALU.add, ALU.mult).then_inc(m_mul, 1)
                        nc.vector.engine_nop().then_inc(m_sum, 1)
                    else:
                        dve.wait_ge(m_mul, 2 * who + j)
                        dve.wait_ge(m_sum, 2 * who + j)
                        if (who, j) == (1, 0):
                            dve.wait_ge(b_T, LAST_Q_T)
                        nc.vector.scalar_tensor_tensor(mt[:, :, :], gs[:, :, :], 1.0, rb[:, :, :],
                                                       ALU.add, ALU.mult).then_inc(m_mul, 1)
                        dve.wait_ge(m_mul, 2 * who + j + 1)
                        nc.vector.tensor_tensor(macc[:, 4 * j:4 * j + 4, :], macc[:, 4 * j:4 * j + 4, :],
                                                mt[:, :, :], ALU.add).then_inc(m_sum, 1)
                elif e[0] == "job":
                    _, u, m = e
                    if m + 1 in (0, 8) :
                        dve.wait_ge(bt_landed[(m + 1) // 8], 16 * (u + 1))
                    dve_step(dve, units[u], JOB0 + 16 * u, m)
                elif e[0] == "finish":
                    finish2(dve, e[1])
                elif e[0] == "branch":
                    b = e[1]
                    dve.wait_ge(br_hi, b + 1)
                    nc.vector.tensor_tensor(ylo[:, 0:4, :], brT[:, :, :], yhi[:, 0:4, :].bitcast(F32),
                                            ALU.subtract).then_inc(br_lo, 1)
            for r in range(4):
                for k in range(2):
                    dve.wait_ge(m_hi, 2 * r + k + 1)
                    nc.vector.scalar_tensor_tensor(hlo[:, 2 * r + k, :], macc[:, 2 * r + k, :], 0.5,
                                                   hhi[:, 2 * r + k, :].bitcast(F32), ALU.mult,
                                                   ALU.subtract).then_inc(m_lo, 1)
                split_lo(dve, N_OUT2 + r + 2)
            dve.wait_ge(tile_used, N_OUT2 + 4)
            add_x()

        def finish2(dve, b):
            at = {0: 1, 1: 2, 2: 10}[b]

            def step(ins):
                nonlocal at
                at += 1
                ins.then_inc(c_step, 1)
                dve.wait_ge(c_step, at)
            u0 = (0, 1, 4)[b]
            nm = nmax[:, 2 * u0:2 * u0 + (2, 6, 2)[b], :].rearrange("p (u g) j -> p u g j", g=2)
            sm = psum_[:, 2 * u0:2 * u0 + (2, 6, 2)[b], :].rearrange("p (u g) j -> p u g j", g=2)
            dve.wait_ge(o_copied, 4 + 2 * ((0, 3, 4)[b] + 1))
            if b == 0:
                step(nc.vector.reciprocal(comb[:, 5], sm[:, 0]))
                parts = [(0, comb[:, 5])]
            elif b == 1:
                step(nc.vector.tensor_tensor(comb[:, 0], nm[:, 0], nm[:, 1], ALU.min))
                step(nc.vector.tensor_tensor(comb[:, 0], comb[:, 0], nm[:, 2], ALU.min))
                step(nc.vector.tensor_tensor(comb[:, 2:5], bc(comb[:, 0], 3, 1), nm, ALU.subtract))
                assert at == C_DIFF[1]
                dve.wait_ge(c_exp, 1)
                step(nc.vector.tensor_tensor(comb[:, 5:8], comb[:, 2:5], sm, ALU.mult))
                step(nc.vector.tensor_tensor(comb[:, 5], comb[:, 5], comb[:, 6], ALU.add))
                step(nc.vector.tensor_tensor(comb[:, 5], comb[:, 5], comb[:, 7], ALU.add))
                step(nc.vector.reciprocal(comb[:, 6], comb[:, 5]))
                step(nc.vector.tensor_tensor(comb[:, 2:5], comb[:, 2:5], bc(comb[:, 6], 3, 1), ALU.mult))
                parts = [(u, comb[:, 1 + u]) for u in (1, 2, 3)]
            else:
                def sink(k):
                    return bc(nsink[:, k, :].rearrange("p (g q) -> p g q", g=2), 2, 2)

                def giq(ap):
                    return ap.rearrange("p g (i q) -> p g i q", i=2)
                step(nc.vector.tensor_tensor(giq(comb[:, 0]), giq(nm[:, 0]), sink(1), ALU.min))
                step(nc.vector.tensor_tensor(comb[:, 1], comb[:, 0], nm[:, 0], ALU.subtract))
                step(nc.vector.tensor_tensor(giq(comb[:, 2]), giq(comb[:, 0]), sink(0), ALU.add))
                assert at == C_DIFF[2]
                dve.wait_ge(c_exp, 2)
                step(nc.vector.tensor_tensor(comb[:, 3], comb[:, 1], sm[:, 0], ALU.mult))
                step(nc.vector.tensor_tensor(comb[:, 3], comb[:, 3], comb[:, 2], ALU.add))
                step(nc.vector.reciprocal(comb[:, 4], comb[:, 3]))
                step(nc.vector.tensor_tensor(comb[:, 5], comb[:, 4], comb[:, 1], ALU.mult))
                parts = [(0, comb[:, 5])]
            dve.wait_ge(b_silu, 2 * b + 2)
            for i in range(NT):
                for k, (o, f) in enumerate(parts):
                    v = ob[:, o, i, :].rearrange("p (g q d) -> p g q d", g=2, q=4)
                    fac = bc(f[:, :, 4 * i:4 * i + 4], HD, 3)
                    o_count[0] += 1
                    nc.vector.tensor_tensor(v, v, fac, ALU.mult).then_inc(o_scaled, 1)
                    if k:
                        dve.wait_ge(o_scaled, o_count[0])
                        o_count[0] += 1
                        first = ob[:, parts[0][0], i, :]
                        nc.vector.tensor_tensor(first, first, ob[:, o, i, :], ALU.add).then_inc(o_scaled, 1)
                dve.wait_ge(o_scaled, o_count[0])
                first = ob[:, parts[0][0], i, :]
                nc.vector.tensor_tensor(first, first, gsil[:, (0, 1, 0)[b], i, :], ALU.mult).then_inc(o_gated, 1)

        o_count = [0]

        def blk2_pool(pool):
            for e in order:
                if e[0] != "sums":
                    continue
                _, item, nq = e
                q = item[0] == "q"
                heads = 4 if item[0] == "kv" else 8
                src = qraw if q else kraw
                sq = (q2T if q else k2T)[:, item[1] % 2].rearrange("p c t -> p (c t)")
                if item[1] >= 2:
                    pool.wait_ge(s_ready, JOB0 + 16 * (item[1] - 1))
                for i in range(NT):
                    pool.wait_ge(emptied, item[3] + i + 1)
                    r = src[:, i, 0:heads * HD]
                    nc.gpsimd.tensor_tensor(sq[:, i * 512:i * 512 + heads * HD], r, r, ALU.mult).then_inc(b_squared, 1)
                pool.wait_ge(b_summed, 2 * nq + 2)
                nc.gpsimd.tensor_scalar(b_ss[:, nq % 2, 1, :, 0:heads], b_ss[:, nq % 2, 0, :, 0:heads], 1.0 / HD, EPS,
                                        ALU.mult, ALU.add).then_inc(b_mean, 1)
                pool.wait_ge(b_mean, nq + 1)
                nc.gpsimd.tensor_tensor(b_inv[:, nq % 2, :, 0:heads], b_ss[:, nq % 2, 1, :, 0:heads],
                                        nhalf[:, 0:2 * heads].rearrange("p (i h) -> p i h", i=2),
                                        ALU.pow).then_inc(b_root, 1)
                pool.wait_ge(b_root, nq + 1)
                for i in range(NT):
                    r = src[:, i, 0:heads * HD].rearrange("p (h d) -> p h d", h=heads)
                    nc.gpsimd.tensor_tensor(r, r, bc(b_inv[:, nq % 2, i, 0:heads], HD, 2),
                                            ALU.mult).then_inc(b_scaled, 1)

        block = ctx.enter_context(nc.Block())

        @block.sync
        def _(sp):
            sp.dma_start(x[:, :, :], a["x"][0].rearrange("(i p) d -> p i d", p=P)).then_inc(x_landed, 16)
            for j, src in enumerate(mix0):
                load_tile(sp, N_MIX0 + j, src)
            ffn_sp(sp, 0, N_FFN0)
            for j, src in enumerate(mix1):
                load_tile(sp, N_MIX1 + j, src)
            ffn_sp(sp, 1, N_FFN1)
            for j, src in enumerate(b2_tiles):
                load_tile(sp, N_B2 + j, src)
            sp.wait_ge(x_added, 20)
            sp.dma_start(out[0].rearrange("(i p) d -> p i d", p=P), x[:, :, :]).then_inc(stored, 16)
            sp.wait_ge(stored, 16)

        @block.gpsimd
        def _(pool):
            nc.gpsimd.memset(eps[:, :], EPS).then_inc(eps_set, 1)
            nc.gpsimd.memset(nhalf[:, :], -0.5).then_inc(nhalf_set, 1)
            nc.gpsimd.memset(pool_a[:, :, 0:16], 0.0).then_inc(zero_set, 1)
            nc.gpsimd.memset(cvp[:, :, 0:2], 0.0).then_inc(zero_set, 1)
            nc.gpsimd.memset(onesd[:, :], 1.0 / CW).then_inc(nhalf_set, 1)
            pool.wait_ge(nhalf_set, 2)
            norm_pool(pool, 0)
            pool.wait_ge(bias_rows, 1)
            pool.dma_start(bias_dram, bc(relrow, P, 1)).then_inc(bias_written, 16)
            norm_pool(pool, 1)
            norm_pool(pool, 2)
            mix1_pool(pool)
            norm_pool(pool, 3)
            norm_pool(pool, 4)
            blk2_pool(pool)

        vector_rows = [
            (V_NORM_MIX, a["norm_mix"].rearrange("d (c p) -> (d c) p", p=P)),
            (V_NORM_FFN, a["norm_ffn"].rearrange("d (c p) -> (d c) p", p=P)),
            (V_LN2, a["ln_g_2"].rearrange("d (c p) -> (d c) p", p=P)),
            (V_CONV_A, a["conv_a"][0].rearrange("k (c p) -> (k c) p", p=P)),
            (V_POOL_S, a["pool_scale"].rearrange("d (c p) -> (d c) p", p=P)),
            (V_DWB, a["conf_dw_b"].rearrange("d (c p) -> (d c) p", p=P)),
            (V_LNG, a["conf_ln_g"].rearrange("d (c p) -> (d c) p", p=P)),
            (V_LNB, a["conf_ln_b"].rearrange("d (c p) -> (d c) p", p=P)),
            (V_POS, a["cmp_pos"][0].rearrange("v (j s) d -> (v j) (s d)", s=2)),
        ]
        N_VECTORS = len(vector_rows) + 3

        @block.scalar
        def _(act):
            for r0, src in vector_rows:
                act.dma_start(vrow[r0:r0 + src.shape[0], :], src).then_inc(vec_landed, 16)
            for half in range(2):
                act.dma_start(vrow[V_QK:V_QK + 6, half * HD:half * HD + HD], a["qk_g_2"][0]).then_inc(vec_landed, 16)
            act.dma_start(vrow2[:, :], a["conf_dw"][0].rearrange("k (c p) -> (k c) p", p=P)).then_inc(vec_landed, 16)
            act.dma_start(ident[:, :], a["c_ident"]).then_inc(ident_landed, 16)
            for dst, src in ((relb, a["rel_bias_2"]), (onehot, a["c_onehot"]), (relmask, a["c_relmask"])):
                act.dma_start(dst, src).then_inc(bias_loaded, 16)
            act.dma_start(rcnt[:, :, :], a["c_rcnt"].partition_broadcast(P)).then_inc(consts_landed, 16)
            act.dma_start(pw[:, :, :], a["pool_w"][0].rearrange("g c d -> c g d")).then_inc(pw_landed, 16)

            split_hi(act, 0)
            split_hi(act, 1)
            norm_act(act, 0, V_NORM_MIX)
            act.wait_ge(zero_set, 2)
            for t in range(8):
                split_hi(act, N_MIX0 + t + 2)
                if t < 2:
                    act.wait_ge(tile_used, N_MIX0 + t + 1)
                    nc.scalar.activation(pool_a[:, 2 * t:2 * t + 2, 16:],
                                         ps[:, t, :].rearrange("p (f t) -> p f t", f=2),
                                         ACT.Copy).then_inc(v_copied, 1)
                if t in (2, 5):
                    act.wait_ge(tile_used, N_MIX0 + t + 1)
                    j = t // 3
                    nc.scalar.activation(ctile[:, 2 * j:2 * j + 2, :].rearrange("p f t -> p (f t)"),
                                         ps[:, t, :], ACT.Copy).then_inc(c_copied, 1)
            act.wait_ge(pool_mm, 1)
            for j in range(CC):
                nc.scalar.activation(yhi[:, CC + j, :], ps[:, j // 2, (j % 2) * T:(j % 2 + 1) * T], ACT.Copy,
                                     scale=vec[:, V_POOL_S + j:V_POOL_S + j + 1]).then_inc(y_hi, 1)
            split_hi(act, N_MIX0 + 10)
            for j in range(CC):
                act.wait_ge(yc_ready, j + 1)
                nc.scalar.activation(yhi[:, j, :], yb[:, j, :], ACT.Copy).then_inc(y_hi, 1)
            for t in range(11, 14):
                split_hi(act, N_MIX0 + t)
            norm_act(act, 1, V_NORM_FFN)
            ffn_act(act, 0, N_FFN0)
            norm_act(act, 2, V_NORM_MIX + KC)
            m1_loads(act)
            mix1_act(act)
            norm_act(act, 3, V_NORM_FFN + KC)
            ffn_act(act, 1, N_FFN1)
            norm_act(act, 4, V_LN2)
            blk2_act(act)

        @block.vector
        def _(dve):
            split_lo(dve, 0)
            split_lo(dve, 1)
            dve.wait_ge(vec_T, 2)
            nc.vector.tensor_copy(vec[:, :], ps[:, 0, 0:V_ROWS]).then_inc(vec_ready, 1)
            nc.vector.tensor_copy(dwv[:, :, :].rearrange("p k c -> p (k c)"),
                                  ps[:, 1, 0:CONF_K * CC]).then_inc(vec_ready, 1)
            dve.wait_ge(vec_ready, 2)
            nc.vector.tensor_scalar(dwv[:, :, :], dwv[:, :, :], 0.5, None, ALU.mult).then_inc(half_set, 1)
            nc.vector.tensor_scalar(qk8[:, :], vec[:, V_QK:V_QK + 6], HD ** -0.5, None, ALU.mult).then_inc(half_set, 1)
            dve.wait_ge(bias_T, 1)
            nc.vector.tensor_copy(relT, ps[0:N_BUCKETS, 2, 0:H_TOT]).then_inc(bias_copied, 1)
            dve.wait_ge(bias_mm, 1)
            nc.vector.tensor_tensor(relrow, relmask, ps[0:H_TOT, 3, 0:DREL], ALU.add).then_inc(bias_rows, 1)
            norm_dve(dve, 0, V_NORM_MIX)

            def pooling():
                dve.wait_ge(v_copied, 2)
                nc.vector.tensor_tensor(pool_b[:, :, 1:], pool_a[:, :, 1:], pool_a[:, :, 0:271],
                                        ALU.add).then_inc(pool_step, 1)
                src, dst, lead = pool_b, pool_c, 1
                for g in range(1, 4):
                    w = 2 ** g
                    lead += w
                    dve.wait_ge(pool_step, g)
                    nc.vector.tensor_tensor(dst[:, g:, lead:], src[:, g:, lead:], src[:, g:, lead - w:272 - w],
                                            ALU.add).then_inc(pool_step, 1)
                    src, dst = dst, src
                dve.wait_ge(pool_step, 4)
                dve.wait_ge(consts_landed, 16)
                for b, g in ((pool_b, 0), (pool_c, 1)):
                    nc.vector.tensor_tensor(b[:, g::2, 16:], b[:, g::2, 16:], rcnt[:, g::2, :],
                                            ALU.mult).then_inc(pool_step, 1)
                dve.wait_ge(pool_step, 6)
                for b, g in ((pool_b, 0), (pool_c, 1)):
                    nc.vector.tensor_tensor(b[:, g::2, 16:], b[:, g::2, 16:], pool_a[:, g::2, 16:],
                                            ALU.subtract).then_inc(pool_step, 1)

            def conv3(j):
                t = 2 + 3 * j
                dve.wait_ge(c_copied, j + 1)
                dve.wait_ge(tile_used, N_MIX0 + t + 2)
                dve.wait_ge(zero_set, 2)
                nc.vector.tensor_tensor(cvp[:, 2 * j:2 * j + 2, 2:], ctile[:, 2 * j:2 * j + 2, :],
                                        ps[:, t + 1, :].rearrange("p (f t) -> p f t", f=2),
                                        ALU.mult).then_inc(cv_ready, 1)
                dve.wait_ge(cv_ready, j + 1)
                for k in range(3):
                    for f in range(2):
                        c = 2 * j + f
                        w = vec[:, V_CONV_A + 4 * k + c:V_CONV_A + 4 * k + c + 1]
                        if k == 0:
                            nc.vector.tensor_scalar(yb[:, c, :], cvp[:, c, 0:T], w, None,
                                                    ALU.mult).then_inc(conv_step, 1)
                        else:
                            dve.wait_ge(conv_step, 6 * j + 2 * (k - 1) + f + 1)
                            nc.vector.scalar_tensor_tensor(yb[:, c, :], cvp[:, c, k:k + T], w, yb[:, c, :],
                                                           ALU.mult, ALU.add).then_inc(conv_step, 1)

            def gate(j):
                t = 2 + 3 * j
                dve.wait_ge(tile_used, N_MIX0 + t + 3)
                dve.wait_ge(conv_step, 6 * j + 6)
                for f in range(2):
                    c = 2 * j + f
                    nc.vector.tensor_tensor(yb[:, c, :], yb[:, c, :],
                                            ps[:, t + 2, f * T:(f + 1) * T], ALU.mult).then_inc(yc_ready, 1)

            for t in range(8):
                split_lo(dve, N_MIX0 + t + 2)
                if t == 2:
                    pooling()
                if t == 3:
                    conv3(0)
                if t == 4:
                    gate(0)
                if t == 6:
                    conv3(1)
            for j in range(CC):
                dve.wait_ge(y_hi, j // 2 * 2 + 2)
                nc.vector.scalar_tensor_tensor(ylo[:, CC + j, :], ps[:, j // 2, (j % 2) * T:(j % 2 + 1) * T],
                                               vec[:, V_POOL_S + j:V_POOL_S + j + 1],
                                               yhi[:, CC + j, :].bitcast(F32),
                                               ALU.mult, ALU.subtract).then_inc(y_lo, 1)
            split_lo(dve, N_MIX0 + 10)
            gate(1)
            for j in range(CC):
                dve.wait_ge(y_hi, CC + j + 1)
                nc.vector.tensor_tensor(ylo[:, j, :], yb[:, j, :], yhi[:, j, :].bitcast(F32),
                                        ALU.subtract).then_inc(y_lo, 1)
            for t in range(11, 14):
                split_lo(dve, N_MIX0 + t)
            dve.wait_ge(tile_used, N_FFN0)
            add_x(2)
            norm_dve(dve, 1, V_NORM_FFN)
            ffn_dve(dve, 0, N_FFN0)
            norm_dve(dve, 2, V_NORM_MIX + KC)
            mix1_dve(dve)
            norm_dve(dve, 3, V_NORM_FFN + KC)
            ffn_dve(dve, 1, N_FFN1)
            norm_dve(dve, 4, V_LN2)
            blk2_dve(dve)

        @block.tensor
        def _(pe):
            pe.wait_ge(ident_landed, 16)
            pe.wait_ge(vec_landed, 16 * N_VECTORS)
            nc.tensor.transpose(ps[:, 0, 0:V_ROWS], vrow[:, :], ident[0:V_ROWS, 0:V_ROWS]).then_inc(vec_T, 1)
            n2 = CONF_K * CC
            nc.tensor.transpose(ps[:, 1, 0:n2], vrow2[:, :], ident[0:n2, 0:n2]).then_inc(vec_T, 1)
            pe.wait_ge(bias_loaded, 48)
            nc.tensor.transpose(ps[0:N_BUCKETS, 2, 0:H_TOT], relb, ident[0:H_TOT, 0:H_TOT]).then_inc(bias_T, 1)
            pe.wait_ge(bias_copied, 1)
            nc.tensor.matmul(ps[0:H_TOT, 3, 0:DREL], relT, onehot, start=True, stop=True).then_inc(bias_mm, 1)
            norm_pe(pe, 0)
            pe.wait_ge(vec_ready, 2)
            pe.wait_ge(bias_rows, 1)
            for t in range(8):
                mm_feature(N_MIX0 + t, t)
            pe.wait_ge(pw_landed, 16)
            pe.wait_ge(pool_step, 8)
            for g in range(CC):
                mm = nc.tensor.matmul(ps[:, g // 2, (g % 2) * T:(g % 2 + 1) * T], pw[:, g, :],
                                      (pool_b, pool_c)[g % 2][:, g, 16:], start=True, stop=True)
            mm.then_inc(pool_mm, 1)
            for j in range(4):
                pe.wait_ge(lo_ready, N_MIX0 + 8 + j + 1)
                pe.wait_ge(y_lo, (2 * j + 2) if j < 2 else (8 if j == 3 else 6))
                if j == 0:
                    pe.wait_ge(yc_ready, 2)
                    pe.wait_ge(c_copied, 2)
                mm_rows(N_MIX0 + 8 + j, yhi, ylo, (4, 6, 0, 2)[j], j == 0, j == 3, 2).then_inc(tile_used, 1)
            pe.wait_ge(x_added, 4)
            norm_pe(pe, 1)
            ffn_pe(pe, 0, N_FFN0)
            pe.wait_ge(x_added, 8)
            norm_pe(pe, 2)
            mix1_pe(pe)
            pe.wait_ge(x_added, 12)
            norm_pe(pe, 3)
            ffn_pe(pe, 1, N_FFN1)
            blk2_pe(pe)


_INS = ["x", "norm_mix", "norm_ffn", "ffn_gate", "ffn_up", "ffn_down", "w_in_even", "conv_a", "pool_w",
        "pool_scale", "w_out_even", "w_in_odd", "q_norm", "k_norm", "cmp_pos", "cmp_w1", "cmp_w2", "conf_dw",
        "conf_dw_b", "conf_ln_g", "conf_ln_b", "w_out_odd", "ln_g_2", "w_in_2", "qk_g_2", "sinks_2",
        "w_branch_2", "w_out_2", "rel_bias_2"]


def kernel(**inputs):
    import numpy as _np
    import concourse.bacc as _bacc
    from concourse import mybir as _mybir
    from concourse.bass_utils import run_bass_kernel_spmd as _run

    arrays = {name: _np.ascontiguousarray(inputs[name]) for name in _INS}
    arrays.update(constants())
    nc = _bacc.Bacc("TRN2", target_bir_lowering=False, num_devices=1)
    a = {name: nc.dram_tensor(name, v.shape, _mybir.dt.from_np(v.dtype), kind="ExternalInput").ap()
         for name, v in arrays.items()}
    out = nc.dram_tensor("out", (1, T, D), F32, kind="ExternalOutput").ap()
    build(nc, a, out)
    r = _run(nc, [arrays], core_ids=[0])
    return r.results[0]["out"]
```

```python
from contextlib import ExitStack

import numpy as np
import concourse.bass as bass
from concourse import mybir

F32 = mybir.dt.float32
F32R = mybir.dt.float32r
ALU = mybir.AluOpType
ACT = mybir.ActivationFunctionType
AX = mybir.AxisListType

P = 128
T = 256
NT = T // P
D = 1024
KC = D // P
FF = 2816
HD = 64
EPS = 1e-6
NEG = -1e30
TINY = 1e-30
CW = 512
CC = CW // P
WINDOWS = (2, 4, 8, 16)
CONF_K = 31
N_CMP = (T - 32) // 16 + 1
N_BUCKETS = 32
BIAS_WRITES = 8
H_TOT = 40
DREL = T + P

RAW = 3
SPLIT = 3
TILE = 2048
FFC = 256
FSTEPS = FF // FFC

V_NORM_MIX, V_NORM_FFN, V_LN2, V_CONV_A, V_POOL_S, V_DWB, V_LNG, V_LNB, V_QK, V_POS = (
    0, 16, 32, 40, 52, 56, 60, 64, 68, 74)
V_ROWS = 106


def constants():
    t = np.arange(T)
    inv = (1.0 / (np.float32(10000.0) ** (np.arange(0, HD, 2, dtype=np.float32) / np.float32(HD)))).astype(np.float32)
    ang = t.astype(np.float32)[:, None] * inv[None, :]
    cnt = np.stack([np.minimum(t + 1, w) for w in WINDOWS]).astype(np.float32)
    dist = 255 - np.arange(DREL)
    d0 = np.maximum(dist, 0)
    large = 16 + (np.log(np.maximum(d0, 1).astype(np.float32) / np.float32(16))
                  / np.float32(np.log(2048 / 16)) * 16).astype(np.int32)
    bucket = np.where(d0 < 16, d0, np.minimum(large, N_BUCKETS - 1))
    onehot = (bucket[None, :] == np.arange(N_BUCKETS)[:, None]).astype(np.float32)
    ok = dist >= 0
    rows = [ok] * 8 + [ok & (dist <= 128)] * 8 + [ok & (dist % 4 == 0)] * 8 + [ok & (dist % 16 == 0)] * 8 \
        + [ok & (dist < 128)] * 8
    relmask = np.where(np.stack(rows), 0.0, NEG).astype(np.float32)
    p = np.arange(P)
    causal = np.where(p[:, None] + P - t[None, :] >= 0, 0.0, NEG).astype(np.float32)
    cmp_end = np.arange(N_CMP) * 16 + 31
    seen = (cmp_end[None, :] <= t[:, None]).astype(np.float32)
    return {
        "c_ident": np.eye(P, dtype=np.float32),
        "c_cos": np.cos(ang).astype(np.float32),
        "c_sin": np.sin(ang).astype(np.float32),
        "c_rcnt": (np.float32(1) / cnt).astype(np.float32),
        "c_onehot": onehot,
        "c_relmask": relmask,
        "c_causal": causal,
        "c_seen": seen,
        "c_unseen": np.where(seen > 0, 0.0, NEG).astype(np.float32),
    }


def tile_list(a):
    def feature(w, c0):
        return w.rearrange("(k p) n -> p k n", p=P)[:, :, c0:c0 + 256]

    def token(w, c0, half):
        return w.rearrange("(k p) n -> p k n", p=P)[:, 4 * half:4 * half + 4, c0:c0 + 512]

    def rows(w, r):
        return w.rearrange("(k p) n -> p k n", p=P)[:, 2 * r:2 * r + 2, :]

    w = a["w_in_even"][0]
    mix0 = [feature(w, c) for c in (1536, 1792, 512, 1024, 0, 768, 1280, 256)]
    mix0 += [rows(a["w_out_even"][0], r) for r in (2, 3, 0, 1)]
    w = a["w_in_odd"][0]
    conf = 512 + 6 * 128 + 24
    mix1 = [feature(w, conf + 512), feature(w, conf)]
    mix1 += [token(w, 0, 0), token(w, 0, 1), token(w, 512, 0), token(w, 512, 1), feature(w, 1024)]
    mix1 += [feature(w, conf + 768), feature(w, conf + 256)]
    for kv in range(2):
        c = a["cmp_w1"][0, kv].rearrange("(k p) n -> p k n", p=P)
        mix1 += [c[:, 0:8, :], c[:, 8:16, :]]
    mix1 += [rows(a["w_out_odd"][0], r) for r in (2, 3, 0, 1)]
    return mix0, mix1


SCRATCH = 22800


def build(nc, a, out):
    ctx = ExitStack()
    with ctx:
        def sb(name, shape, dt=F32):
            return ctx.enter_context(nc.sbuf_tensor(name + "_sb", shape, dt))

        def sem(name):
            return ctx.enter_context(nc.semaphore(name))

        raw = sb("raw", [P, RAW, TILE])
        whi = sb("whi", [P, SPLIT, TILE], F32R)
        wlo = sb("wlo", [P, SPLIT, TILE], F32R)
        x = sb("x", [P, NT, D])
        hhi = sb("hhi", [P, KC, T], F32R)
        hlo = sb("hlo", [P, KC, T], F32R)
        yhi = sb("yhi", [P, KC, T], F32R)
        ylo = sb("ylo", [P, KC, T], F32R)
        gwhi = sb("gwhi", [P, KC, 24], F32R)
        gwlo = sb("gwlo", [P, KC, 24], F32R)
        ident = sb("ident", [P, P])
        vec = sb("vec", [P, V_ROWS])
        dwv = sb("dwv", [P, CONF_K, CC])
        qk8 = sb("qk8", [P, 6])
        eps = sb("eps", [P, 1])
        nhalf = sb("nhalf", [P, 24])
        ssum = sb("ssum", [P, NT])
        smean = sb("smean", [P, NT])
        sinv = sb("sinv", [P, NT])
        b_ss = sb("b_ss", [P, 2, 2, NT, 8])
        b_inv = sb("b_inv", [P, 2, NT, 8])
        comb = sb("comb", [P, 8, 2, 8])
        nsink = sb("nsink", [P, 2, 8])
        onesd = sb("onesd", [P, P])
        nmax = sb("nmax", [P, 10, 8])
        psum_ = sb("psum_", [P, 10, 8])
        rsum = sb("rsum", [P, 10, 8])
        ps = ctx.enter_context(nc.psum_tensor("ps", [P, 8, 512], F32))
        scratch = sb("scratch", [P, SCRATCH])

        def carver(start=0):
            at = [start]

            def carve(*shape):
                n = int(np.prod(shape))
                part = scratch[:, at[0]:at[0] + n]
                at[0] += n
                assert at[0] <= SCRATCH, at[0]
                if len(shape) > 1:
                    names = "abcd"[:len(shape)]
                    part = part.rearrange(f"p ({' '.join(names)}) -> p {' '.join(names)}",
                                          **{c: m for c, m in zip(names, shape)})
                return part
            carve.at = at
            return carve

        carve = carver()
        xn = carve(NT, D)
        sg = carve(2, 2, T)
        gu = carve(2, 2, T)
        ghi = yhi[:, 0:4, :].rearrange("p (b f) t -> p b f t", b=2)
        glo = ylo[:, 0:4, :].rearrange("p (b f) t -> p b f t", b=2)
        carve = carver(NT * D)
        pool_a = carve(CC, 272)
        pool_b = carve(CC, 272)
        pool_c = carve(CC, 272)
        ctile = carve(CC, T)
        cvp = carve(CC, T + 2)
        yb = carve(CC, T)
        rcnt = carve(CC, T)
        pw = carve(CC, P)
        vrow = carve(P)[0:V_ROWS, :]
        vrow2 = carve(P)[0:CONF_K * CC, :]
        relb = carve(N_BUCKETS)[0:H_TOT]
        relT = carve(H_TOT)[0:N_BUCKETS]
        onehot = carve(DREL)[0:N_BUCKETS]
        relmask = carve(DREL)[0:H_TOT]
        relrow = carve(DREL)[0:H_TOT]

        carve = carver(NT * D)
        th = carve(2, 2, T)
        dsq = th.rearrange("p a b t -> p (a b) t")
        zp = carve(CC, T + CONF_K - 1)
        zc = carve(CC, T)
        rstd = carve(T)
        uk = carve(NT, 6, 2, HD)
        cosn = carve(NT, HD // 2)
        sinn = carve(NT, HD // 2)
        causal = carve(T)
        qT = carve(CC, T)
        kT = carve(2, 2, T)
        tok2 = carve(2, 2, T)
        flat = carve(2, 16, 2 * N_CMP)
        tapp = th.rearrange("p a b t -> p (a b) t")
        hidt = carve(T)[0:2 * N_CMP]
        hid = carve(5, 2, 2 * N_CMP)
        hid2 = carve(2, 2, 2 * N_CMP)
        cw2 = carve(2, 2, HD)
        kcn = carve(4, 2, 2, HD)[0:N_CMP]
        vcs = carve(2, HD)[0:N_CMP]
        g2 = carve(HD)[0:N_CMP]
        kcT = carve(2, 16)
        seen = carve(NT, N_CMP)
        unseen = carve(NT, N_CMP)
        gwr = carve(KC, 24)
        gth = carve(NT, 24)
        gate3 = carve(NT, 24)
        cst = carve(NT, 4, 8)
        wgt = carve(NT, 3, 8)
        u_ss = carve(2, NT, 12)
        u_inv = carve(NT, 12)
        kc_ss = carve(3, 2)[0:N_CMP]
        early = carver(carve.at[0])
        uq = early(NT, 8, HD)
        usq = early(12, HD)
        rt = early(4, 20, HD // 2)
        gains = early(16, HD)
        hb = early(NT, 24, HD)
        obr = carve(NT, 2, 512)
        oacc = carve(NT, 512)
        ot = carve(2, 512)
        pc = carve(NT, 8, N_CMP)
        pcT = carve(8, P)[0:N_CMP]
        carve = carver()
        qraw = carve(NT, 512)
        kraw = carve(NT, 512)
        vb = carve(2, NT, 512)
        q2T = carve(2, CC, T)
        k2T = carve(2, CC, T)
        bt = carve(2, 4, T)
        ob = carve(4, NT, 512)
        gsil = carve(2, NT, 512)
        gs = carve(4, T)
        rb = carve(4, T)
        macc = carve(KC, T)
        gth2 = gs.rearrange("p (i a) t -> p i (a t)", i=2)
        brT = rb
        mt = scratch[:, 0:CC * T].rearrange("p (c t) -> p c t", c=CC)
        carve = carver(SCRATCH - 8 * T)
        lg = carve(2, T)
        pr = carve(4, T)
        pT = carve(2, 2, P)

        bias_dram = nc.dram_tensor("bias_rows_dram", (H_TOT, P, DREL), F32, kind="Internal").ap()
        JOB_START, JOB_TAIL = (2, 1, 1, 1, 0), (1, 1, 1, 14, 1)

        tile_landed = [sem(f"tile_landed{r}") for r in range(RAW)]
        hi_ready, lo_ready, tile_used = sem("hi_ready"), sem("lo_ready"), sem("tile_used")
        x_landed, consts_landed = sem("x_landed"), sem("consts_landed")
        eps_set, zero_set = sem("eps_set"), sem("zero_set")
        vec_T, vec_ready = sem("vec_T"), sem("vec_ready")
        sq_sum, rms_mean, rms_inv = sem("sq_sum"), sem("rms_mean"), sem("rms_inv")
        xn1_ready, rows_done = sem("xn1_ready"), sem("rows_done")
        xn_ready, xn_T, h_hi, h_lo = sem("xn_ready"), sem("xn_T"), sem("h_hi"), sem("h_lo")
        x_added = sem("x_added")
        c_copied, cv_ready, conv_step, yc_ready, v_copied = (
            sem("c_copied"), sem("cv_ready"), sem("conv_step"), sem("yc_ready"), sem("v_copied"))
        pool_step, pool_mm = sem("pool_step"), sem("pool_mm")
        y_hi, y_lo = sem("y_hi"), sem("y_lo")
        bias_loaded, bias_T, bias_copied, bias_mm, bias_rows, bias_written, bt_landed, sink_landed = (
            sem("bias_loaded"), sem("bias_T"), sem("bias_copied"), sem("bias_mm"), sem("bias_rows"),
            sem("bias_written"), [sem(f"bt_landed{g}") for g in range(2)], sem("sink_landed"))
        emptied, b_squared, b_summed, b_mean, b_root, b_scaled, b_T, b_gated = (
            sem("emptied"), sem("b_squared"), sem("b_summed"), sem("b_mean"), sem("b_root"), sem("b_scaled"),
            sem("b_T"), sem("b_gated"))
        b_tanh, b_silu = sem("b_tanh"), sem("b_silu")
        c_step, c_exp, o_scaled, o_gated, br_hi, br_lo, m_mul, m_sum, m_hi, m_lo = (
            sem("c_step"), sem("c_exp"), sem("o_scaled"), sem("o_gated"), sem("br_hi"), sem("br_lo"),
            sem("m_mul"), sem("m_sum"), sem("m_hi"), sem("m_lo"))
        o_scaled_p = sem("o_scaled_p")
        nhalf_set, half_set = sem("nhalf_set"), sem("half_set")
        vec_landed, ident_landed, pw_landed = sem("vec_landed"), sem("ident_landed"), sem("pw_landed")
        silu_ready, gu_ready, gu_hi, gu_lo = sem("silu_ready"), sem("gu_ready"), sem("gu_hi"), sem("gu_lo")
        stored = sem("stored")
        s_ready, s_shifted, p_ready, pT_ready, pT_copied, pv_done, o_copied = (
            sem("s_ready"), sem("s_shifted"), sem("p_ready"), sem("pT_ready"), sem("pT_copied"),
            sem("pv_done"), sem("o_copied"))
        m1_consts, zpad_set, g_hi, g_lo, gate_tanh, gate_ready = (
            sem("m1_consts"), sem("zpad_set"), sem("g_hi"), sem("g_lo"), sem("gate_tanh"),
            sem("gate_ready"))
        th_ready, z_ready, conf_step, u_copied, u_squared, u_summed, u_mean, u_root = (
            sem("th_ready"), sem("z_ready"), sem("conf_step"), sem("u_copied"), sem("u_squared"),
            sem("u_summed"), sem("u_mean"), sem("u_root"))
        u_normed, kv_copied, rope_v, rope_p, heads_T, qT_ready, tok_ready = (
            sem("u_normed"), sem("kv_copied"), sem("rope_v"), sem("rope_p"), sem("heads_T"), sem("qT_ready"),
            sem("tok_ready"))
        hidt_copied, hid_T, conf_step_p = sem("hidt_copied"), sem("hid_T"), sem("conf_step_p")
        flat_ready, flat_hi, flat_lo, hid_copied, gelu_step, gelu_tanh, w2_done = (
            sem("flat_ready"), sem("flat_hi"), sem("flat_lo"), sem("hid_copied"), sem("gelu_step"),
            sem("gelu_tanh"), sem("w2_done"))
        kc_copied, kc_step, kc_summed, kc_T, kcT_ready = (
            sem("kc_copied"), sem("kc_step"), sem("kc_summed"), sem("kc_T"), sem("kcT_ready"))
        cs_ready, cs_step, cs_exp, pc_T, pcT_ready, oc_done = (
            sem("cs_ready"), sem("cs_step"), sem("cs_exp"), sem("pc_T"), sem("pcT_ready"), sem("oc_done"))
        fin_w, fin_v, fin_p, oacc_ready, oT_done, oT_hi, oT_lo = (
            sem("fin_w"), sem("fin_v"), sem("fin_p"), sem("oacc_ready"), sem("oT_done"), sem("oT_hi"),
            sem("oT_lo"))
        ln_mm, ln_dev, ln_sq, ln_root, ln_inv, ln_norm, z_silu, z_hi, z_lo = (
            sem("ln_mm"), sem("ln_dev"), sem("ln_sq"), sem("ln_root"), sem("ln_inv"), sem("ln_norm"),
            sem("z_silu"), sem("z_hi"), sem("z_lo"))

        mix0, mix1 = tile_list(a)
        N_MIX0 = 0
        N_FFN0 = N_MIX0 + len(mix0)
        N_MIX1 = N_FFN0 + 3 * FSTEPS
        N_FFN1 = N_MIX1 + len(mix1)
        N_B2 = N_FFN1 + 3 * FSTEPS
        total_tiles = N_B2 + 55

        def split_hi(act, n0, i=0):
            if isinstance(i, int) and n0 + 6 * i >= total_tiles:
                return
            act.wait_ge(tile_landed[n0 % RAW], i * (16 * 6 // RAW) + 16 * (n0 // RAW + 1))
            if not isinstance(i, int) or n0 + 6 * i >= SPLIT:
                act.wait_ge(tile_used, i * 6 + (n0 - SPLIT + 1))
            nc.scalar.activation(whi[:, n0 % SPLIT, :], raw[:, n0 % RAW, :], ACT.Copy).then_inc(hi_ready, 1)

        def split_lo(dve, n0, i=0):
            if isinstance(i, int) and n0 + 6 * i >= total_tiles:
                return
            dve.wait_ge(hi_ready, i * 6 + (n0 + 1))
            nc.vector.tensor_tensor(wlo[:, n0 % SPLIT, :], raw[:, n0 % RAW, :],
                                    whi[:, n0 % SPLIT, :].bitcast(F32), ALU.subtract).then_inc(lo_ready, 1)

        def load_tile(sp, n0, src, i=0):
            if not isinstance(i, int) or n0 + 6 * i >= RAW:
                sp.wait_ge(lo_ready, i * 6 + (n0 - RAW + 1))
            sp.dma_start(raw[:, n0 % RAW, :].rearrange("p (k n) -> p k n", k=src.shape[1]),
                         src).then_inc(tile_landed[n0 % RAW], 16)

        def product(dst, l_hi, l_lo, r_hi, r_lo, first, last):
            nc.tensor.matmul(dst, l_hi, r_hi, start=first, stop=False)
            nc.tensor.matmul(dst, l_hi, r_lo, start=False, stop=False)
            return nc.tensor.matmul(dst, l_lo, r_hi, start=False, stop=last)

        def w_parts(n, k):
            s = n % SPLIT
            return (whi[:, s, :].rearrange("p (k n) -> p k n", k=k), wlo[:, s, :].rearrange("p (k n) -> p k n", k=k))

        def wait_h(pe, e, k, bank=0):
            pe.wait_ge(h_lo, KC * e + max(k + 1, 2 * (bank - 4) + 2))

        def mm_feature(n, bank, norm=None):
            nc.tensor.wait_ge(lo_ready, n + 1)
            hi, lo = w_parts(n, KC)
            for f in range(2):
                for k in range(KC):
                    c = slice(f * P, f * P + P)
                    if f == 0 and norm is not None:
                        wait_h(nc.tensor, norm, k, bank)
                    mm = product(ps[:, bank, f * T:(f + 1) * T], hi[:, k, c], lo[:, k, c],
                                 hhi[:, k, :], hlo[:, k, :], k == 0, k == KC - 1)
            mm.then_inc(tile_used, 1)

        def mm_rows(n, lhs_hi, lhs_lo, k0, first, last, bank=0):
            hi, lo = w_parts(n, 2)
            for i in range(NT):
                for h in range(2):
                    for k in range(2):
                        tok, c = slice(i * P, i * P + P), slice(h * 512, h * 512 + 512)
                        mm = product(ps[:, bank + 2 * i + h, :], lhs_hi[:, k0 + k, tok], lhs_lo[:, k0 + k, tok],
                                     hi[:, k, c], lo[:, k, c], first and k == 0, last and k == 1)
                    if last and 2 * i + h < 3:
                        mm.then_inc(rows_done, 1)
            return mm

        def norm_act(act, e, v0):
            act.wait_ge(x_landed, 16)
            for i in range(NT):
                if e:
                    act.wait_ge(x_added, 4 * e - 2 + 2 * i)
                nc.scalar.activation(xn[:, i, :], x[:, i, :], ACT.Square,
                                     accum_out=ssum[:, i:i + 1]).then_inc(sq_sum, 1)
            if e == 0:
                split_hi(act, 0)
            act.wait_ge(rms_inv, NT * e + 2)
            nc.scalar.activation(xn[:, 1, :], x[:, 1, :], ACT.Copy, scale=sinv[:, 1:2]).then_inc(xn1_ready, 1)
            for k in range(KC):
                act.wait_ge(xn_T, 4 * e + k // 2 + 1)
                if k == 0:
                    act.wait_ge(vec_ready, 2)
                nc.scalar.activation(hhi[:, k, :], ps[:, 4 + k // 2, (k % 2) * T:(k % 2 + 1) * T], ACT.Copy,
                                     scale=vec[:, v0 + k:v0 + k + 1]).then_inc(h_hi, 1)

        def norm_pool(pool, e):
            for i in range(NT):
                t = slice(i, i + 1)
                pool.wait_ge(sq_sum, NT * e + i + 1)
                nc.gpsimd.tensor_scalar(smean[:, t], ssum[:, t], 1.0 / D, EPS, ALU.mult, ALU.add)\
                    .then_inc(rms_mean, 1)
                pool.wait_ge(rms_mean, NT * e + i + 1)
                nc.gpsimd.tensor_tensor(sinv[:, t], smean[:, t], nhalf[:, 0:1], ALU.pow).then_inc(rms_inv, 1)

        def norm_dve(dve, e, v0):
            dve.wait_ge(rms_inv, NT * e + 1)
            nc.vector.tensor_scalar(xn[:, 0, :], x[:, 0, :], sinv[:, 0:1], None, ALU.mult).then_inc(xn_ready, 1)
            if e == 0:
                dve.wait_ge(vec_T, 2)
                nc.vector.tensor_copy(vec[:, :], ps[:, 0, 0:V_ROWS]).then_inc(vec_ready, 1)
                nc.vector.tensor_copy(dwv[:, :, :].rearrange("p k c -> p (k c)"),
                                      ps[:, 1, 0:CONF_K * CC]).then_inc(vec_ready, 1)
                split_lo(dve, 0)
            else:
                split_lo(dve, (N_FFN0, N_MIX1, N_FFN1, N_B2)[e - 1] + 1)
            for k in range(KC):
                dve.wait_ge(h_hi, KC * e + k // 2 * 2 + 2)
                nc.vector.scalar_tensor_tensor(hlo[:, k, :], ps[:, 4 + k // 2, (k % 2) * T:(k % 2 + 1) * T],
                                               vec[:, v0 + k:v0 + k + 1], hhi[:, k, :].bitcast(F32),
                                               ALU.mult, ALU.subtract).then_inc(h_lo, 1)

        def norm_pe(pe, e):
            for i in range(NT):
                pe.wait_ge((xn_ready, xn1_ready)[i], e + 1)
                for k in range(KC):
                    c = (k % 2) * T + i * P
                    mm = nc.tensor.transpose(ps[:, 4 + k // 2, c:c + P], xn[:, i, k * P:(k + 1) * P], ident[:, :])
                    if i and k % 2:
                        mm.then_inc(xn_T, 1)

        def add_x(dve, e, last_tile, bank=0):
            for j in range(4):
                i, h = j // 2, j % 2
                if j < 3:
                    dve.wait_ge(rows_done, 3 * e + j + 1)
                else:
                    dve.wait_ge(tile_used, last_tile)
                xs = x[:, i, h * 512:(h + 1) * 512]
                nc.vector.tensor_tensor(xs, xs, ps[:, bank + j, :], ALU.add).then_inc(x_added, 1)

        def g_tile(n, c):
            return n if c == 0 else n + 3 * c - 1

        def d_tile(n, c):
            return n + 3 * c + 4 if c < FSTEPS - 1 else n + 3 * c + 2

        def ffn_src(l, kind, c):
            if kind == "d":
                return a["ffn_down"][l].rearrange("(k p) n -> p k n", p=P)[:, bass.ds(c * 2, 2), :]
            w = a["ffn_gate" if kind == "g" else "ffn_up"][l]
            return w.rearrange("(k p) n -> p k n", p=P)[:, :, bass.ds(c * FFC, FFC)]

        def steps_of(engine, step, tail):
            step(0, 0)
            step(1, 0)
            with engine.Fori(0, 4) as i:
                step(2, i)
                step(3, i)
            step(10, 0)
            tail()

        def ffn_sp(sp, l, n):
            def step(c, i):
                load_tile(sp, g_tile(n, c), ffn_src(l, "g", i * 2 + c), i)
                load_tile(sp, g_tile(n, c) + 1, ffn_src(l, "u", i * 2 + c), i)
                if c:
                    load_tile(sp, d_tile(n, c - 1), ffn_src(l, "d", i * 2 + (c - 1)), i)
            steps_of(sp, step, lambda: load_tile(sp, n + 32, ffn_src(l, "d", FSTEPS - 1)))

        def ffn_act(act, l, n):
            def step(c, i):
                g, b = g_tile(n, c), 4 + 2 * (c % 2)
                split_hi(act, g + 2, i)
                act.wait_ge(tile_used, i * 6 + (g + 1))
                nc.scalar.activation(sg[:, c % 2, :, :].rearrange("p f t -> p (f t)"), ps[:, b, :],
                                     ACT.Silu).then_inc(silu_ready, 1)
                if c:
                    split_hi(act, g + 3, i)
                split_hi(act, g + 3 + (1 if c else 0), i)
                act.wait_ge(gu_ready, i * 2 + (FSTEPS * l + c + 1))
                nc.scalar.activation(ghi[:, c % 2, :, :], gu[:, c % 2, :, :], ACT.Copy).then_inc(gu_hi, 1)
            steps_of(act, step, lambda: split_hi(act, n + 34))

        def ffn_dve(dve, l, n):
            def step(c, i):
                g, b = g_tile(n, c), 4 + 2 * (c % 2)
                split_lo(dve, g + 2, i)
                if c:
                    split_lo(dve, g + 3, i)
                dve.wait_ge(silu_ready, i * 2 + (FSTEPS * l + c + 1))
                dve.wait_ge(tile_used, i * 6 + (g + 2))
                nc.vector.tensor_tensor(gu[:, c % 2, :, :].rearrange("p f t -> p (f t)"),
                                        sg[:, c % 2, :, :].rearrange("p f t -> p (f t)"),
                                        ps[:, b + 1, :], ALU.mult).then_inc(gu_ready, 1)
                split_lo(dve, g + 3 + (1 if c else 0), i)
                dve.wait_ge(gu_hi, i * 2 + (FSTEPS * l + c + 1))
                nc.vector.tensor_tensor(glo[:, c % 2, :, :], gu[:, c % 2, :, :],
                                        ghi[:, c % 2, :, :].bitcast(F32), ALU.subtract).then_inc(gu_lo, 1)
            steps_of(dve, step, lambda: None)
            add_x(dve, 2 * l + 1, n + 3 * FSTEPS)

        def ffn_pe(pe, l, n):
            def down(c, i, first=False):
                t = d_tile(n, c)
                pe.wait_ge(lo_ready, i * 6 + (t + 1))
                pe.wait_ge(gu_lo, i * 2 + (FSTEPS * l + c + 1))
                mm = mm_rows(t, ghi[:, c % 2, :, :], glo[:, c % 2, :, :], 0, first, c == FSTEPS - 1)
                mm.then_inc(tile_used, 1)

            def step(c, i):
                g, b = g_tile(n, c), 4 + 2 * (c % 2)
                if c >= 2:
                    pe.wait_ge(gu_ready, i * 2 + (FSTEPS * l + c - 1))
                for t, bank in ((g, b), (g + 1, b + 1)):
                    pe.wait_ge(lo_ready, i * 6 + (t + 1))
                    hi, lo = w_parts(t, KC)
                    for f in range(2):
                        for k in range(KC):
                            cs = slice(f * P, f * P + P)
                            if c == 0 and t == g and f == 0:
                                wait_h(pe, 2 * l + 1, k, bank)
                            mm = product(ps[:, bank, f * T:(f + 1) * T], hi[:, k, cs], lo[:, k, cs],
                                         hhi[:, k, :], hlo[:, k, :], k == 0, k == KC - 1)
                    mm.then_inc(tile_used, 1)
                if c:
                    down(c - 1, i, c == 1)
            steps_of(pe, step, lambda: down(FSTEPS - 1, 0))

        def o_bank(g):
            return 4 + g % 2 if g < 4 else 4

        def job_s(pe, jobs, m0, m):
            q, k, bias, v, g = jobs[m]
            if m0 + m >= 2:
                pe.wait_ge(s_shifted, m0 + m - 1)
            nc.tensor.matmul(ps[:, (m0 + m) % 2, 0:len(v) * P], q, k, start=True, stop=True).then_inc(s_ready, 1)

        def job_t(pe, jobs, m0, m):
            n = m0 + m
            pe.wait_ge(p_ready, n + 1)
            if n >= 2:
                pe.wait_ge(pT_copied, n - 1)
            for j in range(len(jobs[m][3])):
                mm = nc.tensor.transpose(ps[:, 2 + n % 2, j * P:(j + 1) * P], pr[:, n % 4, j * P:(j + 1) * P],
                                         ident[:, :])
            mm.then_inc(pT_ready, 1)

        def job_pv(pe, jobs, m0, m):
            n, v, g = m0 + m, jobs[m][3], (m0 + m) // 8
            pe.wait_ge(pT_copied, n + 1)
            if n % 8 == 0 and g >= 2:
                pe.wait_ge(o_copied, g if g >= 4 else g - 1)
            for j in range(len(v)):
                mm = nc.tensor.matmul(ps[:, o_bank(g), (n % 8) * HD:(n % 8 + 1) * HD], pT[:, n % 2, j, :], v[j],
                                      start=(j == 0), stop=(j == len(v) - 1))
            mm.then_inc(pv_done, 1)

        def job_shift(dve, jobs, m0, m):
            n, (q, k, bias, v, g) = m0 + m, jobs[m]
            w = len(v) * P
            dve.wait_ge(s_ready, n + 1)
            if n >= 2:
                dve.wait_ge(p_ready, n - 1)
            nc.vector.tensor_tensor_reduce(lg[:, n % 2, 0:w], ps[:, n % 2, 0:w], bias, -1.0, 3e38, ALU.add,
                                           ALU.min, nmax[:, g, n % 8:n % 8 + 1]).then_inc(s_shifted, 1)

        def job_copy(dve, jobs, m0, m):
            n, w = m0 + m, len(jobs[m][3]) * P
            dve.wait_ge(pT_ready, n + 1)
            if n >= 2:
                dve.wait_ge(pv_done, n - 1)
            nc.vector.tensor_copy(pT[:, n % 2, :, :].rearrange("p j q -> p (j q)")[:, 0:w],
                                  ps[:, 2 + n % 2, 0:w]).then_inc(pT_copied, 1)

        def job_exp(act, jobs, m0, m):
            n, (q, k, bias, v, g) = m0 + m, jobs[m]
            w = len(v) * P
            act.wait_ge(s_shifted, n + 1)
            if n >= 4:
                act.wait_ge(pT_ready, n - 3)
            nc.scalar.activation(pr[:, n % 4, 0:w], lg[:, n % 2, 0:w], ACT.Exp, scale=-1.0,
                                 bias=nmax[:, g, n % 8:n % 8 + 1],
                                 accum_out=psum_[:, g, n % 8:n % 8 + 1]).then_inc(p_ready, 1)

        def group_out(act, g, dst, src=lambda bank: bank):
            act.wait_ge(pv_done, 8 * g + 8)
            nc.scalar.activation(dst, src(ps[:, o_bank(g), :]), ACT.Copy).then_inc(o_copied, 1)

        def pe_step(pe, jobs, m0, m):
            if m + 2 < len(jobs):
                job_s(pe, jobs, m0, m + 2)
            if 0 <= m < len(jobs):
                job_t(pe, jobs, m0, m)
            if m >= 1:
                job_pv(pe, jobs, m0, m - 1)

        def dve_step(dve, jobs, m0, m):
            if 0 <= m + 1 < len(jobs):
                job_shift(dve, jobs, m0, m + 1)
            if 0 <= m < len(jobs):
                job_copy(dve, jobs, m0, m)

        def act_step(act, jobs, m0, m):
            if 0 <= m + 1 < len(jobs):
                job_exp(act, jobs, m0, m + 1)

        jobs1 = []
        for i in range(NT):
            for br in range(2):
                for h in range(8):
                    half = slice((h % 2) * HD, (h % 2) * HD + HD)
                    jobs1.append((qT[half, h // 2, i * P:(i + 1) * P], kT[half, br, h // 4, 0:(i + 1) * P],
                                  causal[:, (1 - i) * P:T], [uk[:, j, 3 + 2 * br, h // 4, :] for j in range(i + 1)],
                                  2 * i + br))
        TOK, CMP, OUT1 = N_MIX1 + 2, N_MIX1 + 9, N_MIX1 + 13
        CONF = ((N_MIX1, N_MIX1 + 1), (N_MIX1 + 7, N_MIX1 + 8))
        TOK_STEP, FLAT_STEP, CMP_STEP, HT_STEP, GELU_STEP = (-1, 1), (0, 2), (4, 5, 9, 10), (6, 12), (7, 13)
        W2_STEP, KCT_STEP, SC_STEP, PCT_STEP, OC_STEP = (11, 17), 19, (20, 28), (23, 31), (25, 32)
        FIN_STEP, SUM_STEP, OT_STEP = (25, 33), (26, 34), (27, 35)
        LN_MEAN, LN_DEV, LN_SQ, LN_VAR, LN_ROOT, LN_NORM, LN_SILU, LN_LO = 26, 26, 27, 28, 29, 30, 32, 32
        GROUP_STEP = (9, 17, 25, 32)
        STEPS1, ROWS_STEP, SPLIT_STEP = range(-2, 36), 33, 15

        def mix1_pe(pe):
            mm_feature(CONF[0][0], 0, 2)
            mm_feature(CONF[0][1], 1)
            for t in range(2):
                for half in range(2):
                    n = TOK + 2 * t + half
                    pe.wait_ge(lo_ready, n + 1)
                    hi, lo = w_parts(n, 4)
                    for i in range(NT):
                        tok = slice(i * P, (i + 1) * P)
                        for k in range(4):
                            mm = product(ps[:, 4 + 2 * t + i, :], hhi[:, 4 * half + k, tok],
                                         hlo[:, 4 * half + k, tok], hi[:, k, :], lo[:, k, :],
                                         half == 0 and k == 0, half == 1 and k == 3)
                    mm.then_inc(tile_used, 1)
            n = TOK + 4
            pe.wait_ge(lo_ready, n + 1)
            pe.wait_ge(g_lo, 1)
            hi, lo = w_parts(n, KC)
            for i in range(NT):
                tok = slice(i * P, (i + 1) * P)
                for k in range(KC):
                    mm = product(ps[:, 2 + i, 256:280], hhi[:, k, tok], hlo[:, k, tok], gwhi[:, k, :],
                                 gwlo[:, k, :], k == 0, k == KC - 1)
                for k in range(KC):
                    mm = product(ps[:, 2 + i, 0:256], hhi[:, k, tok], hlo[:, k, tok], hi[:, k, :],
                                 lo[:, k, :], k == 0, k == KC - 1)
            mm.then_inc(tile_used, 1)
            pe.wait_ge(th_ready, 1)
            mm_feature(CONF[1][0], 0)
            pe.wait_ge(z_ready, 2)
            mm_feature(CONF[1][1], 1)
            pe.wait_ge(u_copied, 6)
            pe.wait_ge(gate_tanh, 2)
            for part, chunks in enumerate((range(4), range(4, 12))):
                for i in range(NT):
                    pe.wait_ge(rope_v, 4 * (2 * part + i + 1))
                    pe.wait_ge(rope_p, 2 * (2 * part + i + 1))
                    for c in chunks:
                        at = (c % 2) * T + i * P
                        mm = nc.tensor.transpose(ps[:, (4, 5, 2, 3, 6, 7)[c // 2], at:at + P],
                                                 hb[:, i, 2 * c:2 * c + 2, :].rearrange("p h d -> p (h d)"),
                                                 ident[:, :])
                mm.then_inc(heads_T, 1)

            def channel_mean(src, at):
                for c in range(CC):
                    mm = nc.tensor.matmul(ps[:, 4, at:at + T], onesd[:, :], src[:, c, :], start=(c == 0),
                                          stop=(c == CC - 1))
                mm.then_inc(ln_mm, 1)

            def out_rows(j, k0, first, last):
                n = OUT1 + j
                pe.wait_ge(lo_ready, n + 1)
                mm_rows(n, yhi, ylo, k0, first, last).then_inc(tile_used, 1)

            pe.wait_ge(qT_ready, 4)
            pe.wait_ge(th_ready, 2)
            pe.wait_ge(z_ready, 4)
            for m in STEPS1:
                if m in CMP_STEP:
                    r = CMP_STEP.index(m)
                    kv, half = r // 2, r % 2
                    n = CMP + r
                    pe.wait_ge(lo_ready, n + 1)
                    pe.wait_ge(flat_lo, kv + 1)
                    pe.wait_ge(tok_ready, 8)
                    if r == 2:
                        pe.wait_ge(hidt_copied, 1)
                    hi, lo = w_parts(n, KC)
                    for k in range(KC):
                        fh = flat_part(yhi, kv)[:, 8 * half + k, :]
                        fl = flat_part(ylo, kv)[:, 8 * half + k, :]
                        mm = product(ps[0:2 * N_CMP, 6, 0:T], fh, fl, hi[:, k, :], lo[:, k, :],
                                     half == 0 and k == 0, half == 1 and k == KC - 1)
                    mm.then_inc(tile_used, 1)
                pe_step(pe, jobs1, 0, m) if m <= len(jobs1) else None
                if m in HT_STEP:
                    kv = HT_STEP.index(m)
                    pe.wait_ge(hidt_copied, kv + 1)
                    if kv:
                        pe.wait_ge(kc_copied, 1)
                    for hc in range(2):
                        mm = nc.tensor.transpose(ps[:, 7, hc * 32:hc * 32 + 2 * N_CMP], hidt[:, hc * P:(hc + 1) * P],
                                                 ident[0:2 * N_CMP, 0:2 * N_CMP])
                    mm.then_inc(hid_T, 1)
                if m in W2_STEP:
                    kv = W2_STEP.index(m)
                    pe.wait_ge(gelu_step, 5 * (kv + 1))
                    for g in range(2):
                        for hc in range(2):
                            mm = nc.tensor.matmul(ps[0:N_CMP, 7, 128 * (kv + 1) + g * HD:128 * (kv + 1) + (g + 1) * HD],
                                                  hid2[:, kv, hc, g * N_CMP:(g + 1) * N_CMP], cw2[:, kv, hc, :],
                                                  start=(hc == 0), stop=(hc == 1))
                    mm.then_inc(w2_done, 1)
                if m == KCT_STEP:
                    pe.wait_ge(kc_step, 5)
                    pe.wait_ge(kc_copied, 2)
                    for g in range(2):
                        mm = nc.tensor.transpose(ps[:, 7, g * 16:g * 16 + N_CMP],
                                                 kcn[:, 3, g, :, :].rearrange("p c d -> p (c d)"),
                                                 ident[0:N_CMP, 0:N_CMP])
                    mm.then_inc(kc_T, 1)
                if m in SC_STEP:
                    i = SC_STEP.index(m)
                    pe.wait_ge(kcT_ready, 1)
                    if i:
                        pe.wait_ge(oT_lo, 1)
                    for h in range(8):
                        half = slice((h % 2) * HD, (h % 2) * HD + HD)
                        mm = nc.tensor.matmul(ps[:, 6 + h % 2, h // 2 * N_CMP:(h // 2 + 1) * N_CMP],
                                              qT[half, h // 2, i * P:(i + 1) * P],
                                              kcT[half, h // 4, 0:N_CMP], start=True, stop=True)
                    mm.then_inc(cs_ready, 1)
                if m in PCT_STEP:
                    i = PCT_STEP.index(m)
                    pe.wait_ge(cs_step, 7 * i + 4)
                    for h in range(8):
                        mm = nc.tensor.transpose(ps[0:N_CMP, 6 + h // 4, (h % 4) * P:(h % 4 + 1) * P],
                                                 pc[:, i, h, :], ident[:, :])
                    mm.then_inc(pc_T, 1)
                if m in OC_STEP:
                    i = OC_STEP.index(m)
                    pe.wait_ge(pcT_ready, 2 * i + 2)
                    for h in range(8):
                        mm = nc.tensor.matmul(ps[:, 6, h * HD:(h + 1) * HD], pcT[:, h, :], vcs[:, h // 4, :],
                                              start=True, stop=True)
                    mm.then_inc(oc_done, 1)
                if m in OT_STEP:
                    i = OT_STEP.index(m)
                    pe.wait_ge(oacc_ready, i + 1)
                    for c in range(4):
                        mm = nc.tensor.transpose(ps[:, 7, c * P:(c + 1) * P], oacc[:, i, c * P:(c + 1) * P], ident[:, :])
                    mm.then_inc(oT_done, 1)
                if m == LN_MEAN:
                    pe.wait_ge(conf_step, 3 * CONF_K)
                    pe.wait_ge(conf_step_p, 2 * CONF_K - 1)
                    pe.wait_ge(o_copied, 3)
                    channel_mean(zc, 0)
                if m == LN_VAR:
                    pe.wait_ge(ln_sq, 1)
                    channel_mean(dsq, T)
                if m == ROWS_STEP:
                    pe.wait_ge(z_lo, 1)
                    out_rows(0, 4, True, False)
                    out_rows(1, 6, False, False)
            pe.wait_ge(oT_lo, 2)
            out_rows(2, 0, False, False)
            out_rows(3, 2, False, True)

        def flat_part(y, kv):
            return y[:, 2 * kv:2 * kv + 2, :].rearrange("p a t -> p (a t)")[:, 0:16 * 2 * N_CMP]\
                .rearrange("p (j n) -> p j n", j=16)

        def m1_loads(act):
            act.wait_ge(bias_written, 16 * BIAS_WRITES)
            k_norm = a["k_norm"][0]
            w_gate = a["w_in_odd"][0].rearrange("(k p) n -> p k n", p=P)[:, :, 1280:1304]
            for dst, src in (
                    (gwr[:, :, :], w_gate),
                    (gains[:, 0:8, :], a["q_norm"][0:1].partition_broadcast(P).broadcast_to([P, 8, HD])),
                    (gains[:, 8:12, :], k_norm[0:1].partition_broadcast(P).broadcast_to([P, 4, HD])),
                    (gains[:, 12:16, :], k_norm[1:2].partition_broadcast(P).broadcast_to([P, 4, HD])),
                    (g2[:, :], k_norm[2].partition_broadcast(N_CMP)),
                    (cosn[:, :, :], a["c_cos"].rearrange("(i p) c -> p i c", p=P)),
                    (sinn[:, :, :], a["c_sin"].rearrange("(i p) c -> p i c", p=P)),
                    (causal[:, :], a["c_causal"]),
                    (seen[:, :, :], a["c_seen"].rearrange("(i p) c -> p i c", p=P)),
                    (unseen[:, :, :], a["c_unseen"].rearrange("(i p) c -> p i c", p=P)),
                    (cw2[:, 0, :, :], a["cmp_w2"][0, 0].rearrange("(c p) n -> p c n", p=P)),
                    (cw2[:, 1, :, :], a["cmp_w2"][0, 1].rearrange("(c p) n -> p c n", p=P))):
                act.dma_start(dst, src).then_inc(m1_consts, 16)

        def mix1_act(act):
            act.wait_ge(m1_consts, 16 * 12)
            nc.scalar.activation(gwhi[:, :, :], gwr[:, :, :], ACT.Copy).then_inc(g_hi, 1)

            def conf_tanh(pair):
                act.wait_ge(tile_used, CONF[pair][0] + 1)
                nc.scalar.activation(th[:, pair, :, :].rearrange("p f t -> p (f t)"), ps[:, 0, :], ACT.Tanh,
                                     scale=0.5).then_inc(th_ready, 1)

            for t in range(9):
                split_hi(act, N_MIX1 + t + 2)
                if t == 0:
                    conf_tanh(0)
                if t == 3:
                    act.wait_ge(tile_used, TOK + 2)
                    for i in range(NT):
                        nc.scalar.activation(uq[:, i, :, :].rearrange("p h d -> p (h d)"), ps[:, 4 + i, :],
                                             ACT.Copy).then_inc(u_copied, 1)
                if t == 5:
                    act.wait_ge(tile_used, TOK + 4)
                    for i in range(NT):
                        nc.scalar.activation(uk[:, i, 0:4, :, :].rearrange("p a g d -> p (a g d)"),
                                             ps[:, 6 + i, :], ACT.Copy).then_inc(u_copied, 1)
                if t == 6:
                    act.wait_ge(tile_used, TOK + 5)
                    for i in range(NT):
                        nc.scalar.activation(uk[:, i, 4:6, :, :].rearrange("p a g d -> p (a g d)"),
                                             ps[:, 2 + i, 0:256], ACT.Copy).then_inc(u_copied, 1)
                        nc.scalar.activation(gth[:, i, :], ps[:, 2 + i, 256:280], ACT.Tanh,
                                             scale=0.5).then_inc(gate_tanh, 1)
                if t == 7:
                    conf_tanh(1)
            act.wait_ge(heads_T, 1)
            for b in range(2):
                nc.scalar.activation(qT[:, 2 * b:2 * b + 2, :].rearrange("p c t -> p (c t)"), ps[:, 4 + b, :],
                                     ACT.Copy, scale=HD ** -0.5).then_inc(qT_ready, 1)
            act.wait_ge(heads_T, 2)
            for b in range(2):
                nc.scalar.activation(kT[:, b, :, :].rearrange("p c t -> p (c t)"), ps[:, 2 + b, :],
                                     ACT.Copy).then_inc(qT_ready, 1)
            for m in STEPS1:
                if m in CMP_STEP:
                    split_hi(act, CMP + CMP_STEP.index(m) + 2)
                act_step(act, jobs1, 0, m)
                if m in TOK_STEP:
                    b = TOK_STEP.index(m)
                    for c in range(2):
                        nc.scalar.activation(tok2[0:HD, b, c, :], ps[0:HD, 6 + b, c * T:(c + 1) * T],
                                             ACT.Copy).then_inc(tok_ready, 1)
                        nc.scalar.activation(tok2[HD:P, b, c, 0:T - 1], ps[HD:P, 6 + b, c * T + 1:(c + 1) * T],
                                             ACT.Copy).then_inc(tok_ready, 1)
                if m in FLAT_STEP:
                    kv = FLAT_STEP.index(m)
                    act.wait_ge(flat_ready, kv + 1)
                    nc.scalar.activation(flat_part(yhi, kv), flat[:, kv, :, :], ACT.Copy).then_inc(flat_hi, 1)
                if m in HT_STEP:
                    kv = HT_STEP.index(m)
                    act.wait_ge(tile_used, CMP + 2 * kv + 2)
                    nc.scalar.activation(hidt, ps[0:2 * N_CMP, 6, 0:T], ACT.Copy).then_inc(hidt_copied, 1)
                if m in GELU_STEP:
                    kv = GELU_STEP.index(m)
                    act.wait_ge(hid_T, kv + 1)
                    nc.scalar.activation(hid[:, 0, :, :],
                                         ps[:, 7, 0:64].rearrange("p (c n) -> p c n", c=2)[:, :, 0:2 * N_CMP],
                                         ACT.Copy).then_inc(hid_copied, 1)
                if m - 2 in GELU_STEP:
                    kv = GELU_STEP.index(m - 2)
                    act.wait_ge(gelu_step, 5 * kv + 3)
                    nc.scalar.activation(hid[:, 3, :, :], hid[:, 3, :, :], ACT.Tanh,
                                         scale=0.7978845608028654).then_inc(gelu_tanh, 1)
                if m == W2_STEP[0] + 1:
                    act.wait_ge(w2_done, 1)
                    nc.scalar.activation(kcn[:, 0, :, 0, :], ps[0:N_CMP, 7, 128:256].rearrange("p (g d) -> p g d", g=2),
                                         ACT.Copy).then_inc(kc_copied, 1)
                if m == W2_STEP[1] + 1:
                    act.wait_ge(w2_done, 2)
                    nc.scalar.activation(vcs[:, :, :], ps[0:N_CMP, 7, 256:384].rearrange("p (g d) -> p g d", g=2),
                                         ACT.Copy).then_inc(kc_copied, 1)
                if m == KCT_STEP:
                    act.wait_ge(kc_T, 1)
                    nc.scalar.activation(kcT[:, :, 0:N_CMP],
                                         ps[:, 7, 0:32].rearrange("p (g n) -> p g n", g=2)[:, :, 0:N_CMP],
                                         ACT.Copy).then_inc(kcT_ready, 1)
                if m - 1 in SC_STEP:
                    i = SC_STEP.index(m - 1)
                    act.wait_ge(cs_step, 7 * i + 3)
                    nc.scalar.activation(pc[:, i, :, :], pc[:, i, :, :], ACT.Exp).then_inc(cs_exp, 1)
                if m in PCT_STEP:
                    i = PCT_STEP.index(m)
                    act.wait_ge(pc_T, i + 1)
                    for b in range(2):
                        nc.scalar.activation(pcT[:, 4 * b:4 * b + 4, :].rearrange("p h q -> p (h q)"),
                                             ps[0:N_CMP, 6 + b, :], ACT.Copy).then_inc(pcT_ready, 1)
                if m in GROUP_STEP:
                    g = GROUP_STEP.index(m)
                    group_out(act, g, obr[:, g // 2, g % 2, :])
                if m in OT_STEP:
                    i = OT_STEP.index(m)
                    act.wait_ge(oT_done, i + 1)
                    nc.scalar.activation(yhi[:, 0:4, i * P:(i + 1) * P],
                                         ps[:, 7, :].rearrange("p (c q) -> p c q", c=4), ACT.Copy).then_inc(oT_hi, 1)
                if m == SPLIT_STEP:
                    split_hi(act, OUT1 + 2)
                if m == LN_SQ:
                    act.wait_ge(ln_dev, 1)
                    nc.scalar.activation(dsq[:, :, :], zc[:, :, :], ACT.Square).then_inc(ln_sq, 1)
                if m == LN_ROOT:
                    act.wait_ge(ln_mm, 2)
                    nc.scalar.activation(rstd[:, :], ps[:, 4, T:2 * T], ACT.Sqrt, bias=eps[:, 0:1]).then_inc(ln_root, 1)
                if m == LN_SILU:
                    act.wait_ge(ln_norm, 1)
                    for c in range(CC):
                        nc.scalar.activation(dsq[:, c, :], zc[:, c, :], ACT.Silu,
                                             scale=vec[:, V_LNG + c:V_LNG + c + 1],
                                             bias=vec[:, V_LNB + c:V_LNB + c + 1]).then_inc(z_silu, 1)
                    act.wait_ge(z_silu, CC)
                    nc.scalar.activation(yhi[:, 4:8, :], dsq[:, :, :], ACT.Copy).then_inc(z_hi, 1)
                if m == ROWS_STEP:
                    split_hi(act, OUT1 + 3)
            split_hi(act, OUT1 + 4)
            split_hi(act, OUT1 + 5)

        def mix1_dve(dve):
            dve.wait_ge(bias_written, 16 * BIAS_WRITES)
            dve.wait_ge(g_hi, 1)
            nc.vector.tensor_tensor(gwlo[:, :, :], gwr[:, :, :], gwhi[:, :, :].bitcast(F32),
                                    ALU.subtract).then_inc(g_lo, 1)
            dve.wait_ge(zpad_set, 1)
            dve.wait_ge(half_set, 1)

            def conf_z(pair):
                dve.wait_ge(th_ready, pair + 1)
                dve.wait_ge(tile_used, CONF[pair][1] + 1)
                for f in range(2):
                    nc.vector.scalar_tensor_tensor(zp[:, 2 * pair + f, CONF_K - 1:], th[:, pair, f, :], 1.0,
                                                   ps[:, 1, f * T:(f + 1) * T], ALU.add, ALU.mult)\
                        .then_inc(z_ready, 1)

            conv_at = [0]

            def conf_taps(count, last=2 * CONF_K):
                for _ in range(count):
                    s = conv_at[0]
                    if s >= last:
                        return
                    conv_at[0] += 1
                    k, c = (s // 2, s % 2) if s < 2 * CONF_K else (s - 2 * CONF_K, 2)
                    src, w = zp[:, c, k:k + T], dwv[:, k, c:c + 1]
                    if k == 0:
                        dve.wait_ge(z_ready, c + 1)
                        nc.vector.tensor_scalar(zc[:, c, :], src, w, vec[:, V_DWB + c:V_DWB + c + 1], ALU.mult,
                                                ALU.add).then_inc(conf_step, 1)
                    else:
                        dve.wait_ge(conf_step, s if c == 2 else s - 1)
                        nc.vector.scalar_tensor_tensor(zc[:, c, :], src, w, zc[:, c, :], ALU.mult,
                                                       ALU.add).then_inc(conf_step, 1)

            def bc(ap, n, axis):
                return ap.unsqueeze(axis).broadcast_to([*ap.shape[:axis], n, *ap.shape[axis:]])

            def rope_norm(part, i):
                n = 2 * part + i
                hs = slice(0, 8) if part == 0 else slice(8, 12)
                dve.wait_ge(u_squared, (1, 2, 4, 6)[n])
                nc.vector.tensor_reduce(u_ss[:, 0, i, hs], usq[:, hs, :], AX.X, ALU.add).then_inc(u_summed, 1)
                conf_taps(4 - 2 * part)
                dve.wait_ge(u_root, n + 1)
                inv = u_inv[:, i, :]
                if part == 0:
                    nc.vector.tensor_tensor(hb[:, i, 0:8, :], uq[:, i, :, :], bc(inv[:, 0:8], HD, 2),
                                            ALU.mult).then_inc(u_normed, 1)
                else:
                    for b in range(2):
                        for g in range(2):
                            at = 8 + 4 * b + 2 * g
                            nc.vector.tensor_scalar(hb[:, i, at:at + 2, :], bc(uk[:, i, 2 + 2 * b, g, :], 2, 1),
                                                    inv[:, 8 + 2 * b + g:9 + 2 * b + g], None, ALU.mult)\
                                .then_inc(u_normed, 1)
                normed = slice(8 * part, 8 * part + 8)
                dve.wait_ge(u_normed, (1, 3, 8, 13)[n])
                nc.vector.tensor_tensor(hb[:, i, normed, :], hb[:, i, normed, :], gains[:, normed, :],
                                        ALU.mult).then_inc(u_normed, 1)
                if part:
                    dve.wait_ge(kv_copied, 2 * (i + 1))
                dve.wait_ge(u_normed, (2, 4, 9, 14)[n])
                hs, w = (slice(0, 8), 8) if part == 0 else (slice(8, 20), 12)
                x1, x2 = hb[:, i, hs, 0:32], hb[:, i, hs, 32:64]
                if n:
                    dve.wait_ge(rope_p, 2 * n)
                nc.vector.tensor_tensor(rt[:, 3, 0:w], x1, bc(sinn[:, i, :], w, 1), ALU.mult).then_inc(rope_v, 1)
                nc.vector.tensor_tensor(rt[:, 0, 0:w], x1, bc(cosn[:, i, :], w, 1), ALU.mult).then_inc(rope_v, 1)
                nc.vector.tensor_tensor(rt[:, 1, 0:w], x2, bc(sinn[:, i, :], w, 1), ALU.mult).then_inc(rope_v, 1)
                conf_taps(2 - part)
                dve.wait_ge(rope_v, 4 * n + 3)
                nc.vector.tensor_tensor(x1, rt[:, 0, 0:w], rt[:, 1, 0:w], ALU.subtract).then_inc(rope_v, 1)

            for t in range(9):
                split_lo(dve, N_MIX1 + t + 2)
                if t == 1:
                    conf_z(0)
                if t >= 1:
                    conf_taps((0, 3, 7, 7, 0, 0, 2, 0, 0)[t])
                if t == 4:
                    rope_norm(0, 0)
                if t == 5:
                    rope_norm(0, 1)
                if t == 6:
                    rope_norm(1, 0)
                    rope_norm(1, 1)
            conf_z(1)

            def flat_blocks(kv):
                dve.wait_ge(tok_ready, 4 * kv + 4)
                src = tok2[:, kv, :, :]
                view = bass.AP(tensor=src.tensor, offset=src.offset,
                               ap=[list(src.ap[0]), [2, 16], [T, 2], [16, N_CMP]])
                pos = bc(bc(vec[:, V_POS + 16 * kv:V_POS + 16 * kv + 16], 2, 2), N_CMP, 3)
                nc.vector.tensor_tensor(flat[:, kv, :, :].rearrange("p j (g n) -> p j g n", g=2), view, pos,
                                        ALU.add).then_inc(flat_ready, 1)

            def finish(i):
                dve.wait_ge(o_copied, 2 * i + 2)
                dve.wait_ge(p_ready, 16 * i + 16)
                nc.vector.reciprocal(rsum[:, 2 * i:2 * i + 2, :], psum_[:, 2 * i:2 * i + 2, :]).then_inc(fin_w, 1)
                dve.wait_ge(fin_w, 4 * i + 1)
                dve.wait_ge(gate_ready, 1)
                g3 = gate3[:, i, :].rearrange("p (h b) -> p b h", b=3)
                dve.wait_ge(cs_step, 7 * i + 7)
                nc.vector.tensor_tensor(wgt[:, i, 0, :], g3[:, 0, :], cst[:, i, 2, :], ALU.mult).then_inc(fin_w, 1)
                for b in range(2):
                    nc.vector.tensor_tensor(wgt[:, i, 1 + b, :], g3[:, 1 + b, :], rsum[:, 2 * i + b, :],
                                            ALU.mult).then_inc(fin_w, 1)

            def sum_branches(i):
                dve.wait_ge(fin_w, 4 * i + 4)
                dve.wait_ge(oc_done, i + 1)
                nc.vector.tensor_tensor(oacc[:, i, :].rearrange("p (h d) -> p h d", h=8),
                                        ps[:, 6, :].rearrange("p (h d) -> p h d", h=8),
                                        bc(wgt[:, i, 0, :], HD, 2), ALU.mult).then_inc(fin_v, 1)
                dve.wait_ge(fin_v, i + 1)
                dve.wait_ge(fin_p, 3 * i + 3)
                nc.vector.tensor_tensor(oacc[:, i, :], oacc[:, i, :], ot[:, 0, :], ALU.add)\
                    .then_inc(oacc_ready, 1)

            for m in STEPS1:
                if m in CMP_STEP:
                    split_lo(dve, CMP + CMP_STEP.index(m) + 2)
                dve_step(dve, jobs1, 0, m)
                if m in TOK_STEP:
                    flat_blocks(TOK_STEP.index(m))
                if m - 1 in FLAT_STEP:
                    kv = FLAT_STEP.index(m - 1)
                    dve.wait_ge(flat_hi, kv + 1)
                    nc.vector.tensor_tensor(flat_part(ylo, kv), flat[:, kv, :, :], flat_part(yhi, kv).bitcast(F32),
                                            ALU.subtract).then_inc(flat_lo, 1)
                if m == W2_STEP[0] + 2:
                    dve.wait_ge(kc_step, 1)
                    nc.vector.tensor_reduce(kc_ss[:, 0, :], kcn[:, 1, :, 0, :], AX.X, ALU.add).then_inc(kc_summed, 1)
                if m - 1 in SC_STEP:
                    i = SC_STEP.index(m - 1)
                    s, c = pc[:, i, :, :], cst[:, i]
                    dve.wait_ge(cs_ready, i + 1)
                    nc.vector.tensor_tensor(s.rearrange("p (q b) n -> p b q n", b=2),
                                            ps[:, 6:8, 0:4 * N_CMP].rearrange("p b (q n) -> p b q n", q=4),
                                            bc(bc(unseen[:, i, :], 4, 1), 2, 1), ALU.add).then_inc(cs_step, 1)
                    dve.wait_ge(cs_step, 7 * i + 1)
                    nc.vector.tensor_reduce(c[:, 0, :], s, AX.X, ALU.max).then_inc(cs_step, 1)
                    dve.wait_ge(cs_step, 7 * i + 2)
                    nc.vector.tensor_tensor(s, s, bc(c[:, 0, :], N_CMP, 2), ALU.subtract).then_inc(cs_step, 1)
                if m - 2 in SC_STEP:
                    i = SC_STEP.index(m - 2)
                    s, c = pc[:, i, :, :], cst[:, i]
                    dve.wait_ge(cs_exp, i + 1)
                    nc.vector.tensor_tensor(s, s, bc(seen[:, i, :], 8, 1), ALU.mult).then_inc(cs_step, 1)
                    dve.wait_ge(cs_step, 7 * i + 4)
                    nc.vector.tensor_reduce(c[:, 1, :], s, AX.X, ALU.add).then_inc(cs_step, 1)
                    dve.wait_ge(cs_step, 7 * i + 5)
                    nc.vector.tensor_scalar(c[:, 1, :], c[:, 1, :], TINY, None, ALU.max).then_inc(cs_step, 1)
                    dve.wait_ge(cs_step, 7 * i + 6)
                    nc.vector.reciprocal(c[:, 2, :], c[:, 1, :]).then_inc(cs_step, 1)
                if m in FIN_STEP:
                    finish(FIN_STEP.index(m))
                if m in SUM_STEP:
                    sum_branches(SUM_STEP.index(m))
                if m in OT_STEP:
                    i = OT_STEP.index(m)
                    dve.wait_ge(oT_hi, i + 1)
                    nc.vector.tensor_tensor(ylo[:, 0:4, i * P:(i + 1) * P],
                                            ps[:, 7, :].rearrange("p (c q) -> p c q", c=4),
                                            yhi[:, 0:4, i * P:(i + 1) * P].bitcast(F32),
                                            ALU.subtract).then_inc(oT_lo, 1)
                conf_taps(2, 3 * CONF_K)
                if m == SPLIT_STEP:
                    split_lo(dve, OUT1 + 2)
                if m == LN_DEV:
                    conf_taps(3 * CONF_K, 3 * CONF_K)
                    dve.wait_ge(ln_mm, 1)
                    nc.vector.tensor_tensor(zc[:, :, :], zc[:, :, :], bc(ps[:, 4, 0:T], CC, 1), ALU.subtract)\
                        .then_inc(ln_dev, 1)
                if m == LN_NORM:
                    dve.wait_ge(ln_root, 1)
                    nc.vector.reciprocal(rstd[:, :], rstd[:, :]).then_inc(ln_inv, 1)
                    dve.wait_ge(ln_inv, 1)
                    nc.vector.tensor_tensor(zc[:, :, :], zc[:, :, :], bc(rstd[:, :], CC, 1), ALU.mult)\
                        .then_inc(ln_norm, 1)
                if m == LN_LO:
                    dve.wait_ge(z_hi, 1)
                    nc.vector.tensor_tensor(ylo[:, 4:8, :], dsq[:, :, :], yhi[:, 4:8, :].bitcast(F32),
                                            ALU.subtract).then_inc(z_lo, 1)
                if m == ROWS_STEP + 1:
                    split_lo(dve, OUT1 + 3)
            split_lo(dve, OUT1 + 4)
            add_x(dve, 2, N_FFN1)

        def mix1_pool(pool):
            pool.wait_ge(x_added, 8)
            pool.wait_ge(bias_written, 16 * BIAS_WRITES)
            nc.gpsimd.memset(zp[:, :, 0:CONF_K - 1], 0.0).then_inc(zpad_set, 1)

            def bc(ap, n, axis):
                return ap.unsqueeze(axis).broadcast_to([*ap.shape[:axis], n, *ap.shape[axis:]])

            def squares_q(i):
                pool.wait_ge(u_copied, i + 1)
                if i:
                    pool.wait_ge(u_summed, 1)
                nc.gpsimd.tensor_tensor(usq[:, 0:8, :], uq[:, i], uq[:, i], ALU.mult).then_inc(u_squared, 1)

            def squares_k(i):
                pool.wait_ge(u_copied, 5 + i)
                if i:
                    pool.wait_ge(u_summed, 3)
                for b in range(2):
                    k = uk[:, i, 2 + 2 * b, :, :]
                    nc.gpsimd.tensor_tensor(usq[:, 8 + 2 * b:10 + 2 * b, :], k, k, ALU.mult).then_inc(u_squared, 1)

            def copies(i):
                for b in range(2):
                    nc.gpsimd.tensor_copy(hb[:, i, 16 + 4 * b:20 + 4 * b, :].rearrange("p (g c) d -> p g c d", g=2),
                                          bc(uk[:, i, b, :, :], 2, 2)).then_inc(kv_copied, 1)

            def roots(part, i):
                n = 2 * part + i
                hs = slice(0, 8) if part == 0 else slice(8, 12)
                pool.wait_ge(u_summed, n + 1)
                nc.gpsimd.tensor_scalar(u_ss[:, 1, i, hs], u_ss[:, 0, i, hs], 1.0 / HD, EPS, ALU.mult, ALU.add)\
                    .then_inc(u_mean, 1)
                pool.wait_ge(u_mean, n + 1)
                nc.gpsimd.tensor_tensor(u_inv[:, i, hs], u_ss[:, 1, i, hs], nhalf[:, hs], ALU.pow).then_inc(u_root, 1)

            def rope(part, i):
                n = 2 * part + i
                hs, w = (slice(0, 8), 8) if part == 0 else (slice(8, 20), 12)
                pool.wait_ge(u_normed, (2, 4, 9, 14)[n])
                if part:
                    pool.wait_ge(kv_copied, 2 * i + 2)
                x2 = hb[:, i, hs, 32:64]
                nc.gpsimd.tensor_tensor(rt[:, 2, 0:w], x2, bc(cosn[:, i, :], w, 1), ALU.mult).then_inc(rope_p, 1)
                pool.wait_ge(rope_p, 2 * n + 1)
                pool.wait_ge(rope_v, 4 * n + 3)
                nc.gpsimd.tensor_tensor(x2, rt[:, 2, 0:w], rt[:, 3, 0:w], ALU.add).then_inc(rope_p, 1)

            conv_at = [0]

            def taps(count):
                c = 3
                for _ in range(count):
                    k = conv_at[0]
                    conv_at[0] += 1
                    src, w = zp[:, c, k:k + T], dwv[:, k, c:c + 1]
                    if k == 0:
                        pool.wait_ge(z_ready, 4)
                        nc.gpsimd.tensor_scalar(zc[:, c, :], src, w, vec[:, V_DWB + c:V_DWB + c + 1], ALU.mult,
                                                ALU.add).then_inc(conf_step_p, 1)
                    else:
                        nc.gpsimd.tensor_tensor(tapp[:, k % 2, :], src, w.broadcast_to([P, T]),
                                                ALU.mult).then_inc(conf_step_p, 1)
                        pool.wait_ge(conf_step_p, 2 * k)
                        nc.gpsimd.tensor_tensor(zc[:, c, :], zc[:, c, :], tapp[:, k % 2, :],
                                                ALU.add).then_inc(conf_step_p, 1)

            squares_q(0)
            roots(0, 0)
            rope(0, 0)
            squares_q(1)
            roots(0, 1)
            rope(0, 1)
            pool.wait_ge(u_copied, 3)
            pool.wait_ge(u_copied, 4)
            squares_k(0)
            copies(0)
            roots(1, 0)
            copies(1)
            rope(1, 0)
            squares_k(1)
            roots(1, 1)
            rope(1, 1)
            pool.wait_ge(gate_tanh, 2)
            nc.gpsimd.tensor_scalar(gate3[:, :, :], gth[:, :, :], 0.5, 0.5, ALU.mult, ALU.add).then_inc(gate_ready, 1)

            def gelu(kv):
                h = hid[:, 0]
                pool.wait_ge(hid_copied, kv + 1)
                nc.gpsimd.tensor_tensor(hid[:, 1], h, h, ALU.mult).then_inc(gelu_step, 1)
                pool.wait_ge(gelu_step, 5 * kv + 1)
                nc.gpsimd.tensor_scalar(hid[:, 2], hid[:, 1], 0.044715, 1.0, ALU.mult, ALU.add).then_inc(gelu_step, 1)
                pool.wait_ge(gelu_step, 5 * kv + 2)
                nc.gpsimd.tensor_tensor(hid[:, 3], hid[:, 2], h, ALU.mult).then_inc(gelu_step, 1)
                pool.wait_ge(gelu_tanh, kv + 1)
                nc.gpsimd.tensor_scalar(hid[:, 4], hid[:, 3], 1.0, 0.5, ALU.add, ALU.mult).then_inc(gelu_step, 1)
                pool.wait_ge(gelu_step, 5 * kv + 4)
                nc.gpsimd.tensor_tensor(hid2[:, kv], hid[:, 4], h, ALU.mult).then_inc(gelu_step, 1)

            taps(8)
            gelu(0)
            taps(3)
            pool.wait_ge(kc_copied, 1)
            raw_kc = kcn[:, 0, :, 0, :]
            nc.gpsimd.tensor_tensor(kcn[:, 1, :, 0, :], raw_kc, raw_kc, ALU.mult).then_inc(kc_step, 1)
            nc.gpsimd.tensor_tensor(kcn[:, 2, :, 0, :], raw_kc, bc(g2[:, :], 2, 1), ALU.mult).then_inc(kc_step, 1)
            pool.wait_ge(kc_summed, 1)
            nc.gpsimd.tensor_scalar(kc_ss[:, 1, :], kc_ss[:, 0, :], 1.0 / HD, EPS, ALU.mult, ALU.add)\
                .then_inc(kc_step, 1)
            pool.wait_ge(kc_step, 3)
            nc.gpsimd.tensor_tensor(kc_ss[:, 2, :], kc_ss[:, 1, :], nhalf[0:N_CMP, 0:2], ALU.pow).then_inc(kc_step, 1)
            pool.wait_ge(kc_step, 4)
            nc.gpsimd.tensor_tensor(kcn[:, 3, :, :, :], bc(kcn[:, 2, :, 0, :], 2, 2),
                                    bc(bc(kc_ss[:, 2, :], 2, 2), HD, 3), ALU.mult).then_inc(kc_step, 1)
            gelu(1)
            taps(CONF_K - 11)

            def sum_two(i):
                pool.wait_ge(fin_w, 4 * i + 4)
                pool.wait_ge(o_copied, 2 * i + 2)
                if i:
                    pool.wait_ge(oacc_ready, 1)
                for b in range(2):
                    nc.gpsimd.tensor_tensor(ot[:, b, :].rearrange("p (h d) -> p h d", h=8),
                                            obr[:, i, b, :].rearrange("p (h d) -> p h d", h=8),
                                            bc(wgt[:, i, 1 + b, :], HD, 2), ALU.mult).then_inc(fin_p, 1)
                pool.wait_ge(fin_p, 3 * i + 2)
                nc.gpsimd.tensor_tensor(ot[:, 0, :], ot[:, 0, :], ot[:, 1, :], ALU.add).then_inc(fin_p, 1)

            sum_two(0)
            sum_two(1)

        W2 = a["w_in_2"][0].rearrange("(k p) n -> p k n", p=P)
        Q_COL = (0, 2048, 2560, 3072, 7168)
        K_COL = (512, 3584, 4096, 4608, 7680)
        V_COL = (1024, 5120, 5632, 6144)
        SG_COL = (1536, 6656, 7936)
        MG_COL = 8448
        G_ROW = ((0, 1), (2, 3), (2, 3), (2, 3), (4, 5))
        JOB0 = len(jobs1)
        units = []
        for u in range(5):
            jobs = []
            for hh in range(2):
                for i in range(NT):
                    for h in range(4 * hh, 4 * hh + 4):
                        half = slice((h % 2) * HD, (h % 2) * HD + HD)
                        kvh = h if u < 4 else h // 4
                        jobs.append((q2T[half, u % 2, h // 2, i * P:(i + 1) * P],
                                     k2T[half, u % 2, h // 2 if u < 4 else h // 4, 0:(i + 1) * P],
                                     bt[:, hh, h % 4, (1 - i) * P:T],
                                     [vb[:, u % 2, j, kvh * HD:(kvh + 1) * HD] for j in range(i + 1)],
                                     2 * u + hh))
            units.append(jobs)

        def token_tiles(c0):
            return [W2[:, 0:4, c0:c0 + 512], W2[:, 4:8, c0:c0 + 512]]

        def merge_items(b):
            out = []
            for j in range(2):
                for f in range(2):
                    c0 = MG_COL + D * b + 512 * j + 256 * f
                    out.append(("G", b, 2 * j + f, [W2[:, :, c0:c0 + 256]]))
                out.append(("R", b, j, [a["w_branch_2"][0, b].rearrange("(k p) n -> p k n", p=P)
                                        [:, :, 512 * j:512 * j + 512]]))
            return out

        def unit_items(u):
            if u == 4:
                return [("q", 4, 0, token_tiles(Q_COL[4])), ("kv", 4, 0, [W2[:, :, K_COL[4]:K_COL[4] + 256]])]
            return [("q", u, 0, token_tiles(Q_COL[u])), ("k", u, 0, token_tiles(K_COL[u])),
                    ("v", u, 0, token_tiles(V_COL[u]))]

        segments = [
            (unit_items(0) + [("s", 0, 0, token_tiles(SG_COL[0]))], None),
            (unit_items(1), 0),
            (unit_items(2), 1),
            (unit_items(3) + [("s", 1, 1, token_tiles(SG_COL[1]))], 2),
            (unit_items(4) + [("s", 2, 0, token_tiles(SG_COL[2]))] + merge_items(0), 3),
            (merge_items(1), 4),
            (merge_items(2), None),
        ]
        BRANCH_END = {0: 0, 3: 1, 4: 2}
        order, b2_tiles, uses, n_qk = [], [], 0, 0

        pending = []

        def place_later(pending, entries, after):
            pending.append([after, entries])

        for items, u in segments:
            body = []
            for kind, who, j, srcs in items:
                use0 = uses
                uses += {"G": 1}.get(kind, 2)
                item = (kind, who, j, use0, N_B2 + len(b2_tiles), len(srcs))
                for t, src in enumerate(srcs):
                    n = N_B2 + len(b2_tiles)
                    b2_tiles.append(src)
                    for part in range(2):
                        body.append(("weights", item, n, t, part))
                        for p in pending:
                            p[0] -= 1
                        if not (part == 1 and t == len(srcs) - 1):
                            for p in [p for p in pending if p[0] <= 0 and p[1][0][0] != "turn"]:
                                body += p[1]
                                pending.remove(p)
                body.append(("empty", item))
                if kind == "G" and j == 0:
                    body.append(("branch", who, uses))
                    uses += 2
                for p in [p for p in pending if p[0] <= 0]:
                    if p[1][0][0] == "turn":
                        p[1] = [(*p[1][0], uses)]
                        uses += 1 if p[1][0][1][0] == "kv" else 2
                    body += p[1]
                    pending.remove(p)
                if kind in ("q", "k", "kv"):
                    place_later(pending, [("sums", item, n_qk)], 1)
                    place_later(pending, [("turn", item)], 3)
                    n_qk += 1
                if kind == "s":
                    place_later(pending, [("gate", item)], 1)
                if kind == "R":
                    place_later(pending, [("merge", item)] + ([("merged", 0), ("merged", 1)]
                                                              if (who, j) == (2, 0) else []), 1)
            if u is not None:
                steps = []
                for m in range(-2, 17):
                    steps.append(("job", u, m))
                    if m in (8, 16):
                        steps.append(("group", u, m // 8 - 1))
                spots = [k for k, e in enumerate(body) if e[0] == "weights"]
                start = JOB_START[u]
                mixed, done = [], 0
                for k, e in enumerate(body):
                    mixed.append(e)
                    if e[0] == "weights":
                        at = spots.index(k) + 1 - start
                        want = max(0, at) * len(steps) // (len(spots) - start - JOB_TAIL[u])
                        mixed += steps[done:max(done, want)]
                        if u in BRANCH_END and done < len(steps) <= want:
                            mixed.append(("finish", BRANCH_END[u]))
                        done = max(done, min(want, len(steps)))
                assert done == len(steps)
                body = mixed
            order += body
        for p in pending:
            order += p[1]
        order += [("merged", 2), ("merged", 3)]
        assert len(b2_tiles) == 51
        N_OUT2 = N_B2 + len(b2_tiles)
        b2_tiles += [a["w_out_2"][0].rearrange("(k p) n -> p k n", p=P)[:, 2 * r:2 * r + 2, :] for r in range(4)]

        def merged(y, h, r, k):
            return y[:, 4 + 2 * r + k, :] if r < 2 else h[:, 2 * r + k, :]

        def bank(use):
            return 5 + use % 3

        def wait_use(pe, use):
            if use >= 3:
                pe.wait_ge(emptied, use - 2)

        def blk2_pe(pe):
            pe.wait_ge(x_added, 16)
            norm_pe(pe, 4)
            for e in order:
                if e[0] == "weights":
                    _, (kind, who, j, use0, n0, count), n, t, part = e
                    if part == 0:
                        pe.wait_ge(lo_ready, n + 1)
                    if kind in "qkvs" or kind == "kv":
                        kc = KC if kind == "kv" else 4
                        if t == 0:
                            wait_use(pe, use0 + part)
                        hi, lo = w_parts(n, kc)
                        tok = slice(part * P, part * P + P)
                        for k in range(kc):
                            if n in (N_B2, N_B2 + 1):
                                wait_h(pe, 4, 4 * t + k, bank(use0 + part))
                            mm = product(ps[:, bank(use0 + part), 0:TILE // kc], hhi[:, 4 * t + k, tok],
                                         hlo[:, 4 * t + k, tok], hi[:, k, :], lo[:, k, :],
                                         t == 0 and k == 0, t == count - 1 and k == kc - 1)
                    elif kind == "G":
                        if part == 0:
                            wait_use(pe, use0)
                        hi, lo = w_parts(n, KC)
                        c = slice(part * P, part * P + P)
                        for k in range(KC):
                            mm = product(ps[:, bank(use0), part * T:(part + 1) * T], hi[:, k, c], lo[:, k, c],
                                         hhi[:, k, :], hlo[:, k, :], k == 0, k == KC - 1)
                    else:
                        if part == 0:
                            pe.wait_ge(br_lo, who + 1)
                        wait_use(pe, use0 + part)
                        hi, lo = w_parts(n, 4)
                        for f in range(2):
                            c = slice((2 * part + f) * P, (2 * part + f + 1) * P)
                            for k in range(4):
                                mm = product(ps[:, bank(use0 + part), f * T:(f + 1) * T], hi[:, k, c], lo[:, k, c],
                                             yhi[:, k, :], ylo[:, k, :], k == 0, k == 3)
                    if part == 1:
                        mm.then_inc(tile_used, 1)
                elif e[0] == "job":
                    _, u, m = e
                    if m == -2:
                        pe.wait_ge(emptied, turned_use(u))
                        if u == 0:
                            pe.wait_ge(h_lo, 5 * KC)
                    pe_step(pe, units[u], JOB0 + 16 * u, m)
                elif e[0] == "turn":
                    _, item, use = e
                    raw_, width = (qraw, 4) if item[0] == "q" else (kraw, 4 if item[0] == "k" else 2)
                    pe.wait_ge(b_scaled, qk_index(item) * 2 + 2)
                    for b in range(width // 2):
                        wait_use(pe, use + b)
                        for c in range(2):
                            for i in range(NT):
                                mm = nc.tensor.transpose(
                                    ps[:, bank(use + b), c * T + i * P:c * T + (i + 1) * P],
                                    raw_[:, i, (2 * b + c) * P:(2 * b + c + 1) * P], ident[:, :])
                        mm.then_inc(b_T, 1)
                elif e[0] == "branch":
                    _, b, use = e
                    pe.wait_ge(o_gated, 2 * b + 2)
                    for f in range(2):
                        wait_use(pe, use + f)
                        for c in range(2):
                            for i in range(NT):
                                mm = nc.tensor.transpose(
                                    ps[:, bank(use + f), c * T + i * P:c * T + (i + 1) * P],
                                    ob[:, BR_OB[b], i, (2 * f + c) * P:(2 * f + c + 1) * P], ident[:, :])
                        mm.then_inc(b_T, 1)
            for r in range(4):
                pe.wait_ge(lo_ready, N_OUT2 + r + 1)
                pe.wait_ge(m_lo, 2 * r + 2)
                mh, ml = (yhi, ylo) if r < 2 else (hhi, hlo)
                mm_rows(N_OUT2 + r, mh, ml, 2 * r + (4 if r < 2 else 0), r == 0, r == 3).then_inc(tile_used, 1)

        BR_OB = (0, 1, 0)

        def qk_index(item):
            return next(e[2] for e in order if e[0] == "sums" and e[1] == item)

        def turned_use(u):
            last = 0
            for e in order:
                if e[0] == "turn" and e[1][1] == u:
                    last = max(last, e[2] + (1 if e[1][0] == "kv" else 2))
                if e[0] == "empty" and e[1][1] == u and e[1][0] in ("v", "kv"):
                    last = max(last, e[1][3] + 2)
            return last

        T_COUNT, at = {}, 0
        for e in order:
            if e[0] == "turn":
                T_COUNT[e[2]] = at
                at += 1 if e[1][0] == "kv" else 2
            if e[0] == "branch":
                T_COUNT[e[2]] = at
                at += 2

        LAST_Q_T = max(T_COUNT[e[2]] + 2 for e in order if e[0] == "turn" and e[1][0] == "q")

        def bias_load(act, u, hh):
            head0 = 8 * u + 4 * hh
            src = bass.AP(tensor=bias_dram.tensor, offset=bias_dram.offset + head0 * P * DREL + P - 1,
                          ap=[[DREL - 1, P], [P * DREL, 4], [1, T]])
            if u:
                act.wait_ge(s_shifted, JOB0 + 16 * (u - 1) + 8 * hh + 8)
            else:
                act.wait_ge(bias_written, 16 * BIAS_WRITES)
            act.dma_start(bt[:, hh, :, :], src).then_inc(bt_landed[hh], 16)

        def blk2_act(act):
            act.wait_ge(h_lo, 5 * KC)
            act.dma_start(nsink[:, 0, :], a["sinks_2"][0].partition_broadcast(P)).then_inc(sink_landed, 16)
            bias_load(act, 0, 0)
            bias_load(act, 0, 1)
            for e in order:
                if e[0] == "weights" and e[4] == 0:
                    split_hi(act, e[2] + 2)
                elif e[0] == "empty":
                    kind, who, j, use0, n0, count = e[1]
                    act.wait_ge(tile_used, n0 + count)
                    if kind in ("q", "k"):
                        dst = qraw if kind == "q" else kraw
                        if qk_index(e[1]) >= 2:
                            act.wait_ge(b_T, before_T(e[1]))
                        for i in range(NT):
                            nc.scalar.activation(dst[:, i, :], ps[:, bank(use0 + i), :], ACT.Copy).then_inc(emptied, 1)
                    elif kind == "kv":
                        act.wait_ge(b_T, before_T(e[1]))
                        act.wait_ge(pv_done, JOB0 + 16 * 3)
                        for i in range(NT):
                            nc.scalar.activation(vb[:, 0, i, 0:2 * HD], ps[:, bank(use0 + i), 2 * HD:4 * HD],
                                                 ACT.Copy).then_inc(b_gated, 1)
                            src = ps[:, bank(use0 + i), 0:2 * HD].rearrange("p (g d) -> p g d", g=2)
                            nc.scalar.activation(
                                kraw[:, i, 0:4 * HD].rearrange("p (g c d) -> p g c d", g=2, c=2),
                                src.unsqueeze(2).broadcast_to([P, 2, 2, HD]), ACT.Copy).then_inc(emptied, 1)
                    elif kind == "v":
                        if who >= 2:
                            act.wait_ge(pv_done, JOB0 + 16 * (who - 1))
                        for i in range(NT):
                            nc.scalar.activation(vb[:, who % 2, i, :], ps[:, bank(use0 + i), :],
                                                 ACT.Copy).then_inc(emptied, 1)
                    elif kind == "s":
                        for i in range(NT):
                            nc.scalar.activation(gth2[:, i, :], ps[:, bank(use0 + i), :], ACT.Tanh,
                                                 scale=0.5).then_inc(b_tanh, 1)
                            nc.scalar.activation(gsil[:, j, i, :], ps[:, bank(use0 + i), :],
                                                 ACT.Copy).then_inc(emptied, 1)
                    elif kind == "G":
                        if 2 * who + j // 2 >= 1:
                            act.wait_ge(m_mul, 2 * who + j // 2)
                        else:
                            act.wait_ge(b_silu, 6)
                        nc.scalar.activation(gs[:, 2 * (j % 2):2 * (j % 2) + 2, :].rearrange("p f t -> p (f t)"),
                                             ps[:, bank(use0), :], ACT.Tanh, scale=0.5).then_inc(emptied, 1)
                    else:
                        if 2 * who + j >= 1:
                            act.wait_ge(m_mul, 2 * who + j)
                        act.wait_ge(br_lo, who + 1)
                        for f in range(2):
                            nc.scalar.activation(rb[:, 2 * f:2 * f + 2, :].rearrange("p f t -> p (f t)"),
                                                 ps[:, bank(use0 + f), :], ACT.Copy).then_inc(emptied, 1)
                elif e[0] == "turn":
                    _, item, use = e
                    u = item[1]
                    q = item[0] == "q"
                    if u >= 2:
                        act.wait_ge(s_ready, JOB0 + 16 * (u - 1))
                    for b in range(1 if item[0] == "kv" else 2):
                        act.wait_ge(b_T, T_COUNT[use] + b + 1)
                        dst = (q2T if q else k2T)[:, u % 2, 2 * b:2 * b + 2, :].rearrange("p c t -> p (c t)")
                        g = qk8[:, G_ROW[u][0]:G_ROW[u][0] + 1] if q else \
                            vec[:, V_QK + G_ROW[u][1]:V_QK + G_ROW[u][1] + 1]
                        nc.scalar.activation(dst, ps[:, bank(use + b), :], ACT.Copy, scale=g).then_inc(emptied, 1)
                elif e[0] == "job":
                    _, u, m = e
                    act_step(act, units[u], JOB0 + 16 * u, m)
                    if m in (7, 15) and u < 4:
                        bias_load(act, u + 1, m // 8)
                elif e[0] == "group":
                    _, u, hh = e
                    if u == 4 and hh == 0:
                        act.wait_ge(b_T, T_COUNT[next(x[2] for x in order if x[0] == "branch")] + 2)
                    group_out(act, 4 + 2 * u + hh,
                              ob[:, u % 4, :, hh * 256:hh * 256 + 256],
                              lambda b: b.rearrange("p (i c) -> p i c", i=2))
                elif e[0] == "finish":
                    b = e[1]
                    if b == 1:
                        act.wait_ge(c_step, C_DIFF[1])
                        nc.scalar.activation(comb[:, 2:5], comb[:, 2:5], ACT.Exp).then_inc(c_exp, 1)
                    if b == 2:
                        act.wait_ge(c_step, C_DIFF[2])
                        nc.scalar.activation(comb[:, 1:3], comb[:, 1:3], ACT.Exp).then_inc(c_exp, 1)
                elif e[0] == "branch":
                    _, b, use = e
                    if b:
                        act.wait_ge(m_mul, 2 * b)
                    for f in range(2):
                        act.wait_ge(b_T, T_COUNT[use] + f + 1)
                        nc.scalar.activation(brT[:, 2 * f:2 * f + 2, :].rearrange("p c t -> p (c t)"),
                                             ps[:, bank(use + f), :], ACT.Copy, scale=0.5).then_inc(emptied, 1)
                    act.wait_ge(emptied, use + 2)
                    if b:
                        act.wait_ge(tile_used, R_TILE[b - 1])
                    nc.scalar.activation(yhi[:, 0:4, :], brT[:, :, :], ACT.Copy).then_inc(br_hi, 1)
                elif e[0] == "merged":
                    r = e[1]
                    act.wait_ge(m_sum, 5 if r < 2 else 6)
                    if r == 2:
                        act.wait_ge(tile_used, N_OUT2)
                    for k in range(2):
                        nc.scalar.activation(merged(yhi, hhi, r, k), macc[:, 2 * r + k, :], ACT.Copy,
                                             scale=0.5).then_inc(m_hi, 1)
                    if r >= 2:
                        split_hi(act, N_OUT2 + r)

        R_TILE = [max(e[2] for e in order if e[0] == "weights" and e[1][0] == "R" and e[1][1] == b) + 1
                  for b in range(3)]
        C_DIFF = (0, 5, 13)

        def before_T(item):
            mine = "q" if item[0] == "q" else "k"
            last = 0
            for e in order:
                if e[0] == "empty" and e[1] == item:
                    return last
                if e[0] == "turn" and e[1][0][0] == mine:
                    last = T_COUNT[e[2]] + 2
            return last

        def bc(ap, n, axis):
            return ap.unsqueeze(axis).broadcast_to([*ap.shape[:axis], n, *ap.shape[axis:]])

        def blk2_dve(dve):
            dve.wait_ge(sink_landed, 16)
            nc.vector.tensor_scalar(nsink[:, 1, :], nsink[:, 0, :], -1.0, None, ALU.mult).then_inc(c_step, 1)
            for e in order:
                if e[0] == "weights" and e[4] == 1:
                    split_lo(dve, e[2] + 2)
                elif e[0] == "sums":
                    _, item, nq = e
                    q = item[0] == "q"
                    heads = 4 if item[0] == "kv" else 8
                    sq = (q2T if q else k2T)[:, item[1] % 2].rearrange("p c t -> p (c t)")
                    dve.wait_ge(b_squared, 2 * nq + 2)
                    for i in range(NT):
                        nc.vector.tensor_reduce(
                            b_ss[:, nq % 2, 0, i, 0:heads],
                            sq[:, i * 512:i * 512 + heads * HD].rearrange("p (h d) -> p h d", h=heads),
                            AX.X, ALU.add).then_inc(b_summed, 1)
                elif e[0] == "gate":
                    kind, who, j, use0, n0, count = e[1]
                    for i in range(NT):
                        dve.wait_ge(emptied, use0 + i + 1)
                        nc.vector.scalar_tensor_tensor(gsil[:, j, i, :], gth2[:, i, :], 1.0, gsil[:, j, i, :],
                                                       ALU.add, ALU.mult).then_inc(b_silu, 1)
                elif e[0] == "merge":
                    kind, who, j, use0, n0, count = e[1]
                    dve.wait_ge(emptied, use0 + 2)
                    if who == 0:
                        nc.vector.scalar_tensor_tensor(macc[:, 4 * j:4 * j + 4, :], gs[:, :, :], 1.0, rb[:, :, :],
                                                       ALU.add, ALU.mult).then_inc(m_mul, 1)
                        nc.vector.engine_nop().then_inc(m_sum, 1)
                    else:
                        dve.wait_ge(m_mul, 2 * who + j)
                        dve.wait_ge(m_sum, 2 * who + j)
                        if (who, j) == (1, 0):
                            dve.wait_ge(b_T, LAST_Q_T)
                        nc.vector.scalar_tensor_tensor(mt[:, :, :], gs[:, :, :], 1.0, rb[:, :, :],
                                                       ALU.add, ALU.mult).then_inc(m_mul, 1)
                        dve.wait_ge(m_mul, 2 * who + j + 1)
                        nc.vector.tensor_tensor(macc[:, 4 * j:4 * j + 4, :], macc[:, 4 * j:4 * j + 4, :],
                                                mt[:, :, :], ALU.add).then_inc(m_sum, 1)
                elif e[0] == "job":
                    _, u, m = e
                    if m + 1 in (0, 8) :
                        dve.wait_ge(bt_landed[(m + 1) // 8], 16 * (u + 1))
                    dve_step(dve, units[u], JOB0 + 16 * u, m)
                elif e[0] == "finish":
                    finish2(dve, e[1])
                elif e[0] == "branch":
                    b = e[1]
                    dve.wait_ge(br_hi, b + 1)
                    nc.vector.tensor_tensor(ylo[:, 0:4, :], brT[:, :, :], yhi[:, 0:4, :].bitcast(F32),
                                            ALU.subtract).then_inc(br_lo, 1)
                elif e[0] == "merged":
                    r = e[1]
                    for k in range(2):
                        dve.wait_ge(m_hi, 2 * r + k + 1)
                        nc.vector.scalar_tensor_tensor(merged(ylo, hlo, r, k), macc[:, 2 * r + k, :], 0.5,
                                                       merged(yhi, hhi, r, k).bitcast(F32), ALU.mult,
                                                       ALU.subtract).then_inc(m_lo, 1)
                    if r >= 2:
                        split_lo(dve, N_OUT2 + r)
            add_x(dve, 4, N_OUT2 + 4)

        def finish2(dve, b):
            at = {0: 1, 1: 2, 2: 10}[b]

            def step(ins):
                nonlocal at
                at += 1
                ins.then_inc(c_step, 1)
                dve.wait_ge(c_step, at)
            u0 = (0, 1, 4)[b]
            nm = nmax[:, 2 * u0:2 * u0 + (2, 6, 2)[b], :].rearrange("p (u g) j -> p u g j", g=2)
            sm = psum_[:, 2 * u0:2 * u0 + (2, 6, 2)[b], :].rearrange("p (u g) j -> p u g j", g=2)
            dve.wait_ge(o_copied, 4 + 2 * ((0, 3, 4)[b] + 1))
            if b == 0:
                step(nc.vector.reciprocal(comb[:, 5], sm[:, 0]))
            elif b == 1:
                step(nc.vector.tensor_tensor(comb[:, 0], nm[:, 0], nm[:, 1], ALU.min))
                step(nc.vector.tensor_tensor(comb[:, 0], comb[:, 0], nm[:, 2], ALU.min))
                step(nc.vector.tensor_tensor(comb[:, 2:5], bc(comb[:, 0], 3, 1), nm, ALU.subtract))
                assert at == C_DIFF[1]
                dve.wait_ge(c_exp, 1)
                step(nc.vector.tensor_tensor(comb[:, 5:8], comb[:, 2:5], sm, ALU.mult))
                step(nc.vector.tensor_tensor(comb[:, 5], comb[:, 5], comb[:, 6], ALU.add))
                step(nc.vector.tensor_tensor(comb[:, 5], comb[:, 5], comb[:, 7], ALU.add))
                step(nc.vector.reciprocal(comb[:, 6], comb[:, 5]))
                step(nc.vector.tensor_tensor(comb[:, 2:5], comb[:, 2:5], bc(comb[:, 6], 3, 1), ALU.mult))
            else:
                def sink(k):
                    return bc(nsink[:, k, :].rearrange("p (g q) -> p g q", g=2), 2, 2)

                def giq(ap):
                    return ap.rearrange("p g (i q) -> p g i q", i=2)
                step(nc.vector.tensor_tensor(giq(comb[:, 0]), giq(nm[:, 0]), sink(1), ALU.min))
                step(nc.vector.tensor_tensor(comb[:, 1], comb[:, 0], nm[:, 0], ALU.subtract))
                step(nc.vector.tensor_tensor(giq(comb[:, 2]), giq(comb[:, 0]), sink(0), ALU.add))
                assert at == C_DIFF[2]
                dve.wait_ge(c_exp, 2)
                step(nc.vector.tensor_tensor(comb[:, 3], comb[:, 1], sm[:, 0], ALU.mult))
                step(nc.vector.tensor_tensor(comb[:, 3], comb[:, 3], comb[:, 2], ALU.add))
                step(nc.vector.reciprocal(comb[:, 4], comb[:, 3]))
                step(nc.vector.tensor_tensor(comb[:, 5], comb[:, 4], comb[:, 1], ALU.mult))
            scale_tile(dve, nc.vector, b, 0, o_scaled, at)

        FACTORS = (2, 10, 17)
        OUTPUTS = (((0, 5),), ((1, 2), (2, 3), (3, 4)), ((0, 5),))

        def scale_tile(engine, ops, b, i, scaled, at):
            assert at == FACTORS[b]
            engine.wait_ge(c_step, at)
            engine.wait_ge(b_silu, 2 * b + 2)
            parts = [(o, comb[:, f]) for o, f in OUTPUTS[b]]
            n = (0, 1, 6)[b]
            for k, (o, f) in enumerate(parts):
                v = ob[:, o, i, :].rearrange("p (g q d) -> p g q d", g=2, q=4)
                fac = bc(f[:, :, 4 * i:4 * i + 4], HD, 3)
                n += 1
                ops.tensor_tensor(v, v, fac, ALU.mult).then_inc(scaled, 1)
                first = ob[:, parts[0][0], i, :]
                if k:
                    engine.wait_ge(scaled, n)
                    n += 1
                    ops.tensor_tensor(first, first, ob[:, o, i, :], ALU.add).then_inc(scaled, 1)
            engine.wait_ge(scaled, n)
            ops.tensor_tensor(first, first, gsil[:, (0, 1, 0)[b], i, :], ALU.mult).then_inc(o_gated, 1)

        def blk2_pool(pool):
            for e in order:
                if e[0] == "finish":
                    scale_tile(pool, nc.gpsimd, e[1], 1, o_scaled_p, FACTORS[e[1]])
                if e[0] != "sums":
                    continue
                _, item, nq = e
                q = item[0] == "q"
                heads = 4 if item[0] == "kv" else 8
                src = qraw if q else kraw
                sq = (q2T if q else k2T)[:, item[1] % 2].rearrange("p c t -> p (c t)")
                if item[1] >= 2:
                    pool.wait_ge(s_ready, JOB0 + 16 * (item[1] - 1))
                for i in range(NT):
                    pool.wait_ge(emptied, item[3] + i + 1)
                    r = src[:, i, 0:heads * HD]
                    nc.gpsimd.tensor_tensor(sq[:, i * 512:i * 512 + heads * HD], r, r, ALU.mult).then_inc(b_squared, 1)
                pool.wait_ge(b_summed, 2 * nq + 2)
                nc.gpsimd.tensor_scalar(b_ss[:, nq % 2, 1, :, 0:heads], b_ss[:, nq % 2, 0, :, 0:heads], 1.0 / HD, EPS,
                                        ALU.mult, ALU.add).then_inc(b_mean, 1)
                pool.wait_ge(b_mean, nq + 1)
                nc.gpsimd.tensor_tensor(b_inv[:, nq % 2, :, 0:heads], b_ss[:, nq % 2, 1, :, 0:heads],
                                        nhalf[:, 0:2 * heads].rearrange("p (i h) -> p i h", i=2),
                                        ALU.pow).then_inc(b_root, 1)
                pool.wait_ge(b_root, nq + 1)
                for i in range(NT):
                    r = src[:, i, 0:heads * HD].rearrange("p (h d) -> p h d", h=heads)
                    nc.gpsimd.tensor_tensor(r, r, bc(b_inv[:, nq % 2, i, 0:heads], HD, 2),
                                            ALU.mult).then_inc(b_scaled, 1)

        block = ctx.enter_context(nc.Block())

        vector_rows = [
            (V_NORM_MIX, a["norm_mix"].rearrange("d (c p) -> (d c) p", p=P)),
            (V_NORM_FFN, a["norm_ffn"].rearrange("d (c p) -> (d c) p", p=P)),
            (V_LN2, a["ln_g_2"].rearrange("d (c p) -> (d c) p", p=P)),
            (V_CONV_A, a["conv_a"][0].rearrange("k (c p) -> (k c) p", p=P)),
            (V_POOL_S, a["pool_scale"].rearrange("d (c p) -> (d c) p", p=P)),
            (V_DWB, a["conf_dw_b"].rearrange("d (c p) -> (d c) p", p=P)),
            (V_LNG, a["conf_ln_g"].rearrange("d (c p) -> (d c) p", p=P)),
            (V_LNB, a["conf_ln_b"].rearrange("d (c p) -> (d c) p", p=P)),
            (V_POS, a["cmp_pos"][0].rearrange("v (j s) d -> (v j) (s d)", s=2)),
        ]
        N_VECTORS = len(vector_rows) + 3

        @block.sync
        def _(sp):
            sp.dma_start(x[:, :, :], a["x"][0].rearrange("(i p) d -> p i d", p=P)).then_inc(x_landed, 16)
            load_tile(sp, N_MIX0, mix0[0])
            for r0, src in vector_rows:
                sp.dma_start(vrow[r0:r0 + src.shape[0], :], src).then_inc(vec_landed, 16)
            for half in range(2):
                sp.dma_start(vrow[V_QK:V_QK + 6, half * HD:half * HD + HD], a["qk_g_2"][0]).then_inc(vec_landed, 16)
            sp.dma_start(vrow2[:, :], a["conf_dw"][0].rearrange("k (c p) -> (k c) p", p=P)).then_inc(vec_landed, 16)
            for j, src in enumerate(mix0[1:]):
                load_tile(sp, N_MIX0 + 1 + j, src)
            ffn_sp(sp, 0, N_FFN0)
            for j, src in enumerate(mix1):
                load_tile(sp, N_MIX1 + j, src)
            ffn_sp(sp, 1, N_FFN1)
            for j, src in enumerate(b2_tiles):
                load_tile(sp, N_B2 + j, src)
            for i in range(NT):
                sp.wait_ge(x_added, 20 - 2 + 2 * i)
                sp.dma_start(out[0, i * P:(i + 1) * P, :], x[:, i, :]).then_inc(stored, 16)
            sp.wait_ge(stored, 32)

        @block.gpsimd
        def _(pool):
            for dst, src in ((relb, a["rel_bias_2"]), (onehot, a["c_onehot"]), (relmask, a["c_relmask"])):
                pool.dma_start(dst, src).then_inc(bias_loaded, 16)
            nc.gpsimd.memset(eps[:, :], EPS).then_inc(eps_set, 1)
            nc.gpsimd.memset(nhalf[:, :], -0.5).then_inc(nhalf_set, 1)
            nc.gpsimd.memset(pool_a[:, :, 0:16], 0.0).then_inc(zero_set, 1)
            nc.gpsimd.memset(cvp[:, :, 0:2], 0.0).then_inc(zero_set, 1)
            nc.gpsimd.memset(onesd[:, :], 1.0 / CW).then_inc(nhalf_set, 1)
            pool.wait_ge(nhalf_set, 2)
            norm_pool(pool, 0)
            pool.dma_start(rcnt[:, :, :], a["c_rcnt"].partition_broadcast(P)).then_inc(consts_landed, 16)
            pool.dma_start(pw[:, :, :], a["pool_w"][0].rearrange("g c d -> c g d")).then_inc(pw_landed, 16)
            norm_pool(pool, 1)
            pool.wait_ge(bias_rows, 1)
            for j in range(BIAS_WRITES):
                hs = slice(j * H_TOT // BIAS_WRITES, (j + 1) * H_TOT // BIAS_WRITES)
                pool.wait_ge(tile_used, N_FFN0 + 3 * j + 1)
                pool.dma_start(bias_dram[hs], bc(relrow[hs], P, 1)).then_inc(bias_written, 16)
            norm_pool(pool, 2)
            mix1_pool(pool)
            norm_pool(pool, 3)
            norm_pool(pool, 4)
            blk2_pool(pool)

        @block.scalar
        def _(act):
            act.dma_start(ident[:, :], a["c_ident"]).then_inc(ident_landed, 16)
            norm_act(act, 0, V_NORM_MIX)
            split_hi(act, 1)
            act.wait_ge(zero_set, 2)
            for t in range(8):
                split_hi(act, N_MIX0 + t + 2)
                if t < 2:
                    act.wait_ge(tile_used, N_MIX0 + t + 1)
                    nc.scalar.activation(pool_a[:, 2 * t:2 * t + 2, 16:],
                                         ps[:, t, :].rearrange("p (f t) -> p f t", f=2),
                                         ACT.Copy).then_inc(v_copied, 1)
                if t in (2, 5):
                    act.wait_ge(tile_used, N_MIX0 + t + 1)
                    j = t // 3
                    nc.scalar.activation(ctile[:, 2 * j:2 * j + 2, :].rearrange("p f t -> p (f t)"),
                                         ps[:, t, :], ACT.Copy).then_inc(c_copied, 1)
            act.wait_ge(pool_mm, 1)
            for j in range(CC):
                nc.scalar.activation(yhi[:, CC + j, :], ps[:, j // 2, (j % 2) * T:(j % 2 + 1) * T], ACT.Copy,
                                     scale=vec[:, V_POOL_S + j:V_POOL_S + j + 1]).then_inc(y_hi, 1)
            split_hi(act, N_MIX0 + 10)
            for j in range(CC):
                act.wait_ge(yc_ready, j + 1)
                nc.scalar.activation(yhi[:, j, :], yb[:, j, :], ACT.Copy).then_inc(y_hi, 1)
            for t in range(11, 14):
                split_hi(act, N_MIX0 + t)
            norm_act(act, 1, V_NORM_FFN)
            ffn_act(act, 0, N_FFN0)
            norm_act(act, 2, V_NORM_MIX + KC)
            m1_loads(act)
            mix1_act(act)
            norm_act(act, 3, V_NORM_FFN + KC)
            ffn_act(act, 1, N_FFN1)
            norm_act(act, 4, V_LN2)
            blk2_act(act)

        @block.vector
        def _(dve):
            norm_dve(dve, 0, V_NORM_MIX)
            split_lo(dve, 1)
            dve.wait_ge(vec_ready, 2)
            nc.vector.tensor_scalar(dwv[:, :, :], dwv[:, :, :], 0.5, None, ALU.mult).then_inc(half_set, 1)
            nc.vector.tensor_scalar(qk8[:, :], vec[:, V_QK:V_QK + 6], HD ** -0.5, None, ALU.mult).then_inc(half_set, 1)

            def pooling():
                dve.wait_ge(v_copied, 2)
                nc.vector.tensor_tensor(pool_b[:, :, 1:], pool_a[:, :, 1:], pool_a[:, :, 0:271],
                                        ALU.add).then_inc(pool_step, 1)
                src, dst, lead = pool_b, pool_c, 1
                for g in range(1, 4):
                    w = 2 ** g
                    lead += w
                    dve.wait_ge(pool_step, g)
                    nc.vector.tensor_tensor(dst[:, g:, lead:], src[:, g:, lead:], src[:, g:, lead - w:272 - w],
                                            ALU.add).then_inc(pool_step, 1)
                    src, dst = dst, src
                dve.wait_ge(pool_step, 4)
                dve.wait_ge(consts_landed, 16)
                for b, g in ((pool_b, 0), (pool_c, 1)):
                    nc.vector.tensor_tensor(b[:, g::2, 16:], b[:, g::2, 16:], rcnt[:, g::2, :],
                                            ALU.mult).then_inc(pool_step, 1)
                dve.wait_ge(pool_step, 6)
                for b, g in ((pool_b, 0), (pool_c, 1)):
                    nc.vector.tensor_tensor(b[:, g::2, 16:], b[:, g::2, 16:], pool_a[:, g::2, 16:],
                                            ALU.subtract).then_inc(pool_step, 1)

            def conv3(j):
                t = 2 + 3 * j
                dve.wait_ge(c_copied, j + 1)
                dve.wait_ge(tile_used, N_MIX0 + t + 2)
                dve.wait_ge(zero_set, 2)
                nc.vector.tensor_tensor(cvp[:, 2 * j:2 * j + 2, 2:], ctile[:, 2 * j:2 * j + 2, :],
                                        ps[:, t + 1, :].rearrange("p (f t) -> p f t", f=2),
                                        ALU.mult).then_inc(cv_ready, 1)
                dve.wait_ge(cv_ready, j + 1)
                for k in range(3):
                    for f in range(2):
                        c = 2 * j + f
                        w = vec[:, V_CONV_A + 4 * k + c:V_CONV_A + 4 * k + c + 1]
                        if k == 0:
                            nc.vector.tensor_scalar(yb[:, c, :], cvp[:, c, 0:T], w, None,
                                                    ALU.mult).then_inc(conv_step, 1)
                        else:
                            dve.wait_ge(conv_step, 6 * j + 2 * (k - 1) + f + 1)
                            nc.vector.scalar_tensor_tensor(yb[:, c, :], cvp[:, c, k:k + T], w, yb[:, c, :],
                                                           ALU.mult, ALU.add).then_inc(conv_step, 1)

            def gate(j):
                t = 2 + 3 * j
                dve.wait_ge(tile_used, N_MIX0 + t + 3)
                dve.wait_ge(conv_step, 6 * j + 6)
                for f in range(2):
                    c = 2 * j + f
                    nc.vector.tensor_tensor(yb[:, c, :], yb[:, c, :],
                                            ps[:, t + 2, f * T:(f + 1) * T], ALU.mult).then_inc(yc_ready, 1)

            for t in range(8):
                split_lo(dve, N_MIX0 + t + 2)
                if t == 1:
                    dve.wait_ge(bias_T, 1)
                    nc.vector.tensor_copy(relT, ps[0:N_BUCKETS, 6, 0:H_TOT]).then_inc(bias_copied, 1)
                if t == 2:
                    dve.wait_ge(bias_mm, 1)
                    nc.vector.tensor_tensor(relrow, relmask, ps[0:H_TOT, 7, 0:DREL], ALU.add).then_inc(bias_rows, 1)
                    pooling()
                if t == 3:
                    conv3(0)
                if t == 4:
                    gate(0)
                if t == 6:
                    conv3(1)
            for j in range(CC):
                dve.wait_ge(y_hi, j // 2 * 2 + 2)
                nc.vector.scalar_tensor_tensor(ylo[:, CC + j, :], ps[:, j // 2, (j % 2) * T:(j % 2 + 1) * T],
                                               vec[:, V_POOL_S + j:V_POOL_S + j + 1],
                                               yhi[:, CC + j, :].bitcast(F32),
                                               ALU.mult, ALU.subtract).then_inc(y_lo, 1)
            split_lo(dve, N_MIX0 + 10)
            gate(1)
            for j in range(CC):
                dve.wait_ge(y_hi, CC + j + 1)
                nc.vector.tensor_tensor(ylo[:, j, :], yb[:, j, :], yhi[:, j, :].bitcast(F32),
                                        ALU.subtract).then_inc(y_lo, 1)
            for t in range(11, 13):
                split_lo(dve, N_MIX0 + t)
            add_x(dve, 0, N_FFN0, 2)
            norm_dve(dve, 1, V_NORM_FFN)
            ffn_dve(dve, 0, N_FFN0)
            norm_dve(dve, 2, V_NORM_MIX + KC)
            mix1_dve(dve)
            norm_dve(dve, 3, V_NORM_FFN + KC)
            ffn_dve(dve, 1, N_FFN1)
            norm_dve(dve, 4, V_LN2)
            blk2_dve(dve)

        @block.tensor
        def _(pe):
            pe.wait_ge(ident_landed, 16)
            pe.wait_ge(vec_landed, 16 * N_VECTORS)
            nc.tensor.transpose(ps[:, 0, 0:V_ROWS], vrow[:, :], ident[0:V_ROWS, 0:V_ROWS]).then_inc(vec_T, 1)
            n2 = CONF_K * CC
            nc.tensor.transpose(ps[:, 1, 0:n2], vrow2[:, :], ident[0:n2, 0:n2]).then_inc(vec_T, 1)
            norm_pe(pe, 0)
            pe.wait_ge(vec_ready, 2)
            for t in range(8):
                mm_feature(N_MIX0 + t, t, 0 if t == 0 else None)
                if t == 1:
                    pe.wait_ge(bias_loaded, 48)
                    nc.tensor.transpose(ps[0:N_BUCKETS, 6, 0:H_TOT], relb, ident[0:H_TOT, 0:H_TOT])\
                        .then_inc(bias_T, 1)
                if t == 2:
                    pe.wait_ge(bias_copied, 1)
                    nc.tensor.matmul(ps[0:H_TOT, 7, 0:DREL], relT, onehot, start=True, stop=True).then_inc(bias_mm, 1)
                if t == 5:
                    pe.wait_ge(bias_rows, 1)
            pe.wait_ge(pw_landed, 16)
            pe.wait_ge(pool_step, 8)
            for g in range(CC):
                mm = nc.tensor.matmul(ps[:, g // 2, (g % 2) * T:(g % 2 + 1) * T], pw[:, g, :],
                                      (pool_b, pool_c)[g % 2][:, g, 16:], start=True, stop=True)
            mm.then_inc(pool_mm, 1)
            for j in range(4):
                pe.wait_ge(lo_ready, N_MIX0 + 8 + j + 1)
                pe.wait_ge(y_lo, (2 * j + 2) if j < 2 else (8 if j == 3 else 6))
                if j == 0:
                    pe.wait_ge(yc_ready, 2)
                    pe.wait_ge(c_copied, 2)
                mm_rows(N_MIX0 + 8 + j, yhi, ylo, (4, 6, 0, 2)[j], j == 0, j == 3, 2).then_inc(tile_used, 1)
            pe.wait_ge(x_added, 4)
            norm_pe(pe, 1)
            ffn_pe(pe, 0, N_FFN0)
            pe.wait_ge(x_added, 8)
            norm_pe(pe, 2)
            mix1_pe(pe)
            pe.wait_ge(x_added, 12)
            norm_pe(pe, 3)
            ffn_pe(pe, 1, N_FFN1)
            blk2_pe(pe)


_INS = ["x", "norm_mix", "norm_ffn", "ffn_gate", "ffn_up", "ffn_down", "w_in_even", "conv_a", "pool_w",
        "pool_scale", "w_out_even", "w_in_odd", "q_norm", "k_norm", "cmp_pos", "cmp_w1", "cmp_w2", "conf_dw",
        "conf_dw_b", "conf_ln_g", "conf_ln_b", "w_out_odd", "ln_g_2", "w_in_2", "qk_g_2", "sinks_2",
        "w_branch_2", "w_out_2", "rel_bias_2"]


def kernel(**inputs):
    import numpy as _np
    import concourse.bacc as _bacc
    from concourse import mybir as _mybir
    from concourse.bass_utils import run_bass_kernel_spmd as _run

    arrays = {name: _np.ascontiguousarray(inputs[name]) for name in _INS}
    arrays.update(constants())
    nc = _bacc.Bacc("TRN2", target_bir_lowering=False, num_devices=1)
    a = {name: nc.dram_tensor(name, v.shape, _mybir.dt.from_np(v.dtype), kind="ExternalInput").ap()
         for name, v in arrays.items()}
    out = nc.dram_tensor("out", (1, T, D), F32, kind="ExternalOutput").ap()
    build(nc, a, out)
    r = _run(nc, [arrays], core_ids=[0])
    return r.results[0]["out"]
```
